# Optimizing a Trainium2 kernel written in Bass

```python
import math
import jax, jax.numpy as jnp
from jax import lax
import numpy as np

D_MODEL = 1024
BATCH = 1
SEQ = 512
DEPTH = 1
DEC_BATCH = 8
DEC_SEQ = 1
PAST_LEN = 2048
PAGE_SIZE = 128

F32 = jnp.float32
EPS = 1e-6
N_META = 16
N_BRANCH = 4
BRANCH_W = D_MODEL // N_BRANCH
HA = 4
DVA = BRANCH_W // HA
DQA = DVA // 2
QBLK = 128
HB = 4
DKB = BRANCH_W // HB
DVB = BRANCH_W // HB
RET_CHUNK = 128
ROPE_BASE = 10000.0
WC = BRANCH_W
HC = 4
BWC = WC // HC
CONV_W = 4
LRU_C = 8.0
HD = 4
DVD = BRANCH_W // HD
DKD = DVD // 2
GLA_RANK = 16
GLA_TAU = 16.0
GLA_CHUNK = 16
N_GROUPS = 4
EXP_PER_GROUP = 4
N_EXPERTS = N_GROUPS * EXP_PER_GROUP
TOP_K_IN = 2
D_EXPERT = 256
SPLITS = (HA * 2 * DQA, HA * 2 * DQA, HA * DVA,
          HB * DKB, HB * DKB, HB * DVB, HB * DVB,
          WC, WC,
          HD * DKD, HD * DKD, HD * DVD, HD * DVD, GLA_RANK)
IN_W = sum(SPLITS)

kernel_name = 'hybrid_diffattn_retention_rglru_gla_hmoe_step'

def rms_norm(x, g):
    xf = x.astype(F32)
    y = xf * lax.rsqrt(jnp.mean(xf * xf, axis=-1, keepdims=True) + EPS)
    return (y * g.astype(F32)).astype(x.dtype)

def group_norm(x, g):
    xf = x.astype(F32)
    mu = jnp.mean(xf, axis=-1, keepdims=True)
    var = jnp.mean(jnp.square(xf - mu), axis=-1, keepdims=True)
    return ((xf - mu) * lax.rsqrt(var + EPS) * g.astype(F32)).astype(x.dtype)

def project(xn, w_in):
    cuts = [int(c) for c in np.cumsum(SPLITS)[:-1]]
    return jnp.split(xn @ w_in, cuts, axis=-1)

def left_pad(t, pad):
    return jnp.pad(t, [(0, 0), (pad, 0)] + [(0, 0)] * (t.ndim - 2))

def chunked(fn, s0, chunk, pad, *xs):
    xs = [left_pad(t, pad) for t in xs]
    b, lp = xs[0].shape[:2]
    nc = lp // chunk
    xc = tuple(t.reshape((b, nc, chunk) + t.shape[2:]).swapaxes(0, 1) for t in xs)
    s, o = lax.scan(lambda s, c: fn(s, *c), s0, xc)
    o = o.swapaxes(0, 1).reshape((b, lp) + o.shape[3:])
    return s, o[:, pad:]

def diff_attn_block(q, k, v, q_pos, k_pos, lam):
    s = jnp.einsum('bqhmd,bkhmd->bhmqk', q, k)
    s = jnp.where(k_pos[None, :] <= q_pos[:, None], s, -jnp.inf)
    p = jax.nn.softmax(s, axis=-1)
    w = p[:, :, 0] - lam * p[:, :, 1]
    return jnp.einsum('bhqk,bkhv->bqhv', w.astype(v.dtype), v)

def diff_attn_prompt(q, k, v, lam):
    b, l = q.shape[:2]
    nb = -(-l // QBLK)
    qp = jnp.pad(q, ((0, 0), (0, nb * QBLK - l), (0, 0), (0, 0), (0, 0)))
    qb = qp.reshape(b, nb, QBLK, HA, 2, DQA).swapaxes(0, 1)
    k_pos = jnp.arange(l)

    def one(args):
        qi, start = args
        return diff_attn_block(qi, k, v, start + jnp.arange(QBLK), k_pos, lam)

    o = lax.map(one, (qb, jnp.arange(nb) * QBLK))
    return o.swapaxes(0, 1).reshape(b, nb * QBLK, HA, DVA)[:, :l]

def rotary(x, pos):
    d = x.shape[-1]
    inv = ROPE_BASE ** (-jnp.linspace(0.0, 1.0, d // 2))
    ang = pos.astype(F32)[:, None] * inv[None]
    cos = jnp.cos(ang)[None, :, None, :]
    sin = jnp.sin(ang)[None, :, None, :]
    x1, x2 = x[..., :d // 2], x[..., d // 2:]
    return jnp.concatenate([x1 * cos - x2 * sin, x1 * sin + x2 * cos], axis=-1)

def ret_log_gamma():
    return jnp.log(1.0 - 2.0 ** (-5.0 - jnp.arange(HB, dtype=F32)))

def ret_chunk(s0, q, k, v):
    t_len = q.shape[1]
    lg = ret_log_gamma()
    t = jnp.arange(t_len, dtype=F32)
    rel = t[:, None] - t[None, :]
    dmat = jnp.where(rel >= 0, jnp.exp(jnp.maximum(rel, 0.0)[None] * lg[:, None, None]), 0.0)
    a = jnp.einsum('bthk,bjhk->bhtj', q, k) * dmat
    o = jnp.einsum('bhtj,bjhv->bthv', a, v)
    o = o + jnp.einsum('bthk,bhkv->bthv', q, s0) * jnp.exp((t[:, None] + 1.0) * lg[None])[None, :, :, None]
    kd = k * jnp.exp((t_len - 1.0 - t)[:, None] * lg[None])[None, :, :, None]
    s = jnp.exp(t_len * lg)[None, :, None, None] * s0 + jnp.einsum('bjhk,bjhv->bhkv', kd, v)
    return s, o

def causal_conv(x, buf, w, b):
    t_len = x.shape[1]
    xx = jnp.concatenate([buf.astype(x.dtype), x], axis=1)
    y = b + xx[:, 0:t_len] * w[0]
    for i in range(1, CONV_W):
        y = y + xx[:, i:i + t_len] * w[i]
    return y, xx[:, -(CONV_W - 1):]

def rglru(x, h0, wa, ba, wx, bx, lam):
    b, t_len = x.shape[:2]
    xb = x.reshape(b, t_len, HC, BWC)
    r = jax.nn.sigmoid(jnp.einsum('bthi,hij->bthj', xb, wa).reshape(b, t_len, WC) + ba)
    i = jax.nn.sigmoid(jnp.einsum('bthi,hij->bthj', xb, wx).reshape(b, t_len, WC) + bx)
    log_a = -LRU_C * r * jax.nn.softplus(-lam)
    a = jnp.exp(log_a)
    u = jnp.sqrt(-jnp.expm1(2.0 * log_a)) * (i * x)

    def comb(left, right):
        al, bl = left
        ar, br = right
        return al * ar, ar * bl + br

    a_cum, b_cum = lax.associative_scan(comb, (a, u), axis=1)
    return a_cum * h0[:, None] + b_cum

def gla_chunk(s0, q, k, v, la):
    t_len = q.shape[1]
    bc = jnp.cumsum(la, axis=1)
    causal = jnp.tril(jnp.ones((t_len, t_len), dtype=bool))
    diff = bc[:, :, None] - bc[:, None, :]
    dec = jnp.exp(jnp.where(causal[None, :, :, None, None], diff, -jnp.inf))
    a = jnp.einsum('bthk,bjhk,btjhk->bhtj', q, k, dec)
    o = jnp.einsum('bhtj,bjhv->bthv', a, v) + jnp.einsum('bthk,bhkv->bthv', q * jnp.exp(bc), s0)
    b_last = bc[:, -1:]
    s = jnp.exp(bc[:, -1])[..., None] * s0 + jnp.einsum('bjhk,bjhv->bhkv', k * jnp.exp(b_last - bc), v)
    return s, o

def hier_moe(x, rg_w, rg_b, re_w, re_b, w1, w3, w2):
    b, l, d = x.shape
    t = x.reshape(-1, d)
    pg = jax.nn.softmax((t @ rg_w + rg_b).astype(F32), axis=-1)
    pg_top, g_idx = lax.top_k(pg, 1)
    g_oh = jax.nn.one_hot(g_idx[:, 0], N_GROUPS, dtype=F32)
    le = (t @ re_w + re_b).astype(F32).reshape(-1, N_GROUPS, EXP_PER_GROUP)
    le_sel = jnp.einsum('ng,nge->ne', g_oh, le)
    e_val, e_idx = lax.top_k(le_sel, TOP_K_IN)
    wts = jax.nn.softmax(e_val, axis=-1) * pg_top
    in_gate = jnp.sum(jax.nn.one_hot(e_idx, EXP_PER_GROUP, dtype=F32) * wts[..., None], axis=1)
    gate = (g_oh[:, :, None] * in_gate[:, None, :]).reshape(-1, N_EXPERTS)
    h = jax.nn.silu(jnp.einsum('nd,edf->nef', t, w1)) * jnp.einsum('nd,edf->nef', t, w3)
    h = h * gate[..., None].astype(h.dtype)
    return jnp.einsum('nef,efd->nd', h, w2).reshape(b, l, d)

def layer(x, l, p, pos0, kv_past, ret_s0, conv_buf, lru_h0, gla_s0):
    b, l_len, _ = x.shape
    prompt = kv_past is None
    xn = rms_norm(x, p['norm1'])
    aq, ak, av, bq, bk, bv, bg, cx, cg, dq, dk, dv, dr, da = project(xn, p['w_in'])

    qa = rms_norm(aq.reshape(b, l_len, HA, 2, DQA), p['qn']).astype(F32) * (DQA ** -0.5)
    ka = rms_norm(ak.reshape(b, l_len, HA, 2, DQA), p['kn'])
    va = av.reshape(b, l_len, HA, DVA)
    lam_init = 0.8 - 0.6 * math.exp(-0.3 * l)
    lv = p['lam'].astype(F32)
    lam = jnp.exp(jnp.sum(lv[0] * lv[1])) - jnp.exp(jnp.sum(lv[2] * lv[3])) + lam_init
    if prompt:
        oa = diff_attn_prompt(qa, ka.astype(F32), va, lam)
    else:
        k_past, v_past = kv_past
        k_all = jnp.concatenate([k_past.astype(F32), ka.astype(F32)], axis=1)
        v_all = jnp.concatenate([v_past.astype(va.dtype), va], axis=1)
        oa = diff_attn_block(qa, k_all, v_all, pos0 + jnp.arange(l_len), jnp.arange(pos0 + l_len), lam)
    oa = (rms_norm(oa, p['an']) * (1.0 - lam_init)).reshape(b, l_len, BRANCH_W).astype(x.dtype)

    pos = pos0 + jnp.arange(l_len)
    qb = rotary(bq.reshape(b, l_len, HB, DKB).astype(F32), pos)
    kb = rotary(bk.reshape(b, l_len, HB, DKB).astype(F32), pos) * (DKB ** -0.5)
    vb = bv.reshape(b, l_len, HB, DVB).astype(F32)
    chunk, pad = (RET_CHUNK, (-N_META) % RET_CHUNK) if prompt else (l_len, 0)
    s_ret, ob = chunked(ret_chunk, ret_s0, chunk, pad, qb, kb, vb)
    ob = (group_norm(ob, p['rn']).reshape(b, l_len, BRANCH_W) * jax.nn.silu(bg.astype(F32))).astype(x.dtype)

    xc, conv_new = causal_conv(cx.astype(F32), conv_buf, p['conv_w'], p['conv_b'])
    h = rglru(xc, lru_h0, p['lru_wa'], p['lru_ba'], p['lru_wx'], p['lru_bx'], p['lru_lam'])
    oc = (h * jax.nn.gelu(cg.astype(F32))).astype(x.dtype)

    qd = dq.reshape(b, l_len, HD, DKD).astype(F32) * (DKD ** -0.5)
    kd = dk.reshape(b, l_len, HD, DKD).astype(F32)
    vd = dv.reshape(b, l_len, HD, DVD).astype(F32)
    la = (jax.nn.log_sigmoid(da.astype(F32) @ p['gla_w2'].astype(F32) + p['gla_b']) / GLA_TAU).reshape(b, l_len, HD, DKD)
    chunk, pad = (GLA_CHUNK, (-N_META) % GLA_CHUNK) if prompt else (l_len, 0)
    s_gla, od = chunked(gla_chunk, gla_s0, chunk, pad, qd, kd, vd, la)
    od = (rms_norm(od, p['gn']).reshape(b, l_len, BRANCH_W) * jax.nn.silu(dr.astype(F32))).astype(x.dtype)

    gates = jax.nn.sigmoid(xn @ p['w_merge'] + p['b_merge']).reshape(b, l_len, N_BRANCH, D_MODEL)
    br = jnp.stack([oa, ob, oc, od], axis=2)
    proj = jnp.einsum('blnw,nwd->blnd', br, p['w_branch'])
    hres = x + jnp.sum(gates * proj, axis=2) @ p['w_out']

    y = hres + hier_moe(rms_norm(hres, p['norm2']), p['rg_w'], p['rg_b'], p['re_w'], p['re_b'],
                        p['ex_w1'], p['ex_w3'], p['ex_w2'])
    new = (ka.reshape(b, l_len, HA, 2 * DQA), va, s_ret, h[:, -1], conv_new, s_gla)
    return y, new

def setup_inputs(seed: int = 0) -> dict:
    key = jax.random.key(seed)
    ks = jax.random.split(key, 40)

    def nrm(i, shape, scale):
        return jax.random.normal(ks[i], shape, F32) * scale

    def gain(i, shape):
        return 1.0 + 0.02 * jax.random.normal(ks[i], shape, F32)

    n_pages = PAST_LEN // PAGE_SIZE
    n_used = DEC_BATCH * n_pages
    n_phys = n_used + max(1, n_used // 4)
    page_table = jax.random.permutation(ks[0], n_phys)[:n_used].reshape(DEC_BATCH, n_pages).astype(jnp.int32)
    u = jax.random.uniform(ks[1], (DEPTH, WC), F32, 0.9, 0.999)
    s = u ** (1.0 / LRU_C)
    lru_lam = jnp.log(s) - jnp.log1p(-s)
    return {
        'x_prompt': nrm(2, (BATCH, SEQ, D_MODEL), 1.0),
        'x_sample': nrm(3, (DEC_BATCH, DEC_SEQ, D_MODEL), 1.0),
        'cache_k_a': nrm(4, (DEPTH, n_phys, PAGE_SIZE, HA, 2 * DQA), 1.0),
        'cache_v_a': nrm(5, (DEPTH, n_phys, PAGE_SIZE, HA, DVA), 1.0),
        'state_ret': nrm(6, (DEPTH, DEC_BATCH, HB, DKB, DVB), 0.5),
        'state_lru_h': nrm(7, (DEPTH, DEC_BATCH, WC), 0.5),
        'state_lru_conv': nrm(8, (DEPTH, DEC_BATCH, CONV_W - 1, WC), 1.0),
        'state_gla': nrm(9, (DEPTH, DEC_BATCH, HD, DKD, DVD), 0.5),
        'page_table': page_table,
        'meta': nrm(10, (N_META, D_MODEL), 1.0),
        'norm1': gain(11, (DEPTH, D_MODEL)),
        'w_in': nrm(12, (DEPTH, D_MODEL, IN_W), D_MODEL ** -0.5),
        'qn': gain(13, (DEPTH, DQA)),
        'kn': gain(14, (DEPTH, DQA)),
        'lam': nrm(15, (DEPTH, 4, DQA), 0.1),
        'an': gain(16, (DEPTH, DVA)),
        'rn': gain(17, (DEPTH, DVB)),
        'conv_w': nrm(18, (DEPTH, CONV_W, WC), CONV_W ** -0.5),
        'conv_b': nrm(19, (DEPTH, WC), 0.01),
        'lru_wa': nrm(20, (DEPTH, HC, BWC, BWC), BWC ** -0.5),
        'lru_ba': nrm(21, (DEPTH, WC), 0.01),
        'lru_wx': nrm(22, (DEPTH, HC, BWC, BWC), BWC ** -0.5),
        'lru_bx': nrm(23, (DEPTH, WC), 0.01),
        'lru_lam': lru_lam,
        'gla_w2': nrm(24, (DEPTH, GLA_RANK, HD * DKD), GLA_RANK ** -0.5),
        'gla_b': nrm(25, (DEPTH, HD * DKD), 0.01),
        'gn': gain(26, (DEPTH, DVD)),
        'w_branch': nrm(27, (DEPTH, N_BRANCH, BRANCH_W, D_MODEL), BRANCH_W ** -0.5),
        'w_merge': nrm(28, (DEPTH, D_MODEL, N_BRANCH * D_MODEL), D_MODEL ** -0.5),
        'b_merge': nrm(29, (DEPTH, N_BRANCH * D_MODEL), 0.01),
        'w_out': nrm(30, (DEPTH, D_MODEL, D_MODEL), D_MODEL ** -0.5),
        'norm2': gain(31, (DEPTH, D_MODEL)),
        'rg_w': nrm(32, (DEPTH, D_MODEL, N_GROUPS), D_MODEL ** -0.5),
        'rg_b': nrm(33, (DEPTH, N_GROUPS), 0.01),
        're_w': nrm(34, (DEPTH, D_MODEL, N_EXPERTS), D_MODEL ** -0.5),
        're_b': nrm(35, (DEPTH, N_EXPERTS), 0.01),
        'ex_w1': nrm(36, (DEPTH, N_EXPERTS, D_MODEL, D_EXPERT), D_MODEL ** -0.5),
        'ex_w3': nrm(37, (DEPTH, N_EXPERTS, D_MODEL, D_EXPERT), D_MODEL ** -0.5),
        'ex_w2': nrm(38, (DEPTH, N_EXPERTS, D_EXPERT, D_MODEL), D_EXPERT ** -0.5),
    }

def reference(x_prompt, x_sample, cache_k_a, cache_v_a, state_ret, state_lru_h, state_lru_conv, state_gla,
              page_table, meta, norm1, w_in, qn, kn, lam, an, rn, conv_w, conv_b, lru_wa, lru_ba, lru_wx,
              lru_bx, lru_lam, gla_w2, gla_b, gn, w_branch, w_merge, b_merge, w_out, norm2, rg_w, rg_b,
              re_w, re_b, ex_w1, ex_w3, ex_w2):
    bp, bd = x_prompt.shape[0], x_sample.shape[0]
    xp = jnp.concatenate([jnp.broadcast_to(meta.astype(x_prompt.dtype)[None], (bp, N_META, D_MODEL)), x_prompt], axis=1)
    xs = x_sample
    new_p, new_s = [], []
    for l in range(DEPTH):
        p = dict(norm1=norm1[l], w_in=w_in[l], qn=qn[l], kn=kn[l], lam=lam[l], an=an[l], rn=rn[l],
                 conv_w=conv_w[l], conv_b=conv_b[l], lru_wa=lru_wa[l], lru_ba=lru_ba[l], lru_wx=lru_wx[l],
                 lru_bx=lru_bx[l], lru_lam=lru_lam[l], gla_w2=gla_w2[l], gla_b=gla_b[l], gn=gn[l],
                 w_branch=w_branch[l], w_merge=w_merge[l], b_merge=b_merge[l], w_out=w_out[l], norm2=norm2[l],
                 rg_w=rg_w[l], rg_b=rg_b[l], re_w=re_w[l], re_b=re_b[l], ex_w1=ex_w1[l], ex_w3=ex_w3[l],
                 ex_w2=ex_w2[l])
        xp, st = layer(xp, l, p, 0, None,
                       jnp.zeros((bp, HB, DKB, DVB), F32), jnp.zeros((bp, CONV_W - 1, WC), F32),
                       jnp.zeros((bp, WC), F32), jnp.zeros((bp, HD, DKD, DVD), F32))
        new_p.append(st)
        kv_past = (cache_k_a[l][page_table].reshape(bd, -1, HA, 2, DQA),
                   cache_v_a[l][page_table].reshape(bd, -1, HA, DVA))
        xs, st = layer(xs, l, p, PAST_LEN, kv_past, state_ret[l].astype(F32), state_lru_conv[l].astype(F32),
                       state_lru_h[l].astype(F32), state_gla[l].astype(F32))
        new_s.append(st)

    def stk(states, i, dt):
        return jnp.stack([s[i] for s in states]).astype(dt)

    dp, ds = x_prompt.dtype, x_sample.dtype
    return (xp[:, N_META:], xs,
            stk(new_p, 0, dp), stk(new_p, 1, dp), stk(new_p, 2, dp), stk(new_p, 3, dp), stk(new_p, 4, dp), stk(new_p, 5, dp),
            stk(new_s, 0, ds), stk(new_s, 1, ds), stk(new_s, 2, ds), stk(new_s, 3, ds), stk(new_s, 4, ds), stk(new_s, 5, ds))


_drawn_inputs = setup_inputs


def setup_inputs(seed=0):
    import zlib

    import numpy as np

    out = dict(_drawn_inputs(seed))
    spreads = {}
    factors = {'kn': 3.181,
     'an': 12.597,
     'rn': 18.628,
     'lru_ba': 26.613,
     'lru_bx': 8.0,
     'gla_b': 8.0,
     'gn': 22.658,
     'b_merge': 8.0,
     'rg_b': 24.165,
     're_b': 35.782,
     'norm2': 6.033}
    for name, (base, spread) in spreads.items():
        noise = np.random.default_rng([zlib.crc32(name.encode()), seed]).standard_normal(out[name].shape)
        drawn = base * np.exp(spread * noise) if base else spread * noise
        out[name] = __import__('jax').numpy.asarray(drawn.astype(out[name].dtype))
    for name, factor in factors.items():
        out[name] = (out[name] * factor).astype(out[name].dtype)
    return out
```

```python
from contextlib import ExitStack

import concourse.bass as bass
from concourse import mybir

F32 = mybir.dt.float32
I32 = mybir.dt.int32
ALU = mybir.AluOpType
ACT = mybir.ActivationFunctionType
X = mybir.AxisListType.X

P = 128
DM = 1024
KT = DM // P
META, SEQ, DEC = 16, 512, 8
L = META + SEQ
T = L + DEC
HT = T // 2
N = SEQ + DEC
HN = N // 2
NB = 5
TAIL = L - 4 * P
H = 4
PAST, PAGE = 2048, 128
PAGES = PAST // PAGE
HALF = PAGES // 2
SLOTS = PAGES + 1
XT = L + 2 * DEC
NV = 2
GROUPS = 64 // NV
NE = 16
PAIRS = NE // 2
RB = N // NB
WCH = 1280
RING = 6
EPS = 1e-6
LAM0 = 0.8 - 0.6
NEG = -1.0e30

C_ID, C_PERM, C_B32, C_B64, C_ONE = 0, 128, 256, 384, 512
C_SEL = 640
C_COS = C_SEL + 159
C_SIN = C_COS + T
C_DT = C_SIN + T
C_MASK = C_DT + H * L
C_DEC = C_MASK + 144
C_GAM = C_DEC + NB * H
C_NEW = C_GAM + 2
C_EPS = C_NEW + 1
C_W = C_EPS + 1

V_N1, V_N2, V_QN, V_KN, V_AN, V_RN, V_GN = 0, 8, 16, 17, 18, 19, 20
V_CW, V_CB, V_BA, V_BX, V_LL, V_GB, V_BM, V_RB = 22, 30, 32, 34, 36, 38, 39, 71
V_LAM, V_ST = 91, 219
V_WA = V_ST + 64
V_WX = V_WA + 256
V_RW = V_WX + 256
V_DA = V_RW + 160
V_G2 = V_DA + 128
V_W = V_G2 + 128

PROJ = (["AQ0", "AQ1", "AK0", "AK1", "V0", "V1", "V2", "V3", "AMS0", "AMS1", "AMS2", "AMS3",
         "BQ0", "BQ1", "BK0", "BK1", "BG0", "BG1", "ROT0", "ROT1", "ROT2", "ROT3",
         "CX0", "CX1", "CG0", "CG1", "DQ", "DK", "DV0", "DV1", "DR0", "DR1", "DA", "LA"]
        + ["BMEAN0", "BMEAN1", "BVAR0", "BVAR1", "CR0", "CR1", "CI0", "CI1"]
        + [f"{k}{n}{m}" for n in "BC" for m in range(KT) for k in "GP"]
        + [f"GD{m}" for m in range(KT)] + ["AOS0", "AOS1"]
        + [f"{k}A{m}" for m in range(KT) for k in "GP"]
        + ["DOS"] + [f"PD{m}" for m in range(KT)])
AT = {name: i for i, name in enumerate(PROJ)}
UNIT0 = AT["BK0"]
CHUNKS = ["AQ0", "AQ1", "AK0", "AK1", "V0", "V1", "V2", "V3", "BQ0", "BQ1", "BK0", "BK1",
          "BG0", "BG1", "CX0", "CX1", "CG0", "CG1", "DQ", "DK", "DV0", "DV1", "DR0", "DR1"]
N_IN = len(CHUNKS)
MERGES = [f"G{n}{m}" for n in "BC" for m in range(KT)] + [f"GD{m}" for m in range(KT)] + [f"GA{m}" for m in range(KT)]
BR = {"A": 0, "B": 2, "C": 4, "D": 6}
CH = CHUNKS + MERGES + ["DP0", "DP1"] + [f"WO{m}" for m in range(KT)]
CAT = {name: i for i, name in enumerate(CH)}


def program(nc, w_in, w_mg, w_dp, w_out, w_ex, xT_d, const_d, vec_d, ret0_d, gla0_d, kc, vc, pt, o):
    with ExitStack() as ctx:
        def sb(name, cols, dt=F32):
            return ctx.enter_context(nc.sbuf_tensor(name, [P, cols], dt))

        def sem(name):
            return ctx.enter_context(nc.semaphore(name))

        def scratch(name, shape):
            return nc.dram_tensor(name, shape, F32, kind="Internal").ap()

        scr_qk = scratch("scr_qk", (DEC, 512))
        scr_v = scratch("scr_v", (DEC, 512))
        scr_dv = scratch("scr_dv", (256, XT))
        scr_gate = scratch("scr_gate", (NE, N))

        cst = sb("cst", C_W)
        vec = sb("vec", V_W)
        xn = sb("xn", KT * T)
        ring = sb("ring", RING * WCH)
        sgd = sb("sgd", KT * N)
        qk = sb("qk", 8 * T)
        bg, cg, dr = sb("bg", 2 * T), sb("cg", 2 * T), sb("dr", 2 * T)
        cx = sb("cx", 2 * (L + 3))
        dqk = sb("dqk", 2 * XT)
        dv = sb("dv", 2 * XT)
        ea = sb("ea", NV * XT)
        vtok = sb("vtok", NB * 512)
        br = sb("br", 8 * N)
        kv = sb("kv", SLOTS * 256)
        tmp = sb("tmp", 4288)
        qb = sb("qb", 2144)
        sgt = sb("sgt", 2 * N)
        g0 = sb("g0", 512)
        small = sb("small", 200)
        pts = ctx.enter_context(nc.sbuf_tensor("pts", [1, DEC * PAGES], I32))
        ps = ctx.enter_context(nc.psum_tensor("ps", [P, 8, 512], F32))

        def cc(at, n=1, rows=slice(0, P)):
            return cst[rows, at:at + n]

        def vv(at, n=1, rows=slice(0, P)):
            return vec[rows, at:at + n]

        def view(t, off, *dims):
            n = 1
            for d in dims:
                n *= d
            a = t[:, off:off + n]
            if len(dims) == 1:
                return a
            names = "abcd"[:len(dims)]
            return a.rearrange(f"p ({' '.join(names)}) -> p {' '.join(names)}", **dict(zip(names[1:], dims[1:])))

        ident = cc(C_ID, P)
        xnv, xraw = view(xn, 0, KT, T), view(tmp, 0, KT, T)
        tT = view(xn, 0, KT, N)
        aqk, bqk = view(qk, 0, 4, T), view(qk, 4 * T, 4, T)
        acc = view(qk, 0, KT, N)
        bgv, cgv, drv = view(bg, 0, 2, T), view(cg, 0, 2, T), view(dr, 0, 2, T)
        cxv = view(cx, 0, 2, L + 3)
        dqv, dkv = dqk[:, 0:XT], dqk[:, XT:2 * XT]
        dvv = view(dv, 0, 2, XT)
        gst = view(dv, 0, 1 + DEC, 64)
        vt = view(vtok, 0, NB, 512)
        brv = view(br, 0, 8, N)
        sgv, sgtv = view(sgd, 0, KT, N), view(sgt, 0, 2, N)
        ptv = view(cst, C_COS, 2, N)
        kvv = view(kv, 0, SLOTS, 256)
        kvb = [kvv[:, 0:HALF, :], kvv[:, HALF:SLOTS, :]]
        asq, arr = view(tmp, 0, 4, T), view(tmp, 4 * T, 4, T)
        prb = view(tmp, 0, 2, 2, L)
        wtb = view(tmp, 4 * L, 2, NB, P)
        rot = view(qb, 0, 2, T)
        xc = view(qb, 2 * T, 2, T)
        atb = view(tmp, 0, 2, 512)
        kdv = view(tmp, 1024, NB, 256)
        rv = view(tmp, 2304, 2, DEC, 64)
        rs0 = view(qb, 0, 2, DEC, 64)
        rst = sgd[0:64, 2000:2256].rearrange("p (h v) -> p h v", h=H)
        bn, bsd = view(tmp, 0, 2, N), view(sgt, 0, 2, N)
        osq, osd = view(kv, 0, 2, N), view(kv, 2 * N, 2, N)
        rr, ri = view(tmp, 0, 2, T), view(tmp, 2 * T, 2, T)
        aa, th = view(tmp, 4 * T, 2, T), view(tmp, 6 * T, 2, T)
        xxs = view(small, 0, 2, DEC, 4)
        cst_out = view(small, 64, 2, 36)
        sc = small[:, 136:200]
        S = view(cst, C_DT, DEC, SLOTS, 8)
        W = view(cst, C_DT + 1088, DEC, SLOTS, 4)
        mx, sm = view(cst, C_DT + 1632, 64), view(cst, C_DT + 1696, 64)
        mxb, mx1 = cst[0:64, C_DT + 1760:C_DT + 1888], cst[0:64, C_DT + 1888:C_DT + 1889]
        Mb = view(cst, C_DT + 1900, DEC, 8)
        qbc = view(qb, 0, DEC, 256)
        qk8 = sgt[0:DEC, 0:512]
        vb = view(tmp, 0, 2, NV, XT)
        pbv = view(tmp, 2 * NV * XT, 2, NV, L)
        dg = view(sgd, 0, 2, T)
        das = sgt[0:16, 0:T]
        hres = view(tmp, 0, KT, N)
        sq = view(br, 0, KT, N)
        hh = view(br, 0, 4, N)
        gbc = view(br, 4 * N, 2, N)
        si, rstd = view(sgd, 0, 2, N), view(sgd, 2 * N, N)
        lg = view(sgd, 3 * N, NB, 20)
        gate = view(sgd, 3 * N + 100, NB, NE)
        rt = view(sgd, 3 * N + 180, 20, NB, 4)
        gT = sgt[0:NE, 0:N]

        w_ld = [sem(f"w_ld{i}") for i in range(RING)]
        ld_x, ld_c, ld_v, ld_pt, ld_g0 = sem("ld_x"), sem("ld_c"), sem("ld_v"), sem("ld_pt"), sem("ld_g0")
        ld_rs, ld_q = sem("ld_rs"), sem("ld_q")
        x_sq, x_used = sem("x_sq"), sem("x_used")
        xms, xsd, xn_ok = sem("xms"), sem("xsd"), sem("xn_ok")
        pj, pj_free = sem("pj"), sem("pj_free")
        a_sq, a_ok = sem("a_sq"), sem("a_ok")
        t8, t8_ev, s_qk, s_v = sem("t8"), sem("t8_ev"), sem("s_qk"), sem("s_v")
        sco, smx, sexp, scomb = sem("sco"), sem("smx"), sem("sexp"), sem("scomb")
        swt, swt_ev, sav, sav_ev = sem("swt"), sem("swt_ev"), sem("sav"), sem("sav_ev")
        rot_ok, conv_ok = sem("rot_ok"), sem("conv_ok")
        at_s, at_w, at_o, ob_ev = sem("at_s"), sem("at_w"), sem("at_o"), sem("ob_ev")
        kt_t, kd_ok, st_mm, st_ev = sem("kt_t"), sem("kd_ok"), sem("st_mm"), sem("st_ev")
        rs_ok, ro_mm, b_raw = sem("rs_ok"), sem("ro_mm"), sem("b_raw")
        b_cen, b_sq, br_ok = sem("b_cen"), sem("b_sq"), sem("br_ok")
        c_par, c_act, c_q, c_ok, c_out = sem("c_par"), sem("c_act"), sem("c_q"), sem("c_ok"), sem("c_out")
        mg, mg_used = sem("mg"), sem("mg_used")
        kv_ld = [sem("kv_ld0"), sem("kv_ld1")]
        k_used, v_used = sem("k_used"), sem("v_used")
        s_mx, s_mxt, s_mx1, s_mxm, s_sub, s_exp, s_sum, s_tot, s_w = [sem(f"smp{i}") for i in range(9)]
        s_av, a_raw, a_osq = sem("s_av"), sem("a_raw"), sem("a_osq")
        la_z, la_e, la_m, dg_in, s_dv = sem("la_z"), sem("la_e"), sem("la_m"), sem("dg_in"), sem("s_dv")
        vb_ld = [sem("vb_ld0"), sem("vb_ld1")]
        vb_s0, g_scan, g_st, g_p, g_mm = sem("vb_s0"), sem("g_scan"), sem("g_st"), sem("g_p"), sem("g_mm")
        d_raw, d_sq = sem("d_raw"), sem("d_sq")
        wo, wo_free, ld_x2 = sem("wo"), sem("wo_free"), sem("ld_x2")
        h_sq, n2, n2_sd, t_ok = sem("h_sq"), sem("n2"), sem("n2_sd"), sem("t_ok")
        lgm, r1, r2, g_ok, g_t, g_ev = sem("lgm"), sem("r1"), sem("r2"), sem("g_ok"), sem("g_t"), sem("g_ev")
        s_gate, gb_ld = sem("s_gate"), sem("gb_ld")
        e_h1, e_s, e_h3, e_t, e_h, e_y, e_acc = [sem(f"e_{k}") for k in ("h1", "s", "h3", "t", "h", "y", "acc")]
        dch, ach, pch, outs = sem("dch"), sem("ach"), sem("pch"), sem("outs")
        y_out = sem("y_out")
        kv0, ea_ok, rst_out, rs_out = sem("kv0"), sem("ea_ok"), sem("rst_out"), sem("rs_out")
        k_out, par, lam_e, c_st, d_sd = sem("k_out"), sem("par"), sem("lam_e"), sem("c_st"), sem("d_sd")
        block = ctx.enter_context(nc.Block())

        class Chain:
            def __init__(self, eng, s):
                self.eng, self.s, self.n = eng, s, 0

            def __call__(self, ins):
                self.n += 1
                ins.then_inc(self.s, 1)
                self.eng.wait_ge(self.s, self.n)

        def bank2(pair, w, base=0):
            return ps[:, 2 * pair + base:2 * pair + base + 2, 0:w]

        def fold(a, w):
            return a.rearrange("p (a b) -> p a b", a=2)

        POOL_OUTS = 4

        @block.sync
        def _(sp):
            def reader_done(c):
                name = CH[c]
                if name in MERGES and name[1] != "D":
                    sp.wait_ge(pj, AT["P" + name[1:]] + 1)
                elif name.startswith("DP"):
                    sp.wait_ge(pj, AT[f"PD{4 * int(name[2]) + 3}"] + 1)
                elif name.startswith("WO"):
                    sp.wait_ge(wo, int(name[2]) + 1)
                else:
                    sp.wait_ge(pj, AT[name] + 1)

            def chunk(c):
                name = CH[c]
                if c >= RING:
                    reader_done(c - RING)
                if name in CHUNKS:
                    src, n = w_in[c], 1024
                elif name in MERGES:
                    src, n = w_mg[c - N_IN], 1280
                elif name.startswith("DP"):
                    src, n = w_dp[int(name[2])], 1024
                else:
                    src, n = w_out[int(name[2])], 1024
                s = c % RING
                sp.dma_start(ring[:, s * WCH:s * WCH + n], src).then_inc(w_ld[s], 16)

            def cache(j):
                b, half, is_v = j % 16 // 2, j % 2, j // 16
                if j >= 2:
                    i = j - 2
                    sp.wait_ge(*((k_used, i + 1) if i < 16 else (v_used, i - 15)))
                if j == 0:
                    sp.wait_ge(ld_pt, 16)
                    sp.wait_ge(kv0, 1)
                src = vc if is_v else kc
                for g in range(HALF):
                    at = b * PAGES + half * HALF + g
                    page = sp.value_load(pts[0:1, at:at + 1], min_val=0, max_val=kc.shape[0] - 1)
                    sp.dma_start(kvb[half][:, g, :], src[bass.ds(page, 1), :, :].rearrange("a p c -> (a p) c"))\
                      .then_inc(kv_ld[half], 16)
                if half:
                    if j == 1:
                        sp.wait_ge(s_qk, 16)
                        sp.wait_ge(s_v, 16)
                    row = scr_v[b:b + 1, 0:256] if is_v else scr_qk[b:b + 1, 256:512]
                    sp.dma_start(kvb[1][0:1, HALF, :], row).then_inc(kv_ld[1], 16)

            def values(j):
                if j >= 2:
                    sp.wait_ge(g_p, j - 1)
                    sp.wait_ge(g_st, j - 1)
                else:
                    sp.wait_ge(s_dv, 16)
                    sp.wait_ge(br_ok, 2)
                for h in range(H):
                    src = scr_dv[h * 64 + j * NV:h * 64 + (j + 1) * NV, :]
                    sp.dma_start(vb[32 * h:32 * h + 32, j % 2, :, :], src.partition_broadcast(32))\
                      .then_inc(vb_ld[j % 2], 16)

            sp.dma_start(xraw, xT_d).then_inc(ld_x, 16)
            for c in range(RING):
                chunk(c)
            sp.dma_start(pts[0:1, :], pt).then_inc(ld_pt, 16)
            sp.dma_start(g0[:, :], gla0_d).then_inc(ld_g0, 16)
            c = RING
            while c < CAT["BG0"]:
                chunk(c)
                c += 1
            sp.wait_ge(xn_ok, 1)
            cache(0)
            cache(1)
            while c < CAT["GB0"]:
                chunk(c)
                c += 1
            sp.wait_ge(rot_ok, 4)
            sp.dma_start(rs0, ret0_d).then_inc(ld_rs, 16)
            sp.wait_ge(sav, 16)
            for h in range(H):
                sp.dma_start(rv[64 * (h % 2):64 * (h % 2) + 64, h // 2, :, :],
                             scr_v[:, 256 + h * 64:256 + h * 64 + 64].partition_broadcast(64)).then_inc(ld_rs, 16)
            while c < CAT["GC0"]:
                chunk(c)
                c += 1
            sp.wait_ge(br_ok, 2)
            sp.wait_ge(rs_out, 16)
            sp.dma_start(qbc, scr_qk[:, 0:256].partition_broadcast(P)).then_inc(ld_q, 16)
            for j in range(2, 18):
                cache(j)
                if j % 2 and c < CAT["GD2"]:
                    chunk(c)
                    c += 1
            values(0)
            values(1)
            for j in range(18, 32):
                while c < min(CAT["GD0"] + (j - 18) // 2 + 3, CAT["GA0"]):
                    chunk(c)
                    c += 1
                cache(j)
            for j in range(2, GROUPS):
                while c < min(CAT["GA0"] + (j - 2) // 4 + 4, len(CH)):
                    chunk(c)
                    c += 1
                values(j)
            while c < len(CH):
                chunk(c)
                c += 1
            sp.wait_ge(g_mm, GROUPS)
            sp.dma_start(hres, xT_d[:, :, META:T]).then_inc(ld_x2, 16)
            def expert(p, q):
                s = q % RING
                src = w_ex[p, q] if isinstance(p, int) else w_ex[bass.ds(p, 1), q, :, :].rearrange("a p n -> (a p) n")
                sp.dma_start(ring[:, s * WCH:s * WCH + 1024], src).then_inc(w_ld[s], 16)

            def second_half(p):
                for q in range(6, 12):
                    sp.wait_ge(e_h3 if q % 2 else e_h1, p * 4 + (q - 6) // 2 + 1)
                    expert(p, q)

            for q in range(6):
                sp.wait_ge(wo, q + 3)
                expert(0, q)
            with sp.Fori(0, PAIRS - 1) as p:
                second_half(p)
                sp.wait_ge(s_gate, 16)
                sp.dma_start(gbc, scr_gate[bass.ds(p * 2, 2), :].partition_broadcast(P)).then_inc(gb_ld, 16)
                for q in range(6):
                    if q < 2:
                        sp.wait_ge(e_h3 if q % 2 else e_h1, p * 4 + 4)
                    else:
                        sp.wait_ge(e_y, p * KT + 2 * q - 2)
                    expert(p + 1, q)
            second_half(PAIRS - 1)
            sp.wait_ge(e_h, 4 * (PAIRS - 1))
            sp.dma_start(gbc, scr_gate[2 * PAIRS - 2:2 * PAIRS, :].partition_broadcast(P)).then_inc(gb_ld, 16)
            for m in range(KT):
                sp.wait_ge(e_acc, KT * (PAIRS - 1) + m + 1)
                sp.dma_start(o["y"][:, m, :], hres[:, m, :]).then_inc(y_out, 16)
            sp.wait_ge(y_out, 16 * KT)

        @block.tensor
        def _(pe):
            def loaded(c):
                pe.wait_ge(w_ld[c % RING], 16 * (c // RING + 1))

            def wsl(c, k, n=P):
                s = c % RING * WCH
                return ring[:, s + k * P:s + k * P + n]

            def free(t):
                if t >= 2:
                    pe.wait_ge(pj_free, t - 1)

            def stat(name, lhsT, srcs, hw):
                t = AT[name]
                free(t)
                for h in range(2):
                    for i, s in enumerate(srcs):
                        mm = pe.matmul(ps[:, 2 * (t % 2) + h, 0:hw], lhsT, s[:, h * hw:(h + 1) * hw],
                                       start=(i == 0), stop=(i == len(srcs) - 1))
                mm.then_inc(pj, 1)

            def tiled(name, hw=HT, col0=0):
                t, c = AT[name], CAT[name]
                free(t)
                loaded(c)
                for h in range(2):
                    for k in range(KT):
                        mm = pe.matmul(ps[:, 2 * (t % 2) + h, 0:hw], wsl(c, k),
                                       xnv[:, k, col0 + h * hw:col0 + (h + 1) * hw], start=(k == 0), stop=(k == KT - 1))
                mm.then_inc(pj, 1)

            pe.wait_ge(ld_c, 16)
            for k in range(KT):
                pe.wait_ge(x_sq, k + 1)
                for h in range(2):
                    mm = pe.matmul(ps[:, 4 + h, 0:HT], cc(C_ONE, P), view(kv, (k % 2) * T, 2, HT)[:, h, :],
                                   start=(k == 0), stop=(k == KT - 1))
                mm.then_inc(xms, 1)
            pe.wait_ge(xn_ok, 1)
            pe.wait_ge(ld_v, 16)

            def values_tile(i):
                t, c = AT[f"V{i}"], CAT[f"V{i}"]
                free(t)
                loaded(c)
                for b in range(NB):
                    rows = min(P, T - b * P)
                    for k in range(KT):
                        mm = pe.matmul(ps[0:rows, 2 * (t % 2) + b // 4, (b % 4) * P:(b % 4 + 1) * P],
                                       xnv[:, k, b * P:b * P + rows], wsl(c, k), start=(k == 0), stop=(k == KT - 1))
                mm.then_inc(pj, 1)

            def scores(s):
                h, i = s // 4, s % 4
                n = META + P * (i + 1)
                if s >= 1:
                    pe.wait_ge(sexp, 2 * s)
                if n > 512:
                    pe.wait_ge(sav_ev, s - 1)
                for m in range(2):
                    r = slice(32 * ((2 * h + m) % 4), 32 * ((2 * h + m) % 4) + 32)
                    for a, b, bk, at in ((0, min(n, 512), 4 + m, 0), (512, n, 7, 256 + META * m)):
                        if a < b:
                            if bk == 7 and m:
                                pe.wait_ge(sco, 2 * s + 1)
                            mm = pe.matmul(ps[:, bk, at:at + b - a], aqk[r, h // 2, META + P * i:META + P * (i + 1)],
                                           aqk[r, 2 + h // 2, a:b], start=True, stop=True)
                    mm.then_inc(sco, 1)

            def wt_at(b):
                return (6, P * b) if b < 4 else (7, 0)

            def transposes(s):
                i = s % 4
                pe.wait_ge(scomb, s + 1)
                if s >= 1:
                    pe.wait_ge(swt_ev, s)
                if i == 3:
                    pe.wait_ge(sav_ev, s)
                for b in range(i + 2):
                    rows = P if b <= i else META
                    bk, c0 = wt_at(b)
                    mm = pe.transpose(ps[0:rows, bk, c0:c0 + P], prb[:, s % 2, 0, b * P:b * P + rows], ident)
                mm.then_inc(swt, 1)

            def weighted(s):
                h, i = s // 4, s % 4
                pe.wait_ge(swt_ev, s + 1)
                if s >= 1:
                    pe.wait_ge(sav_ev, s)
                if i == 2:
                    pe.wait_ge(sexp, 2 * s + 4)
                for b in range(i + 2):
                    rows = P if b <= i else META
                    mm = pe.matmul(ps[64 * (h % 2):64 * (h % 2) + 64, 7, 384:512], vt[0:rows, b, h * 64:h * 64 + 64],
                                   wtb[0:rows, s % 2, b, :], start=(b == 0), stop=(b == i + 1))
                mm.then_inc(sav, 1)

            def extras(name):
                s = AT[name] - UNIT0
                if s == 0:
                    pe.wait_ge(a_ok, 4)
                if 2 <= s < 18:
                    weighted(s - 2)
                if 1 <= s < 17:
                    transposes(s - 1)
                if 0 <= s < 16:
                    scores(s)

            for name in PROJ[:AT["LA"] + 1]:
                t = AT[name]
                if name == "BQ1":
                    pe.wait_ge(a_ok, 4)
                    for i in range(4):
                        mm = pe.transpose(ps[0:DEC, 4, i * P:(i + 1) * P], aqk[:, i, L:T], ident)
                    mm.then_inc(t8, 1)
                if name[0] == "V":
                    values_tile(int(name[1]))
                elif name.startswith("AMS"):
                    pe.wait_ge(a_sq, int(name[3]) + 1)
                    stat(name, cc(C_B32, P), [asq[:, int(name[3]), :]], HT)
                elif name.startswith("ROT"):
                    pe.wait_ge(pj_free, AT["BK1"] + 1)
                    stat(name, cc(C_PERM, P), [bqk[:, int(name[3]), :]], HT)
                elif name == "DA":
                    free(t)
                    for h in range(2):
                        for k in range(KT):
                            mm = pe.matmul(ps[0:16, 2 * (t % 2) + h, 0:HT], vv(V_DA + 16 * k, 16),
                                           xnv[:, k, h * HT:(h + 1) * HT], start=(k == 0), stop=(k == KT - 1))
                    mm.then_inc(pj, 1)
                elif name == "LA":
                    free(t)
                    pe.wait_ge(pj_free, AT["DA"] + 1)
                    for h in range(2):
                        mm = pe.matmul(ps[:, 2 * (t % 2) + h, 0:HT], vv(V_G2, P, slice(0, 16)),
                                       das[:, h * HT:(h + 1) * HT], start=True, stop=True)
                    mm.then_inc(pj, 1)
                else:
                    tiled(name)
                if UNIT0 <= t:
                    if t == UNIT0:
                        pe.wait_ge(t8_ev, 1)
                    extras(name)

            pe.wait_ge(rot_ok, 4)
            pe.wait_ge(sexp, 32)
            pe.wait_ge(swt_ev, 16)
            pe.wait_ge(sav_ev, 16)
            units = [(h, j) for h in range(H) for j in range(NB)]

            def ret_scores(u):
                h, j = units[u]
                rows, t0 = min(P, L - j * P), max(META, j * P)
                r = slice(64 * (h % 2), 64 * (h % 2) + 64)
                if u >= 2:
                    pe.wait_ge(at_w, u - 1)
                pe.matmul(ps[0:rows, 4 + u % 2, 0:L - t0], bqk[r, 2 + h // 2, j * P:j * P + rows],
                          bqk[r, h // 2, t0:L], start=True, stop=True).then_inc(at_s, 1)

            def ret_out(u):
                h, j = units[u]
                rows, t0 = min(P, L - j * P), max(META, j * P)
                pe.wait_ge(at_w, u + 1)
                pe.matmul(ps[64 * (h % 2):64 * (h % 2) + 64, 6 + h // 2, t0 - META:SEQ],
                          vt[0:rows, j, 256 + h * 64:256 + h * 64 + 64], atb[0:rows, u % 2, 0:L - t0],
                          start=(j == 0), stop=(j == NB - 1)).then_inc(at_o, 1)

            for u in range(len(units) + 1):
                if u < len(units):
                    ret_scores(u)
                if u >= 1:
                    ret_out(u - 1)
            for t in range(2):
                for b in range(4):
                    pe.transpose(ps[:, 4 + t, b * P:(b + 1) * P], bqk[:, 2 + t, b * P:(b + 1) * P], ident)
            pe.wait_ge(ob_ev, 1)
            for t in range(2):
                mm = pe.transpose(ps[0:TAIL, 6, t * P:(t + 1) * P], bqk[:, 2 + t, 4 * P:L], ident)
            mm.then_inc(kt_t, 1)
            pe.wait_ge(kd_ok, 1)
            pe.wait_ge(ob_ev, 2)
            for h in range(H):
                for b in range(NB):
                    rows = P if b < 4 else TAIL
                    mm = pe.matmul(ps[0:64, 7, h * 64:h * 64 + 64], kdv[0:rows, b, h * 64:h * 64 + 64],
                                   vt[0:rows, b, 256 + h * 64:256 + h * 64 + 64], start=(b == 0), stop=(b == NB - 1))
            mm.then_inc(st_mm, 1)
            pe.wait_ge(rs_ok, 1)
            for h in range(H):
                r = slice(64 * (h % 2), 64 * (h % 2) + 64)
                for b in range(DEC):
                    mm = pe.matmul(ps[r, 6, (h // 2) * DEC + b:(h // 2) * DEC + b + 1], rs0[r, h // 2, b, :],
                                   bqk[r, h // 2, L + b:L + b + 1], start=True, stop=True)
            mm.then_inc(ro_mm, 1)
            pe.wait_ge(b_raw, 1)
            for t in range(2):
                stat(f"BMEAN{t}", cc(C_B64, P), [brv[:, 2 + t, :]], HN)
            for t in range(2):
                pe.wait_ge(b_sq, t + 1)
                stat(f"BVAR{t}", cc(C_B64, P), [bn[:, t, :]], HN)

            for g, at in (("CR", V_WA), ("CI", V_WX)):
                for t in range(2):
                    pe.wait_ge(conv_ok, 2)
                    stat(f"{g}{t}", vv(at + t * P, P), [xc[:, t, :]], HT)

            def gate_tile(n, m):
                tiled(f"G{n}{m}", HN, META)

            def branch_tile(n, m):
                name = f"P{n}{m}"
                t = AT[name]
                free(t)
                if n == "D":
                    c = CAT["DP0"] + m // 4
                    loaded(c)
                for h in range(2):
                    for k in range(2):
                        w = (wsl(CAT["DP0"] + m // 4, (m % 4) * 2 + k) if n == "D" else wsl(CAT[f"G{n}{m}"], KT + k))
                        mm = pe.matmul(ps[:, 2 * (t % 2) + h, 0:HN], w,
                                       brv[:, BR[n] + k, h * HN:(h + 1) * HN], start=(k == 0), stop=(k == 1))
                mm.then_inc(pj, 1)

            for i, n in enumerate("BC"):
                for m in range(KT):
                    gate_tile(n, m)
                    if m == 0:
                        pe.wait_ge(br_ok, i + 1)
                    branch_tile(n, m)
            pe.wait_ge(s_mx, 1)
            pe.transpose(ps[0:64, 4, 0:P], mx, ident).then_inc(s_mxt, 1)
            pe.wait_ge(s_mx1, 1)
            pe.matmul(ps[:, 5, 0:64], mxb, cst[0:64, C_ID:C_ID + 64], start=True, stop=True).then_inc(s_mxm, 1)
            gate_tile("D", 0)
            pe.wait_ge(s_sum, 1)
            pe.matmul(ps[:, 5, 64:128], cc(C_ONE, P), sm, start=True, stop=True).then_inc(s_tot, 1)
            gate_tile("D", 1)
            pe.wait_ge(s_w, 1)

            def sample_values(j):
                b, half = j // 2, j % 2
                ns = HALF + half
                pe.wait_ge(kv_ld[half], (128, 144)[half] * (DEC + b + 1))
                for s in range(ns):
                    for t in range(2):
                        mm = pe.matmul(ps[:, 4 + t, 256 + 2 * b:256 + 2 * b + 2], kvb[half][:, s, t * P:(t + 1) * P],
                                       W[:, b, half * HALF + s, 2 * t:2 * t + 2],
                                       start=(half == 0 and s == 0), stop=(half == 1 and s == ns - 1))
                mm.then_inc(v_used, 1)

            j = 0
            for m in range(2, KT):
                gate_tile("D", m)
                for _ in range(3 if m < 6 else 2):
                    sample_values(j)
                    j += 1
            assert j == 16

            for t in range(2):
                pe.wait_ge(a_osq, t + 1)
                stat(f"AOS{t}", cc(C_B64, P), [osq[:, t, :]], HN)
            pe.wait_ge(st_ev, 1)

            def gla(j):
                pe.wait_ge(g_p, j + 1)
                for i in range(NV):
                    v = j * NV + i
                    g, v32 = v // 32, v % 32
                    lhsT = cst[:, C_SEL + 31 - v32:C_SEL + 31 - v32 + P]
                    pe.matmul(ps[:, 6 + g, 0:SEQ], lhsT, pbv[:, j % 2, i, 0:SEQ], start=(v32 == 0), stop=(v32 == 31))
                    mm = pe.matmul(ps[:, 4, g * DEC:(g + 1) * DEC], lhsT, pbv[:, j % 2, i, SEQ + 1:L:2],
                                   start=(v32 == 0), stop=(v32 == 31))
                mm.then_inc(g_mm, 1)

            for m in range(KT):
                gate_tile("A", m)
                gla(4 * m)
                gla(4 * m + 1)
                if m == 0:
                    pe.wait_ge(br_ok, 3)
                branch_tile("A", m)
                gla(4 * m + 2)
                gla(4 * m + 3)
            pe.wait_ge(d_sq, 2)
            stat("DOS", cc(C_B32, P), [osq[:, t, :] for t in range(2)], HN)
            pe.wait_ge(br_ok, 4)
            for m in range(KT):
                branch_tile("D", m)

            pe.wait_ge(mg_used, 4 * KT)
            for m in range(KT):
                c = CAT[f"WO{m}"]
                loaded(c)
                if m == 0:
                    pe.wait_ge(pj_free, len(PROJ))
                if m >= 4:
                    pe.wait_ge(wo_free, m - 3)
                for h in range(2):
                    for k in range(KT):
                        mm = pe.matmul(ps[:, 2 * (m % 4) + h, 0:HN], wsl(c, k), acc[:, k, h * HN:(h + 1) * HN],
                                       start=(k == 0), stop=(k == KT - 1))
                mm.then_inc(wo, 1)
            pe.wait_ge(wo_free, KT)
            for m in range(KT):
                pe.wait_ge(h_sq, m + 1)
                for h in range(2):
                    mm = pe.matmul(ps[:, h, 0:HN], cc(C_ONE, P), sq[:, m, h * HN:(h + 1) * HN],
                                   start=(m == 0), stop=(m == KT - 1))
            mm.then_inc(n2, 1)
            pe.wait_ge(t_ok, KT)
            for b in range(NB):
                for k in range(KT):
                    mm = pe.matmul(ps[0:RB, 6, b * 32:b * 32 + 20], tT[:, k, b * RB:(b + 1) * RB],
                                   vv(V_RW + 20 * k, 20), start=(k == 0), stop=(k == KT - 1))
            mm.then_inc(lgm, 1)

            def pair_of_experts(p, first=False):
                def chunk_loaded(q):
                    pe.wait_ge(w_ld[q % RING], 16 * (len(CH) // RING + q // RING + 1) + p * 32)

                for ef in range(4):
                    for three in range(2):
                        q = 2 * ef + three
                        chunk_loaded(q)
                        pe.wait_ge(e_t if three else e_s, p * 4 + ef)
                        for h in range(2):
                            for k in range(KT):
                                s = q % RING * WCH + k * P
                                mm = pe.matmul(ps[:, 2 * three + h, 0:HN], ring[:, s:s + P], tT[:, k, h * HN:(h + 1) * HN],
                                               start=(k == 0), stop=(k == KT - 1))
                        mm.then_inc(e_h3 if three else e_h1, 1)
                if first:
                    pe.wait_ge(g_ok, 1)
                    for b in range(NB):
                        mm = pe.transpose(ps[0:NE, 4 + b // 4, (b % 4) * RB:(b % 4 + 1) * RB], gate[0:RB, b, :],
                                          cst[0:RB, C_ID:C_ID + RB])
                    mm.then_inc(g_t, 1)
                    pe.wait_ge(g_ev, 1)
                pe.wait_ge(e_h, p * 4 + 4)
                for m in range(KT):
                    chunk_loaded(8 + m // 2)
                    if m >= 2:
                        pe.wait_ge(e_acc, p * KT + m - 1)
                    for h in range(2):
                        for k in range(4):
                            s = (8 + m // 2) % RING * WCH + ((m % 2) * 4 + k) * P
                            mm = pe.matmul(ps[:, 4 + 2 * (m % 2) + h, 0:HN], ring[:, s:s + P],
                                           hh[:, k, h * HN:(h + 1) * HN], start=(k == 0), stop=(k == 3))
                    mm.then_inc(e_y, 1)

            pair_of_experts(0, first=True)
            with pe.Fori(1, PAIRS) as p:
                pair_of_experts(p)

        @block.scalar
        def _(act):
            link = Chain(act, ach)
            act.dma_start(cst[:, :], const_d).then_inc(ld_c, 16)
            act.dma_start(vec[:, :], vec_d).then_inc(ld_v, 16)
            act.wait_ge(ld_x, 16)
            for k in range(KT):
                if k >= 2:
                    act.wait_ge(xms, k - 1)
                act.activation(view(kv, (k % 2) * T, T), xraw[:, k, :], ACT.Square).then_inc(x_sq, 1)
            act.wait_ge(ld_c, 16)
            act.wait_ge(ld_v, 16)
            eps = cc(C_EPS)
            act.wait_ge(xms, KT)
            act.activation(fold(view(kv, 0, T), HT), bank2(2, HT), ACT.Sqrt, bias=eps, scale=1.0 / DM).then_inc(xsd, 1)

            act.activation(xxs[:, :, :, 0:3], view(vec, V_ST, 2, DEC, 3), ACT.Copy).then_inc(c_st, 1)
            act.wait_ge(par, 1)
            act.activation(sc[:, 3:5], sc[:, 1:3], ACT.Exp).then_inc(lam_e, 1)
            link(act.activation(sc[:, 24:26], vv(V_LL, 2), ACT.Abs))
            act.activation(sc[:, 26:28], sc[:, 24:26], ACT.Exp, scale=-1.0).then_inc(lam_e, 1)

            def ready(name):
                act.wait_ge(pj, AT[name] + 1)
                return 2 * (AT[name] % 2)

            def pair(name, w):
                b = ready(name)
                return ps[:, b:b + 2, 0:w]

            def copy(name, dst, w, func=ACT.Copy, **kw):
                act.activation(fold(dst, w), pair(name, w), func, **kw).then_inc(pj_free, 1)

            def spread(name, dst, off=0, scale=1.0, smp=None):
                b = ready(name)
                act.activation(dst[:, off:off + HT], ps[:, b, 0:HT], ACT.Copy, scale=scale)
                act.activation(dst[:, off + HT:off + L], ps[:, b + 1, 0:L - HT], ACT.Copy, scale=scale)
                act.activation(smp, ps[:, b + 1, L - HT:HT], ACT.Copy, scale=scale).then_inc(pj_free, 1)

            def exps(s):
                i = s % 4
                n = META + P * (i + 1)
                if s >= 2:
                    act.wait_ge(swt, s - 1)
                for m in range(2):
                    act.wait_ge(smx, 2 * s + (2 if i == 3 else m + 1))
                    nb = sc[:, 8 + 2 * (s % 2) + m:9 + 2 * (s % 2) + m]
                    ins = act.activation(prb[:, s % 2, m, 0:min(n, 512)], ps[:, 4 + m, 0:min(n, 512)], ACT.Exp, bias=nb,
                                         accum_out=sc[:, 12 + 2 * (s % 2) + m:13 + 2 * (s % 2) + m])
                    if i == 3:
                        c0 = 256 + META * m
                        ins = act.activation(prb[:, s % 2, m, 512:n], ps[:, 7, c0:c0 + META], ACT.Exp, bias=nb,
                                             accum_out=sc[:, 36 + m:37 + m])
                    ins.then_inc(sexp, 1)

            def wt_copy(s):
                i = s % 4
                act.wait_ge(swt, s + 1)
                if s >= 2:
                    act.wait_ge(sav, s - 1)
                act.activation(wtb[:, s % 2, 0:i + 1, :], ps[:, 6, 0:(i + 1) * P].rearrange("p (a b) -> p a b", b=P),
                               ACT.Copy)
                src = ps[0:META, 7, 0:P] if i == 3 else ps[0:META, 6, P * (i + 1):P * (i + 2)]
                act.activation(wtb[0:META, s % 2, i + 1, :], src, ACT.Copy).then_inc(swt_ev, 1)

            for name in PROJ[:AT["LA"] + 1]:
                t = AT[name]
                kind, i = name[:-1], (int(name[-1]) if name[-1].isdigit() else 0)
                if kind in ("AQ", "AK"):
                    j = 2 * (kind == "AK") + i
                    act.activation(fold(aqk[:, j, :], HT), pair(name, HT), ACT.Copy).then_inc(pj_free, 1)
                    act.wait_ge(pj_free, t + 1)
                    act.wait_ge(xn_ok, 1)
                    act.activation(asq[:, j, :], aqk[:, j, :], ACT.Square).then_inc(a_sq, 1)
                elif kind == "V":
                    b = ready(name)
                    act.activation(vt[:, 0:4, i * P:(i + 1) * P], ps[:, b, :].rearrange("p (a c) -> p a c", c=P), ACT.Copy)
                    act.activation(vt[0:T - 4 * P, 4, i * P:(i + 1) * P], ps[0:T - 4 * P, b + 1, 0:P], ACT.Copy)\
                       .then_inc(pj_free, 1)
                    if i == 3:
                        act.wait_ge(pj_free, t + 1)
                        act.dma_start(scr_v[:, :], vt[TAIL:TAIL + DEC, 4, :]).then_inc(s_v, 16)
                elif kind == "AMS":
                    copy(name, arr[:, i, :], HT, ACT.Sqrt, bias=eps)
                elif kind == "BQ":
                    copy(name, bqk[:, i, :], HT)
                    if i == 1:
                        act.wait_ge(t8, 1)
                        link(act.activation(qk8, ps[0:DEC, 4, :], ACT.Copy))
                        act.sem_inc(t8_ev, 1)
                        act.dma_start(scr_qk[:, :], qk8).then_inc(s_qk, 16)
                elif kind == "BK":
                    copy(name, bqk[:, 2 + i, :], HT, ACT.Copy, scale=0.125)
                elif kind == "BG":
                    copy(name, bgv[:, i, :], HT, ACT.Silu)
                elif kind == "ROT":
                    if i >= 2:
                        act.wait_ge(rot_ok, i - 1)
                    copy(name, rot[:, i % 2, :], HT)
                elif kind == "CX":
                    spread(name, cxv[:, i, :], 3, smp=xxs[:, i, :, 3])
                elif kind == "CG":
                    copy(name, cgv[:, i, :], HT, ACT.Gelu_apprx_tanh)
                elif name == "DQ":
                    spread(name, dqv, 0, 32 ** -0.5, smp=dqv[:, L + 1:XT:2])
                elif name == "DK":
                    spread(name, dkv, smp=dkv[:, L + 1:XT:2])
                elif kind == "DV":
                    spread(name, dvv[:, i, :], smp=dvv[:, i, L + 1:XT:2])
                    if i == 1:
                        act.wait_ge(pj_free, t + 1)
                        act.wait_ge(kv0, 1)
                        act.dma_start(scr_dv.rearrange("(a p) t -> p a t", p=P), dvv).then_inc(s_dv, 16)
                elif kind == "DR":
                    copy(name, drv[:, i, :], HT, ACT.Silu)
                elif name == "DA":
                    b = ready(name)
                    act.wait_ge(s_qk, 16)
                    act.activation(fold(das, HT), ps[0:16, b:b + 2, 0:HT], ACT.Copy).then_inc(pj_free, 1)
                elif name == "LA":
                    act.activation(fold(dg[:, 0, :], HT), pair(name, HT), ACT.Identity, bias=vv(V_GB)).then_inc(pj_free, 1)
                    act.wait_ge(pj_free, t + 1)
                    link(act.activation(dg[:, 1, :], dg[:, 0, :], ACT.Abs))
                    link(act.activation(dg[:, 1, :], dg[:, 1, :], ACT.Exp, scale=-1.0))
                    act.activation(dg[:, 1, :], dg[:, 1, :], ACT.Ln, bias=cc(C_ONE)).then_inc(la_z, 1)
                s = t - UNIT0
                if 0 <= s < 16:
                    exps(s)
                if 1 <= s < 17:
                    wt_copy(s - 1)
            act.wait_ge(la_m, 1)
            for i in range(NV):
                act.activation(ea[:, i * XT:i * XT + L], dg[:, 0, 0:L], ACT.Exp, scale=1.0 / 16)
                act.activation(ea[:, i * XT + L + 1:(i + 1) * XT:2], dg[:, 0, L:T], ACT.Exp, scale=1.0 / 16).then_inc(la_e, 1)
            for t in range(2):
                act.wait_ge(at_o, 2 * NB * (t + 1))
                act.activation(brv[:, 2 + t, 0:SEQ], ps[:, 6 + t, :], ACT.Copy).then_inc(ob_ev, 1)
            act.wait_ge(st_mm, 1)
            act.activation(rst, ps[0:64, 7, 0:256].rearrange("p (h v) -> p h v", h=H), ACT.Copy).then_inc(st_ev, 1)
            act.wait_ge(ro_mm, 1)
            act.activation(brv[:, 2:4, SEQ:N], ps[:, 6, 0:2 * DEC].rearrange("p (t b) -> p t b", t=2), ACT.Copy)\
               .then_inc(b_raw, 1)
            for t in range(2):
                copy(f"BMEAN{t}", bsd[:, t, :], HN)
            for t in range(2):
                act.wait_ge(b_cen, t + 1)
                act.activation(bn[:, t, :], brv[:, 2 + t, :], ACT.Square).then_inc(b_sq, 1)
            for t in range(2):
                copy(f"BVAR{t}", bsd[:, t, :], HN, ACT.Sqrt, bias=eps)
            act.wait_ge(c_par, 1)
            for t in range(2):
                copy(f"CR{t}", rr[:, t, :], HT, ACT.Sigmoid, bias=vv(V_BA + t))
            for t in range(2):
                copy(f"CI{t}", ri[:, t, :], HT, ACT.Sigmoid, bias=vv(V_BX + t))
            act.wait_ge(pj_free, AT["CI1"] + 1)
            for t in range(2):
                act.activation(aa[:, t, :], rr[:, t, :], ACT.Exp, scale=sc[:, 20 + t:21 + t])
                act.activation(th[:, t, :], rr[:, t, :], ACT.Tanh, scale=sc[:, 20 + t:21 + t]).then_inc(c_act, 1)
            act.wait_ge(c_q, 1)
            act.activation(rr[:, :, :], th[:, :, :], ACT.Sqrt, scale=-1.0).then_inc(c_act, 1)

            def merge(n, m, i):
                if i >= 2:
                    act.wait_ge(mg_used, i - 1)
                if i == 0:
                    act.wait_ge(br_ok, 1)
                copy(f"G{n}{m}", sgtv[:, i % 2, :], HN, ACT.Sigmoid, bias=vv(V_BM + 8 * "ABCD".index(n) + m))
                copy(f"P{n}{m}", ptv[:, i % 2, :], HN)
                act.wait_ge(pj_free, AT[f"P{n}{m}"] + 1)
                act.sem_inc(mg, 1)

            for i in range(2 * KT):
                merge("BC"[i // KT], i % KT, i)
            act.wait_ge(rst_out, 16)
            act.wait_ge(la_e, NV)
            for m in range(KT):
                if m == 1:
                    act.wait_ge(s_sub, 1)
                    act.activation(S[:, :, :, :], S[:, :, :, :], ACT.Exp).then_inc(s_exp, 1)
                copy(f"GD{m}", sgv[:, m, :], HN, ACT.Sigmoid, bias=vv(V_BM + 24 + m))
            act.wait_ge(v_used, 2 * DEC)
            for t in range(2):
                for hh_ in range(2):
                    r = slice(64 * hh_, 64 * hh_ + 64)
                    ins = act.activation(brv[r, t, SEQ:N], ps[r, 4 + t, 256 + hh_:256 + 2 * DEC:2], ACT.Copy)
                ins.then_inc(a_raw, 1)
            for t in range(2):
                act.wait_ge(a_raw, 2)
                act.activation(osq[:, t, :], brv[:, t, :], ACT.Square).then_inc(a_osq, 1)
            for t in range(2):
                copy(f"AOS{t}", osd[:, t, :], HN, ACT.Sqrt, bias=eps)
            for m in range(KT):
                merge("A", m, 2 * KT + m)
            act.wait_ge(g_mm, GROUPS)
            for g in range(2):
                act.activation(brv[:, 6 + g, 0:SEQ], ps[:, 6 + g, :], ACT.Copy)
                act.activation(brv[:, 6 + g, SEQ:N], ps[:, 4, g * DEC:(g + 1) * DEC], ACT.Copy).then_inc(d_raw, 1)
            act.wait_ge(d_raw, 2)
            act.wait_ge(br_ok, 3)
            for g in range(2):
                act.activation(osq[:, g, :], brv[:, 6 + g, :], ACT.Square).then_inc(d_sq, 1)
            copy("DOS", osd[:, 0, :], HN, ACT.Sqrt, bias=eps, scale=0.5)
            for m in range(KT):
                i = 3 * KT + m
                act.wait_ge(mg_used, i - 1)
                copy(f"PD{m}", ptv[:, i % 2, :], HN)
                act.wait_ge(pj_free, AT[f"PD{m}"] + 1)
                act.sem_inc(mg, 1)
            for m in range(KT):
                act.wait_ge(wo_free, m + 1)
                act.activation(sq[:, m, :], hres[:, m, :], ACT.Square).then_inc(h_sq, 1)
            act.wait_ge(n2, 1)
            act.activation(fold(rstd, HN), ps[:, 0:2, 0:HN], ACT.Sqrt, bias=eps, scale=1.0 / DM).then_inc(n2_sd, 1)
            act.wait_ge(r1, 1)
            act.activation(rt[0:RB, 0, :, :], rt[0:RB, 0, :, :], ACT.Exp).then_inc(r2, 1)
            act.wait_ge(r1, 2)
            act.activation(rt[0:RB, 1, :, 0:1], rt[0:RB, 1, :, 0:1], ACT.Exp).then_inc(r2, 1)

            def silus(p):
                for ef in range(4):
                    act.wait_ge(e_h1, p * 4 + ef + 1)
                    act.activation(fold(si[:, ef % 2, :], HN), ps[:, 0:2, 0:HN], ACT.Silu).then_inc(e_s, 1)

            silus(0)
            act.wait_ge(g_t, 1)
            act.activation(gT[:, 0:4 * RB], ps[0:NE, 4, 0:4 * RB], ACT.Copy)
            act.activation(gT[:, 4 * RB:N], ps[0:NE, 5, 0:RB], ACT.Copy).then_inc(g_ev, 1)
            act.wait_ge(g_ev, 1)
            act.dma_start(scr_gate[:, :], gT).then_inc(s_gate, 16)
            with act.Fori(1, PAIRS) as p:
                silus(p)

        @block.vector
        def _(dve):
            link = Chain(dve, dch)
            tt, ts, stt = dve.tensor_tensor, dve.tensor_scalar, dve.scalar_tensor_tensor

            dve.wait_ge(ld_v, 16)
            lv = view(vec, V_LAM, 2, 2, 32)
            lp = view(sgt, 0, 2, 32)
            link(tt(lp, lv[:, :, 0, :], lv[:, :, 1, :], ALU.mult))
            dve.tensor_reduce(sc[:, 1:3], lp, X, ALU.add).then_inc(par, 1)
            dve.wait_ge(lam_e, 1)
            link(tt(sc[:, 5:6], sc[:, 3:4], sc[:, 4:5], ALU.subtract))
            link(ts(sc[:, 0:1], sc[:, 5:6], LAM0, None, ALU.add))
            link(ts(sc[:, 22:23], vv(V_AN), 1.0 - LAM0, None, ALU.mult))
            link(ts(sc[:, 23:24], vv(V_QN), 32 ** -0.5, None, ALU.mult))
            dve.wait_ge(lam_e, 2)
            e, z, z2, q = sc[:, 26:28], sc[:, 28:30], sc[:, 30:32], sc[:, 32:34]
            link(ts(z, e, 2.0, None, ALU.add))
            link(dve.reciprocal(z, z))
            link(tt(z, z, e, ALU.mult))
            link(tt(z2, z, z, ALU.mult))
            link(ts(q, z2, 1.0 / 17, None, ALU.mult))
            for k in range(15, 1, -2):
                link(stt(q, q, 1.0 / k, z2, ALU.add, ALU.mult))
            link(stt(q, q, 1.0, z, ALU.add, ALU.mult))
            link(ts(z, vv(V_LL, 2), 0.0, 8.0, ALU.min, ALU.mult))
            stt(sc[:, 20:22], q, -16.0, z, ALU.mult, ALU.add).then_inc(c_par, 1)

            dve.wait_ge(xsd, 1)
            link(dve.reciprocal(view(kv, 0, T), view(kv, 0, T)))
            for k in range(KT):
                ins = stt(xnv[:, k, :], xraw[:, k, :], vv(V_N1 + k), view(kv, 0, T), ALU.mult, ALU.mult)
            ins.then_inc(xn_ok, 1)
            for i in range(4):
                dve.wait_ge(pj_free, AT[f"AMS{i}"] + 1)
                link(dve.reciprocal(arr[:, i, :], arr[:, i, :]))
                stt(aqk[:, i, :], aqk[:, i, :], sc[:, 23:24] if i < 2 else vv(V_KN), arr[:, i, :], ALU.mult, ALU.mult)\
                   .then_inc(a_ok, 1)

            def causal_max(s):
                i = s % 4
                n = META + P * (i + 1)
                for m in range(2):
                    dve.wait_ge(sco, 2 * s + m + 1)
                    main, nb = ps[:, 4 + m, :], sc[:, 8 + 2 * (s % 2) + m:9 + 2 * (s % 2) + m]
                    k = min(n, 512)
                    last = ps[:, 7, 256 + META * m:256 + META * (m + 1)]
                    link(tt(main[:, n - 144:k], main[:, n - 144:k], cc(C_MASK, k - n + 144), ALU.add))
                    if i < 3:
                        dve.tensor_reduce(nb, main[:, 0:k], X, ALU.max, negate=True).then_inc(smx, 1)
                    else:
                        dve.wait_ge(sco, 2 * s + 2)
                        link(tt(last, last, cc(C_MASK + P, META), ALU.add))
                        dve.tensor_reduce(sc[:, 38:39], main, X, ALU.max, negate=True)
                        link(dve.tensor_reduce(sc[:, 39:40], last, X, ALU.max, negate=True))
                        tt(nb, sc[:, 38:39], sc[:, 39:40], ALU.min).then_inc(smx, 1)

            def combine(s):
                i = s % 4
                n = META + P * (i + 1)
                dve.wait_ge(sexp, 2 * s + 2)
                r = sc[:, 16:18]
                sums = sc[:, 12 + 2 * (s % 2):14 + 2 * (s % 2)]
                if i == 3:
                    link(tt(sums, sums, sc[:, 36:38], ALU.add))
                link(dve.reciprocal(r, sums))
                link(tt(r[:, 1:2], r[:, 1:2], sc[:, 0:1], ALU.mult))
                link(ts(prb[:, s % 2, 1, 0:n], prb[:, s % 2, 1, 0:n], r[:, 1:2], None, ALU.mult))
                stt(prb[:, s % 2, 0, 0:n], prb[:, s % 2, 0, 0:n], r[:, 0:1], prb[:, s % 2, 1, 0:n], ALU.mult, ALU.subtract)\
                   .then_inc(scomb, 1)

            def av_copy(s):
                h, i = s // 4, s % 4
                dve.wait_ge(sav, s + 1)
                r = slice(64 * (h % 2), 64 * (h % 2) + 64)
                dve.tensor_copy(brv[r, h // 2, P * i:P * (i + 1)], ps[r, 7, 384:512]).then_inc(sav_ev, 1)

            def rotate(i):
                dve.wait_ge(pj_free, AT[f"ROT{i}"] + 1)
                link(tt(rot[:, i % 2, :], rot[:, i % 2, :], cc(C_SIN, T), ALU.mult))
                link(tt(bqk[:, i, :], bqk[:, i, :], cc(C_COS, T), ALU.mult))
                tt(bqk[:, i, :], bqk[:, i, :], rot[:, i % 2, :], ALU.add).then_inc(rot_ok, 1)

            def conv(t):
                dve.wait_ge(pj_free, AT[f"CX{t}"] + 1)
                dve.wait_ge(c_st, 1)
                dve.wait_ge(kv0, 1)
                w = [vv(V_CW + 2 * k + t) for k in range(4)]
                link(ts(xc[:, t, 0:L], cxv[:, t, 0:L], w[0], vv(V_CB + t), ALU.mult, ALU.add))
                link(ts(xc[:, t, L:T], xxs[:, t, :, 0], w[0], vv(V_CB + t), ALU.mult, ALU.add))
                for k in range(1, 4):
                    link(stt(xc[:, t, 0:L], cxv[:, t, k:k + L], w[k], xc[:, t, 0:L], ALU.mult, ALU.add))
                    ins = stt(xc[:, t, L:T], xxs[:, t, :, k], w[k], xc[:, t, L:T], ALU.mult, ALU.add)
                    if k < 3:
                        link(ins)
                ins.then_inc(conv_ok, 1)

            for s in range(18):
                if s >= 2:
                    av_copy(s - 2)
                if s < 16:
                    causal_max(s)
                if 5 <= s < 9:
                    rotate(s - 5)
                if s in (10, 11):
                    conv(s - 10)
                if s < 16:
                    combine(s)
            dve.wait_ge(la_z, 1)
            stt(dg[:, 0, :], dg[:, 0, :], 0.0, dg[:, 1, :], ALU.min, ALU.subtract).then_inc(la_m, 1)
            for u in range(H * NB):
                h, j = u // NB, u % NB
                rows, t0 = min(P, L - j * P), max(META, j * P)
                dve.wait_ge(at_s, u + 1)
                if u >= 2:
                    dve.wait_ge(at_o, u - 1)
                d0 = C_DT + h * L + t0 - j * P
                tt(atb[0:rows, u % 2, 0:L - t0], ps[0:rows, 4 + u % 2, 0:L - t0], cst[0:rows, d0:d0 + L - t0], ALU.mult)\
                  .then_inc(at_w, 1)
            dve.wait_ge(kt_t, 1)
            for t in range(2):
                dec = view(cst, C_DEC, NB, H)[:, :, 2 * t:2 * t + 2]
                tt(kdv[:, 0:4, t * P:(t + 1) * P].rearrange("p b (h k) -> p b h k", h=2),
                   ps[:, 4 + t, :].rearrange("p (b h k) -> p b h k", b=4, h=2),
                   dec[:, 0:4, :].unsqueeze(3).to_broadcast([P, 4, 2, 64]), ALU.mult)
                ins = tt(kdv[0:TAIL, 4, t * P:(t + 1) * P].rearrange("p (h k) -> p h k", h=2),
                         ps[0:TAIL, 6, t * P:(t + 1) * P].rearrange("p (h k) -> p h k", h=2),
                         dec[0:TAIL, 4, :].unsqueeze(2).to_broadcast([TAIL, 2, 64]), ALU.mult)
            ins.then_inc(kd_ok, 1)
            dve.wait_ge(ld_rs, 16 * (1 + H))
            for t in range(2):
                kb = bqk[:, 2 + t, L:T].unsqueeze(2).to_broadcast([P, DEC, 64])
                link(tt(rv[:, t, :, :], rv[:, t, :, :], kb, ALU.mult))
                ins = stt(rs0[:, t, :, :], rs0[:, t, :, :], cc(C_GAM + t), rv[:, t, :, :], ALU.mult, ALU.add)
            ins.then_inc(rs_ok, 1)
            for t in range(2):
                dve.wait_ge(pj_free, AT[f"BMEAN{t}"] + 1)
                tt(brv[:, 2 + t, :], brv[:, 2 + t, :], bsd[:, t, :], ALU.subtract).then_inc(b_cen, 1)
            for t in range(2):
                dve.wait_ge(pj_free, AT[f"BVAR{t}"] + 1)
                link(dve.reciprocal(bsd[:, t, :], bsd[:, t, :]))
                link(stt(brv[:, 2 + t, :], brv[:, 2 + t, :], vv(V_RN), bsd[:, t, :], ALU.mult, ALU.mult))
                ins = tt(brv[:, 2 + t, :], brv[:, 2 + t, :], bgv[:, t, META:T], ALU.mult)
            ins.then_inc(br_ok, 1)
            dve.wait_ge(c_act, 2)
            link(tt(rr[:, :, :], aa[:, :, :], aa[:, :, :], ALU.mult))
            stt(th[:, :, :], rr[:, :, :], 1.0, th[:, :, :], ALU.add, ALU.mult).then_inc(c_q, 1)
            link(tt(ri[:, :, :], ri[:, :, :], xc[:, :, :], ALU.mult))
            dve.wait_ge(c_act, 3)
            link(tt(ri[:, :, :], ri[:, :, :], rr[:, :, :], ALU.mult))
            for t in range(2):
                dve.tensor_tensor_scan(th[:, t, 0:L], aa[:, t, 0:L], ri[:, t, 0:L], 0.0, ALU.mult, ALU.add)
            link(tt(th[:, :, L:T], aa[:, :, L:T], view(vec, V_ST + 48, 2, DEC), ALU.mult))
            link(tt(th[:, :, L:T], th[:, :, L:T], ri[:, :, L:T], ALU.add))
            tt(brv[:, 4:6, :], th[:, :, META:T], cgv[:, :, META:T], ALU.mult).then_inc(br_ok, 1)
            dve.tensor_copy(cst_out[:, :, 0:1 + DEC], th[:, :, L - 1:T])
            dve.tensor_copy(cst_out[:, :, 9:12], cxv[:, :, L:L + 3])
            dve.tensor_copy(cst_out[:, :, 12:36].rearrange("p t (b i) -> p t b i", b=DEC), xxs[:, :, :, 1:4]).then_inc(c_out, 1)

            dve.wait_ge(ld_q, 16)
            for j in range(2 * DEC):
                b, half = j // 2, j % 2
                ns = HALF + half
                dve.wait_ge(kv_ld[half], (128, 144)[half] * (b + 1))
                kb = kvb[half]
                link(tt(kb, kb, qbc[:, b:b + 1, :].to_broadcast([P, ns, 256]), ALU.mult))
                dve.tensor_reduce(S[:, b, half * HALF:half * HALF + ns, :], kb.rearrange("p s (m d) -> p s m d", d=32),
                                  X, ALU.add).then_inc(k_used, 1)
            dve.wait_ge(k_used, 2 * DEC)
            link(ts(S[:, :, PAGES, :], S[:, :, PAGES, :], cc(C_NEW), None, ALU.add))
            dve.tensor_reduce(mx.rearrange("p (b m) -> p b m", m=8), S.rearrange("p b s m -> p b m s"), X, ALU.max)\
               .then_inc(s_mx, 1)
            dve.wait_ge(s_mxt, 1)
            link(dve.tensor_reduce(mx1, ps[0:64, 4, 0:P], X, ALU.max))
            ts(mxb, cst[0:64, C_ONE:C_ONE + P], mx1, None, ALU.mult).then_inc(s_mx1, 1)
            dve.wait_ge(s_mxm, 1)
            link(dve.tensor_copy(Mb.rearrange("p b m -> p (b m)"), ps[:, 5, 0:64]))
            tt(S, S, Mb.unsqueeze(2).to_broadcast([P, DEC, SLOTS, 8]), ALU.subtract).then_inc(s_sub, 1)
            dve.wait_ge(s_exp, 1)
            dve.tensor_reduce(sm.rearrange("p (b m) -> p b m", m=8), S.rearrange("p b s m -> p b m s"), X, ALU.add)\
               .then_inc(s_sum, 1)
            dve.wait_ge(s_tot, 1)
            rc = Mb
            link(dve.reciprocal(rc.rearrange("p b m -> p (b m)"), ps[:, 5, 64:128]))
            odd = rc.rearrange("p b (h m) -> p (b h) m", m=2)[:, :, 1]
            link(ts(odd, odd, sc[:, 0:1], None, ALU.mult))
            link(tt(S, S, rc.unsqueeze(2).to_broadcast([P, DEC, SLOTS, 8]), ALU.mult))
            Sp = S.rearrange("p b s (h m) -> p (b s h) m", m=2)
            tt(W.rearrange("p b s h -> p (b s h)"), Sp[:, :, 0], Sp[:, :, 1], ALU.subtract).then_inc(s_w, 1)

            qx = dqv[:, META:XT].unsqueeze(1).to_broadcast([P, NV, L])
            kx = dkv.unsqueeze(1).to_broadcast([P, NV, XT])
            dve.wait_ge(ea_ok, 1)

            def gla(j):
                v = vb[:, j % 2, :, :]
                dve.wait_ge(vb_s0, j + 1)
                link(tt(v, v, kx, ALU.mult))
                vf = v.rearrange("p a t -> p (a t)")
                link(dve.tensor_tensor_scan(vf, ea[:, :], vf, 0.0, ALU.mult, ALU.add))
                dve.sem_inc(g_scan, 1)
                if j >= 2:
                    dve.wait_ge(g_mm, j - 1)
                tt(pbv[:, j % 2, :, :], v[:, :, META:XT], qx, ALU.mult).then_inc(g_p, 1)

            def a_norm():
                for t in range(2):
                    dve.wait_ge(pj_free, AT[f"AOS{t}"] + 1)
                    link(dve.reciprocal(osd[:, t, :], osd[:, t, :]))
                    ins = stt(brv[:, t, :], brv[:, t, :], sc[:, 22:23], osd[:, t, :], ALU.mult, ALU.mult)
                ins.then_inc(br_ok, 1)

            for j in range(GROUPS):
                if j == 2:
                    a_norm()
                gla(j)
            dve.wait_ge(pj_free, AT["DOS"] + 1)
            link(dve.reciprocal(osd[:, 0, :], osd[:, 0, :]))
            for g in range(2):
                link(stt(brv[:, 6 + g, :], brv[:, 6 + g, :], vv(V_GN + g), osd[:, 0, :], ALU.mult, ALU.mult))
                ins = tt(brv[:, 6 + g, :], brv[:, 6 + g, :], drv[:, g, META:T], ALU.mult)
            ins.then_inc(br_ok, 1)

            dve.wait_ge(ld_x2, 16)
            for m in range(KT):
                dve.wait_ge(wo, m + 1)
                b = 2 * (m % 4)
                tt(fold(hres[:, m, :], HN), fold(hres[:, m, :], HN), ps[:, b:b + 2, 0:HN], ALU.add).then_inc(wo_free, 1)
            dve.wait_ge(n2_sd, 1)
            link(dve.reciprocal(rstd, rstd))
            for m in range(KT):
                stt(tT[:, m, :], hres[:, m, :], vv(V_N2 + m), rstd, ALU.mult, ALU.mult).then_inc(t_ok, 1)

            dve.wait_ge(lgm, 1)
            R = slice(0, RB)
            l_ = lg[R, :, :]
            link(tt(l_, ps[R, 6, 0:NB * 32].rearrange("p (b n) -> p b n", b=NB)[:, :, 0:20],
                    vec[R, V_RB:V_RB + 20].unsqueeze(1).to_broadcast([RB, NB, 20]), ALU.add))
            r = [rt[R, i, :, :] for i in range(20)]
            one = [rt[R, i, :, 0:1] for i in range(20)]

            def first_of(oh, eq, c):
                link(dve.tensor_copy(oh[:, :, 0:1], eq[:, :, 0:1]))
                link(dve.tensor_copy(c, eq[:, :, 0:1]))
                for i in range(1, 4):
                    link(tt(oh[:, :, i:i + 1], eq[:, :, i:i + 1], c, ALU.is_gt))
                    link(tt(c, c, eq[:, :, i:i + 1], ALU.max))

            gl, le = l_[:, :, 0:4], l_[:, :, 4:20].rearrange("p b (g e) -> p b g e", g=4)
            link(dve.tensor_reduce(one[2], gl, X, ALU.max))
            tt(r[0], gl, one[2].to_broadcast([RB, NB, 4]), ALU.subtract).then_inc(r1, 1)
            link(tt(r[3], gl, one[2].to_broadcast([RB, NB, 4]), ALU.is_equal))
            first_of(r[4], r[3], one[5])
            dve.wait_ge(r2, 1)
            link(dve.tensor_reduce(one[6], r[0], X, ALU.add))
            link(dve.reciprocal(one[6], one[6]))
            ge = gate[R, :, :].rearrange("p b (g e) -> p b g e", g=4)
            for b in range(NB):
                ins = tt(ge[:, b, :, :], le[:, b, :, :], r[4][:, b, :].unsqueeze(2).to_broadcast([RB, 4, 4]), ALU.mult)
            link(ins)
            link(dve.tensor_reduce(r[7], ge.rearrange("p b g e -> p b e g"), X, ALU.add))
            link(dve.tensor_reduce(one[8], r[7], X, ALU.max))
            link(tt(r[9], r[7], one[8].to_broadcast([RB, NB, 4]), ALU.is_equal))
            first_of(r[10], r[9], one[5])
            link(stt(r[11], r[10], NEG, r[7], ALU.mult, ALU.add))
            link(dve.tensor_reduce(one[12], r[11], X, ALU.max))
            tt(one[1], one[12], one[8], ALU.subtract).then_inc(r1, 1)
            link(tt(r[13], r[11], one[12].to_broadcast([RB, NB, 4]), ALU.is_equal))
            first_of(r[14], r[13], one[5])
            dve.wait_ge(r2, 2)
            link(ts(one[15], one[1], 1.0, None, ALU.add))
            link(dve.reciprocal(one[15], one[15]))
            link(tt(one[15], one[15], one[6], ALU.mult))
            link(tt(one[16], one[15], one[1], ALU.mult))
            link(tt(r[17], r[10], one[15].to_broadcast([RB, NB, 4]), ALU.mult))
            link(tt(r[18], r[14], one[16].to_broadcast([RB, NB, 4]), ALU.mult))
            link(tt(r[17], r[17], r[18], ALU.add))
            for b in range(NB):
                ins = tt(ge[:, b, :, :], r[17][:, b, :].unsqueeze(1).to_broadcast([RB, 4, 4]),
                         r[4][:, b, :].unsqueeze(2).to_broadcast([RB, 4, 4]), ALU.mult)
            ins.then_inc(g_ok, 1)

            with dve.Fori(0, PAIRS) as p:
                for ef in range(4):
                    dve.wait_ge(e_s, p * 4 + ef + 1)
                    dve.wait_ge(e_h3, p * 4 + ef + 1)
                    tt(fold(hh[:, ef, :], HN), fold(si[:, ef % 2, :], HN), ps[:, 2:4, 0:HN], ALU.mult).then_inc(e_t, 1)
                    if ef == 3:
                        dve.wait_ge(gb_ld, p * 16 + 16)
                        for f in range(4):
                            dve.wait_ge(e_t, p * 4 + f + 1)
                            tt(hh[:, f, :], hh[:, f, :], gbc[:, f // 2, :], ALU.mult).then_inc(e_h, 1)
                for m in range(KT):
                    dve.wait_ge(e_y, p * KT + m + 1)
                    b = 4 + 2 * (m % 2)
                    if m == 0:
                        dve.wait_ge(wo_free, KT)
                    tt(fold(hres[:, m, :], HN), fold(hres[:, m, :], HN), ps[:, b:b + 2, 0:HN], ALU.add).then_inc(e_acc, 1)

        @block.gpsimd
        def _(pool):
            link = Chain(pool, pch)
            pool.memset(cxv[:, :, 0:3], 0.0)
            pool.memset(dqv[:, L:XT:2], 0.0)
            pool.memset(dkv[:, L:XT:2], 1.0)
            pool.memset(dvv[:, :, L:XT:2], 0.0)
            for i in range(NV):
                pool.memset(ea[:, i * XT + L:(i + 1) * XT:2], 0.0)
            pool.memset(kvb[1][:, HALF, :], 0.0).then_inc(kv0, 1)
            pool.wait_ge(a_ok, 4)
            pool.dma_start(o["k"], aqk[:, 2:4, :]).then_inc(k_out, 16)
            pool.wait_ge(s_v, 16)
            pool.dma_start(o["v"][0:4 * P, :].rearrange("(b p) c -> p b c", p=P), vt[:, 0:4, 0:256]).then_inc(outs, 16)
            pool.dma_start(o["v"][4 * P:T, :], vt[0:T - 4 * P, 4, 0:256]).then_inc(outs, 16)
            pool.wait_ge(la_e, NV)
            for i in range(NV):
                ins = pool.memset(ea[:, i * XT:i * XT + 1], 0.0)
            ins.then_inc(ea_ok, 1)
            pool.wait_ge(st_ev, 1)
            pool.dma_start(o["ret_p"], rst).then_inc(rst_out, 16)
            pool.wait_ge(rs_ok, 1)
            pool.dma_start(o["ret_s"], rs0).then_inc(rs_out, 16)
            pool.wait_ge(c_out, 1)
            pool.dma_start(o["c"], cst_out).then_inc(outs, 16)

            def merge(i, n, m):
                pool.wait_ge(mg, i + 1)
                p_ = ptv[:, i % 2, :]
                g = sgv[:, m, :] if n == "D" else sgtv[:, i % 2, :]
                if i < KT:
                    pool.tensor_tensor(acc[:, m, :], g, p_, ALU.mult).then_inc(mg_used, 1)
                else:
                    link(pool.tensor_tensor(p_, g, p_, ALU.mult))
                    pool.tensor_tensor(acc[:, m, :], acc[:, m, :], p_, ALU.add).then_inc(mg_used, 1)

            pool.wait_ge(k_out, 16)
            pool.wait_ge(ro_mm, 1)
            for i in range(2 * KT):
                merge(i, "BC"[i // KT], i % KT)
            pool.wait_ge(ld_g0, 16)

            def fill(j):
                pool.wait_ge(vb_ld[j % 2], 64 * (j // 2 + 1))
                pool.tensor_copy(vb[:, j % 2, :, L:XT:2], view(g0, 0, 64, DEC)[:, j * NV:(j + 1) * NV, :]).then_inc(vb_s0, 1)

            def states(j):
                pool.wait_ge(g_scan, j + 1)
                pool.tensor_copy(gst[:, :, j * NV:(j + 1) * NV].rearrange("p n v -> p v n"), vb[:, j % 2, :, L - 1:XT:2])\
                    .then_inc(g_st, 1)

            fill(0)
            fill(1)
            for m in range(KT):
                for q in range(4):
                    j = 4 * m + q
                    states(j)
                    if j + 2 < GROUPS:
                        fill(j + 2)
                    if q == 2:
                        merge(2 * KT + m, "A", m)
            pool.wait_ge(g_st, GROUPS)
            pool.dma_start(o["gla"], gst).then_inc(outs, 16)
            for m in range(KT):
                merge(3 * KT + m, "D", m)
            for stored, n in ((k_out, 1), (rst_out, 1), (rs_out, 1), (outs, POOL_OUTS)):
                pool.wait_ge(stored, 16 * n)



def constants():
    import numpy as np
    c = np.zeros((P, C_W), np.float32)
    p = np.arange(P)
    c[:, C_ID:C_ID + P] = np.eye(P)
    c[p, C_PERM + (p ^ 32)] = 1.0
    c[:, C_B32:C_B32 + P] = (p[:, None] // 32 == p[None] // 32) / 32.0
    c[:, C_B64:C_B64 + P] = (p[:, None] // 64 == p[None] // 64) / 64.0
    c[:, C_ONE:C_ONE + P] = 1.0
    c[p, C_SEL + 31 + 32 * (p // 32)] = 1.0
    inv = (np.float32(10000.0) ** (-np.linspace(0.0, 1.0, 32, dtype=np.float32))).astype(np.float32)
    pos = np.concatenate([np.arange(L), np.full(DEC, PAST)]).astype(np.float32)
    ang = (pos[None, :] * inv[p % 32][:, None]).astype(np.float32)
    c[:, C_COS:C_COS + T] = np.cos(ang)
    c[:, C_SIN:C_SIN + T] = np.where(p[:, None] % 64 < 32, -np.sin(ang), np.sin(ang))
    lgam = np.log(1.0 - 2.0 ** (-5.0 - np.arange(H)))
    x = np.arange(L)
    for h in range(H):
        rel = x[None, :] - p[:, None]
        c[:, C_DT + h * L:C_DT + (h + 1) * L] = np.where(rel >= 0, np.exp(np.maximum(rel, 0) * lgam[h]), 0.0)
    q = np.arange(144)
    c[:, C_MASK:C_MASK + 144] = np.where(q[None, :] <= p[:, None] + META, 0.0, NEG)
    for b in range(NB):
        for h in range(H):
            at = np.minimum(b * P + p, L - 1)
            c[:, C_DEC + b * H + h] = np.exp((L - 1 - at) * lgam[h])
    for t in range(2):
        c[:, C_GAM + t] = np.exp(lgam[2 * t + p // 64])
    c[1:, C_NEW] = NEG
    c[:, C_EPS] = EPS
    return c


_OUT = {"y": (P, KT, N), "k": (P, 2, T), "v": (T, 256), "ret_p": (64, H, 64), "ret_s": (P, 2, DEC, 64),
        "c": (P, 2, 36), "gla": (P, 1 + DEC, 64)}


def kernel(**inputs):
    import numpy as np
    import concourse.bacc as bacc
    from concourse.bass_utils import run_bass_kernel_spmd as run

    a = {k: np.asarray(v) for k, v in inputs.items()}

    def cols(v):
        return np.ascontiguousarray(v.reshape(-1, P).T)

    def tiles(w):
        return w.reshape(KT, P, -1).transpose(1, 0, 2)

    w = a["w_in"][0]
    cut = np.cumsum([0, 256, 256, 256, 256, 256, 256, 256, 256, 256, 128, 128, 256, 256, 16])
    aq, ak, av, bq, bk, bv, bg_, cx_, cg_, dq, dk, dv_, dr_, da = [w[:, i:j] for i, j in zip(cut[:-1], cut[1:])]
    dr_ = dr_.reshape(DM, H, 2, 32).transpose(0, 2, 1, 3).reshape(DM, 256)
    w_in = np.concatenate([aq, ak, av, bv, bq, bk, bg_, cx_, cg_, dq, dk, dv_, dr_], 1)
    w_in = w_in.reshape(KT, P, N_IN, P).transpose(2, 1, 0, 3).reshape(N_IN, P, 1024)
    wb = a["w_branch"][0].copy()
    wb = np.stack([wb[0], wb[1], wb[2], wb[3].reshape(H, 2, 32, DM).transpose(1, 0, 2, 3).reshape(256, DM)])
    wm = a["w_merge"][0].reshape(KT, P, 4, KT, P).transpose(2, 3, 1, 0, 4)
    wbt = wb.reshape(4, 2, P, KT, P).transpose(0, 3, 2, 1, 4)
    both = np.concatenate([wm.reshape(4, KT, P, 1024), wbt.reshape(4, KT, P, 256)], 3)
    w_mg = np.concatenate([both["ABCD".index(n)] for n in "BCDA"])
    w_dp = wbt[3].reshape(2, 4, P, 256).transpose(0, 2, 1, 3).reshape(2, P, 1024)
    w_out = a["w_out"][0].reshape(KT, P, KT, P).transpose(2, 1, 0, 3).reshape(KT, P, 1024)
    w1 = a["ex_w1"][0].reshape(NE, KT, P, 2, P).transpose(0, 3, 2, 1, 4).reshape(NE, 2, P, 1024)
    w3 = a["ex_w3"][0].reshape(NE, KT, P, 2, P).transpose(0, 3, 2, 1, 4).reshape(NE, 2, P, 1024)
    w13 = np.stack([w1, w3], 2).reshape(PAIRS, 8, P, 1024)
    w2 = a["ex_w2"][0].reshape(PAIRS, 4, P, 4, 2, P).transpose(0, 3, 2, 4, 1, 5).reshape(PAIRS, 4, P, 1024)
    w_ex = np.concatenate([w13, w2], 1)

    x = np.concatenate([a["meta"], a["x_prompt"][0], a["x_sample"][:, 0]], 0)
    xT = x.T.reshape(KT, P, T).transpose(1, 0, 2)

    v = np.zeros((P, V_W), np.float32)
    v[:, V_N1:V_N1 + 8], v[:, V_N2:V_N2 + 8] = cols(a["norm1"][0]), cols(a["norm2"][0])
    v[:, V_QN], v[:, V_KN] = np.tile(a["qn"][0], 4), np.tile(a["kn"][0], 4)
    v[:, V_AN], v[:, V_RN] = np.tile(a["an"][0], 2), np.tile(a["rn"][0], 2)
    v[:, V_GN], v[:, V_GN + 1] = np.tile(a["gn"][0][:32], 4), np.tile(a["gn"][0][32:], 4)
    for k in range(4):
        v[:, V_CW + 2 * k:V_CW + 2 * k + 2] = cols(a["conv_w"][0, k])
    for at, name in ((V_CB, "conv_b"), (V_BA, "lru_ba"), (V_BX, "lru_bx"), (V_LL, "lru_lam")):
        v[:, at:at + 2] = cols(a[name][0])
    v[:, V_GB] = a["gla_b"][0]
    v[:, V_BM:V_BM + 32] = cols(a["b_merge"][0])
    v[:, V_RB:V_RB + 4], v[:, V_RB + 4:V_RB + 20] = a["rg_b"][0], a["re_b"][0]
    v[:, V_LAM:V_LAM + 128] = a["lam"][0].reshape(-1)
    v[:, V_ST:V_ST + 48] = a["state_lru_conv"][0].transpose(2, 0, 1).reshape(2, P, 24).transpose(1, 0, 2).reshape(P, 48)
    v[:, V_ST + 48:V_ST + 64] = a["state_lru_h"][0].T.reshape(2, P, DEC).transpose(1, 0, 2).reshape(P, 16)
    for at, name in ((V_WA, "lru_wa"), (V_WX, "lru_wx")):
        for h in range(H):
            r = 64 * (h % 2)
            v[r:r + 64, at + P * (h // 2) + r:at + P * (h // 2) + r + 64] = a[name][0, h]
    v[:, V_RW:V_RW + 160] = tiles(np.concatenate([a["rg_w"][0], a["re_w"][0]], 1)).reshape(P, 160)
    v[:, V_DA:V_DA + 128] = tiles(da).reshape(P, 128)
    v[0:16, V_G2:V_G2 + 128] = a["gla_w2"][0]

    ret0 = a["state_ret"][0].reshape(DEC, 2, P, 64).transpose(2, 1, 0, 3)
    gla0 = a["state_gla"][0].reshape(DEC, P, 64).transpose(1, 2, 0).reshape(P, 512)
    kcache = a["cache_k_a"][0].reshape(-1, PAGE, 256)
    vcache = a["cache_v_a"][0].reshape(-1, PAGE, 256)
    pt = a["page_table"].reshape(1, -1)

    nc = bacc.Bacc("TRN2", target_bir_lowering=False, num_devices=1)
    arrays, args = {}, []
    for name, arr in (("w_in", w_in), ("w_mg", w_mg), ("w_dp", w_dp), ("w_out", w_out), ("w_ex", w_ex), ("xT", xT),
                      ("const", constants()), ("vec", v), ("ret0", ret0), ("gla0", gla0), ("kc", kcache),
                      ("vc", vcache), ("pt", pt)):
        arr = np.ascontiguousarray(arr)
        arrays["in_" + name] = arr
        args.append(nc.dram_tensor("in_" + name, arr.shape, mybir.dt.from_np(arr.dtype), kind="ExternalInput").ap())
    o = {k: nc.dram_tensor("out_" + k, s, F32, kind="ExternalOutput").ap() for k, s in _OUT.items()}
    program(nc, *args, o)
    res = run(nc, [arrays], core_ids=[0]).results[0]
    r = {k: np.asarray(res["out_" + k]).reshape(s) for k, s in _OUT.items()}

    y = r["y"].transpose(2, 1, 0).reshape(N, DM)
    k = r["k"].transpose(2, 1, 0).reshape(T, H, 64)
    vv_ = r["v"].reshape(T, H, 64)
    c = r["c"].transpose(1, 0, 2).reshape(256, 36)
    g = r["gla"]
    rs = r["ret_s"].reshape(2, 64, 2, DEC, 64).transpose(3, 2, 0, 1, 4).reshape(DEC, H, 64, 64)
    outs = (y[:SEQ][None], y[SEQ:][:, None], k[:L][None, None], vv_[:L][None, None],
            r["ret_p"].transpose(1, 0, 2)[None, None], c[:, 0][None, None], c[:, 9:12].T[None, None],
            g[:, 0].reshape(H, 32, 64)[None, None],
            k[L:][None, :, None], vv_[L:][None, :, None], rs[None], c[:, 1:9].T[None],
            c[:, 12:36].reshape(256, DEC, 3).transpose(1, 2, 0)[None],
            g[:, 1:].transpose(1, 0, 2).reshape(DEC, H, 32, 64)[None])
    return tuple(np.ascontiguousarray(t) for t in outs)
```

```python
from contextlib import ExitStack

import concourse.bass as bass
from concourse import mybir

F32 = mybir.dt.float32
I32 = mybir.dt.int32
ALU = mybir.AluOpType
ACT = mybir.ActivationFunctionType
X = mybir.AxisListType.X

P = 128
DM = 1024
KT = DM // P
META, SEQ, DEC = 16, 512, 8
L = META + SEQ
T = L + DEC
HT = T // 2
N = SEQ + DEC
HN = N // 2
NB = 5
TAIL = L - 4 * P
H = 4
PAST, PAGE = 2048, 128
PAGES = PAST // PAGE
HALF = PAGES // 2
SLOTS = PAGES + 1
XT = L + 2 * DEC
NV = 2
GROUPS = 64 // NV
NE = 16
PAIRS = NE // 2
DEEP = 4
OVER = 8
ROWS = (NE + OVER) * P
RB = N // NB
WCH = 1280
RING = 6
EPS = 1e-6
LAM0 = 0.8 - 0.6
NEG = -1.0e30

C_ID, C_PERM, C_B32, C_B64, C_ONE = 0, 128, 256, 384, 512
C_SEL = 640
C_COS = C_SEL + 159
C_SIN = C_COS + T
C_DT = C_SIN + T
C_MASK = C_DT + H * L
C_DEC = C_MASK + 144
C_GAM = C_DEC + NB * H
C_NEW = C_GAM + 2
C_EPS = C_NEW + 1
C_LT = C_EPS + 1
C_IO = C_LT + P
C_W = C_IO + 16

V_N1, V_N2, V_QN, V_KN, V_AN, V_RN, V_GN = 0, 8, 16, 17, 18, 19, 20
V_CW, V_CB, V_BA, V_BX, V_LL, V_GB, V_BM, V_RB = 22, 30, 32, 34, 36, 38, 39, 71
V_LAM, V_ST = 91, 219
V_WA = V_ST + 64
V_WX = V_WA + 256
V_RW = V_WX + 256
V_DA = V_RW + 160
V_G2 = V_DA + 128
V_W = V_G2 + 128

PROJ = (["AQ0", "AQ1", "AK0", "AK1", "V0", "V1", "V2", "V3", "AMS0", "AMS1", "AMS2", "AMS3",
         "BQ0", "BQ1", "BK0", "BK1", "BG0", "BG1", "ROT0", "ROT1", "ROT2", "ROT3",
         "CX0", "CX1", "CG0", "CG1", "DQ", "DK", "DV0", "DV1", "DR0", "DR1", "DA", "LA"]
        + ["BMEAN0", "BMEAN1", "BVAR0", "BVAR1", "CR0", "CR1", "CI0", "CI1"]
        + [f"{k}{n}{m}" for n in "BC" for m in range(KT) for k in "GP"]
        + [f"GD{m}" for m in range(KT)] + ["AOS0", "AOS1"]
        + [f"{k}A{m}" for m in range(KT) for k in "GP"]
        + ["DOS"] + [f"PD{m}" for m in range(KT)])
AT = {name: i for i, name in enumerate(PROJ)}
UNIT0 = AT["BK0"]
CHUNKS = ["AQ0", "AQ1", "AK0", "AK1", "V0", "V1", "V2", "V3", "BQ0", "BQ1", "BK0", "BK1",
          "BG0", "BG1", "CX0", "CX1", "CG0", "CG1", "DQ", "DK", "DV0", "DV1", "DR0", "DR1"]
N_IN = len(CHUNKS)
MERGES = [f"G{n}{m}" for n in "BC" for m in range(KT)] + [f"GD{m}" for m in range(KT)] + [f"GA{m}" for m in range(KT)]
BR = {"A": 0, "B": 2, "C": 4, "D": 6}
CH = CHUNKS + MERGES + ["DP0", "DP1"] + [f"WO{m}" for m in range(KT)]
CAT = {name: i for i, name in enumerate(CH)}


def program(nc, w_in, w_mg, w_dp, w_out, w_13, w_2, x_d, n2_d, xT_d, const_d, vec_d, ret0_d, gla0_d, kc, vc, pt, o):
    with ExitStack() as ctx:
        def sb(name, cols, dt=F32):
            return ctx.enter_context(nc.sbuf_tensor(name, [P, cols], dt))

        def sem(name):
            return ctx.enter_context(nc.semaphore(name))

        def scratch(name, shape):
            return nc.dram_tensor(name, shape, F32, kind="Internal").ap()

        scr_qk = scratch("scr_qk", (DEC, 512))
        scr_v = scratch("scr_v", (DEC, 512))
        scr_dv = scratch("scr_dv", (256, XT))
        scr_x = scratch("scr_x", (ROWS, DM))
        scr_y = scratch("scr_y", (ROWS, DM))

        cst = sb("cst", C_W)
        vec = sb("vec", V_W)
        xn = sb("xn", KT * T)
        ring = sb("ring", RING * WCH)
        sgd = sb("sgd", KT * N)
        qk = sb("qk", 8 * T)
        bg, cg, dr = sb("bg", 2 * T), sb("cg", 2 * T), sb("dr", 2 * T)
        cx = sb("cx", 2 * (L + 3))
        dqk = sb("dqk", 2 * XT)
        dv = sb("dv", 2 * XT)
        ea = sb("ea", NV * XT)
        vtok = sb("vtok", NB * 512)
        br = sb("br", 8 * N)
        kv = sb("kv", SLOTS * 256)
        tmp = sb("tmp", 4288)
        qb = sb("qb", 2144)
        sgt = sb("sgt", 2 * N)
        g0 = sb("g0", 512)
        small = sb("small", 200)
        pts = ctx.enter_context(nc.sbuf_tensor("pts", [1, DEC * PAGES], I32))
        itab = ctx.enter_context(nc.sbuf_tensor("itab", [P, 10 + OVER + 1], I32))
        ps = ctx.enter_context(nc.psum_tensor("ps", [P, 8, 512], F32))

        def cc(at, n=1, rows=slice(0, P)):
            return cst[rows, at:at + n]

        def vv(at, n=1, rows=slice(0, P)):
            return vec[rows, at:at + n]

        def view(t, off, *dims):
            n = 1
            for d in dims:
                n *= d
            a = t[:, off:off + n]
            if len(dims) == 1:
                return a
            names = "abcd"[:len(dims)]
            return a.rearrange(f"p ({' '.join(names)}) -> p {' '.join(names)}", **dict(zip(names[1:], dims[1:])))

        ident = cc(C_ID, P)
        xnv, xraw = view(xn, 0, KT, T), view(tmp, 0, KT, T)
        tT = view(xn, 0, KT, N)
        aqk, bqk = view(qk, 0, 4, T), view(qk, 4 * T, 4, T)
        acc = view(qk, 0, KT, N)
        bgv, cgv, drv = view(bg, 0, 2, T), view(cg, 0, 2, T), view(dr, 0, 2, T)
        cxv = view(cx, 0, 2, L + 3)
        dqv, dkv = dqk[:, 0:XT], dqk[:, XT:2 * XT]
        dvv = view(dv, 0, 2, XT)
        gst = view(dv, 0, 1 + DEC, 64)
        vt = view(vtok, 0, NB, 512)
        brv = view(br, 0, 8, N)
        sgv, sgtv = view(sgd, 0, KT, N), view(sgt, 0, 2, N)
        ptv = view(cst, C_COS, 2, N)
        kvv = view(kv, 0, SLOTS, 256)
        kvb = [kvv[:, 0:HALF, :], kvv[:, HALF:SLOTS, :]]
        asq, arr = view(tmp, 0, 4, T), view(tmp, 4 * T, 4, T)
        prb = view(tmp, 0, 2, 2, L)
        wtb = view(tmp, 4 * L, 2, NB, P)
        rot = view(qb, 0, 2, T)
        xc = view(qb, 2 * T, 2, T)
        atb = view(tmp, 0, 2, 512)
        kdv = view(tmp, 1024, NB, 256)
        rv = view(tmp, 2304, 2, DEC, 64)
        rs0 = view(qb, 0, 2, DEC, 64)
        rst = sgd[0:64, 2000:2256].rearrange("p (h v) -> p h v", h=H)
        bn, bsd = view(tmp, 0, 2, N), view(sgt, 0, 2, N)
        osq, osd = view(kv, 0, 2, N), view(kv, 2 * N, 2, N)
        rr, ri = view(tmp, 0, 2, T), view(tmp, 2 * T, 2, T)
        aa, th = view(tmp, 4 * T, 2, T), view(tmp, 6 * T, 2, T)
        xxs = view(small, 0, 2, DEC, 4)
        cst_out = view(small, 64, 2, 36)
        sc = small[:, 136:200]
        S = view(cst, C_DT, DEC, SLOTS, 8)
        W = view(cst, C_DT + 1088, DEC, SLOTS, 4)
        mx, sm = view(cst, C_DT + 1632, 64), view(cst, C_DT + 1696, 64)
        mxb, mx1 = cst[0:64, C_DT + 1760:C_DT + 1888], cst[0:64, C_DT + 1888:C_DT + 1889]
        Mb = view(cst, C_DT + 1900, DEC, 8)
        qbc = view(qb, 0, DEC, 256)
        qk8 = sgt[0:DEC, 0:512]
        vb = view(tmp, 0, 2, NV, XT)
        pbv = view(tmp, 2 * NV * XT, 2, NV, L)
        dg = view(sgd, 0, 2, T)
        das = sgt[0:16, 0:T]
        hres = [view(tmp, b * DM, DM)[0:RB] for b in range(4)] + [bg[0:RB, 0:DM]]
        tk = [view(xn, b * DM, DM)[0:RB] for b in range(4)] + [cg[0:RB, 0:DM]]
        tT = view(qk, 0, KT, N)
        n2row = dqk[0:RB, 0:DM]
        lg = view(ea, 0, NB, 20)
        rt = view(ea, 100, 20, NB, 4)
        f1, f2, sel, pos = [view(dr, 80 * i, NB, 4, 4) for i in range(4)]
        tot = view(dr, 320, NB, NE)
        ecnt, eov, eend, edel = [view(dr, 400 + 16 * i, NE) for i in range(4)]
        ecmp = view(dr, 464, OVER, NE)
        pos_f, tab_f = view(dr, 600, 10), view(dr, 610, OVER + 1)
        w13b = [view(t, 0, KT, 512) for t in (kv, br, qk, xn)]
        w2b = [view(sgd, 0, 2, DM), view(sgd, 2 * DM, 2, DM), view(qb, 0, 2, DM), view(vtok, 0, 2, DM)]
        xe = [view(ring, DM * i, DM) for i in range(2)]
        xeT = [view(ring, 2 * DM + DM * i, KT, P) for i in range(2)]
        yb = [view(ring, 4 * DM + DM * i, 2, 512) for i in range(2)]
        si = [view(ring, 6 * DM + 256 * i, 256) for i in range(2)]
        hm = [view(ring, 6 * DM + 512 + 256 * i, 256) for i in range(2)]
        hT = [view(cx, 256 * i, 2, P) for i in range(2)]
        y1 = [view(kv, b * DM, DM)[0:RB] for b in range(4)] + [view(xn, 0, DM)[0:RB]]
        y2 = [view(br, b * DM, DM)[0:RB] for b in range(4)] + [view(xn, DM, DM)[0:RB]]

        w_ld = [sem(f"w_ld{i}") for i in range(RING)]
        ld_x, ld_c, ld_v, ld_pt, ld_g0 = sem("ld_x"), sem("ld_c"), sem("ld_v"), sem("ld_pt"), sem("ld_g0")
        ld_rs, ld_q = sem("ld_rs"), sem("ld_q")
        x_sq = sem("x_sq")
        xms, xsd, xn_ok = sem("xms"), sem("xsd"), sem("xn_ok")
        pj, pj_free = sem("pj"), sem("pj_free")
        a_sq, a_ok = sem("a_sq"), sem("a_ok")
        t8, t8_ev, s_qk, s_v = sem("t8"), sem("t8_ev"), sem("s_qk"), sem("s_v")
        sco, smx, sexp, scomb = sem("sco"), sem("smx"), sem("sexp"), sem("scomb")
        swt, swt_ev, sav, sav_ev = sem("swt"), sem("swt_ev"), sem("sav"), sem("sav_ev")
        rot_ok, conv_ok = sem("rot_ok"), sem("conv_ok")
        at_s, at_w, at_o, ob_ev = sem("at_s"), sem("at_w"), sem("at_o"), sem("ob_ev")
        kt_t, kd_ok, st_mm, st_ev = sem("kt_t"), sem("kd_ok"), sem("st_mm"), sem("st_ev")
        rs_ok, ro_mm, b_raw = sem("rs_ok"), sem("ro_mm"), sem("b_raw")
        b_cen, b_sq, br_ok = sem("b_cen"), sem("b_sq"), sem("br_ok")
        c_par, c_act, c_q, c_out = sem("c_par"), sem("c_act"), sem("c_q"), sem("c_out")
        mg, mg_used = sem("mg"), sem("mg_used")
        kv_ld = [sem("kv_ld0"), sem("kv_ld1")]
        k_used, v_used = sem("k_used"), sem("v_used")
        s_mx, s_mxt, s_mx1, s_mxm, s_sub, s_exp, s_sum, s_tot, s_w = [sem(f"smp{i}") for i in range(9)]
        a_raw, a_osq = sem("a_raw"), sem("a_osq")
        la_z, la_e, la_m, s_dv = sem("la_z"), sem("la_e"), sem("la_m"), sem("s_dv")
        vb_ld = [sem("vb_ld0"), sem("vb_ld1")]
        vb_s0, g_scan, g_st, g_p, g_mm = sem("vb_s0"), sem("g_scan"), sem("g_st"), sem("g_p"), sem("g_mm")
        d_raw, d_sq = sem("d_raw"), sem("d_sq")
        wo, wo_free, ld_x2 = sem("wo"), sem("wo_free"), sem("ld_x2")
        wo_rd = [sem("wo_rd0"), sem("wo_rd1")]
        ld_n2, h_sq, n2_sd, t_ok = sem("ld_n2"), sem("h_sq"), sem("n2_sd"), sem("t_ok")
        tt_t, tt_a, tt_d, lgm = sem("tt_t"), sem("tt_a"), sem("tt_d"), sem("lgm")
        r1, r2, sel_ok, rank_ok, idx_ok = sem("r1"), sem("r2"), sem("sel_ok"), sem("rank_ok"), sem("idx_ok")
        zero_ok, zeroed, xs_ok = sem("zero_ok"), sem("zeroed"), sem("xs_ok")
        m_w = [sem(f"m_w{i}") for i in range(DEEP)]
        m_xe, m_yst = [sem("m_xe0"), sem("m_xe1")], [sem("m_yst0"), sem("m_yst1")]
        m_t, m_tev, m_h1, m_si, m_h = sem("m_t"), sem("m_tev"), sem("m_h1"), sem("m_si"), sem("m_h")
        m_ht, m_htev, m_y, m_ya, m_yd = sem("m_ht"), sem("m_htev"), sem("m_y"), sem("m_ya"), sem("m_yd")
        o_go, o_ld, o_t, o_tev, o_h1 = sem("o_go"), sem("o_ld"), sem("o_t"), sem("o_tev"), sem("o_h1")
        o_si, o_h, o_ht, o_htev, o_y, o_ya, o_yd, o_st = [sem(f"o_{k}") for k in ("si", "h", "ht", "htev", "y", "ya", "yd", "st")]
        yg, y_ok = [sem(f"yg{b}") for b in range(NB)], sem("y_ok")
        dch, ach, pch, outs = sem("dch"), sem("ach"), sem("pch"), sem("outs")
        y_out = sem("y_out")
        kv0, ea_ok, rst_out, rs_out = sem("kv0"), sem("ea_ok"), sem("rst_out"), sem("rs_out")
        k_out, par, lam_e, c_st = sem("k_out"), sem("par"), sem("lam_e"), sem("c_st")
        block = ctx.enter_context(nc.Block())

        def on_rows(idx):
            return bass.IndirectOffsetOnAxis(ap=idx, axis=0)

        class Chain:
            def __init__(self, eng, s):
                self.eng, self.s, self.n = eng, s, 0

            def __call__(self, ins):
                self.n += 1
                ins.then_inc(self.s, 1)
                self.eng.wait_ge(self.s, self.n)

        def bank2(pair, w, base=0):
            return ps[:, 2 * pair + base:2 * pair + base + 2, 0:w]

        def fold(a, w):
            return a.rearrange("p (a b) -> p a b", a=2)

        POOL_OUTS = 4

        @block.sync
        def _(sp):
            def reader_done(c):
                name = CH[c]
                if name in MERGES and name[1] != "D":
                    sp.wait_ge(pj, AT["P" + name[1:]] + 1)
                elif name.startswith("DP"):
                    sp.wait_ge(pj, AT[f"PD{4 * int(name[2]) + 3}"] + 1)
                elif name.startswith("WO"):
                    sp.wait_ge(wo_rd[int(name[2])], 1)
                else:
                    sp.wait_ge(pj, AT[name] + 1)

            def chunk(c):
                name = CH[c]
                if c >= RING:
                    reader_done(c - RING)
                if name in CHUNKS:
                    src, n = w_in[c], 1024
                elif name in MERGES:
                    src, n = w_mg[c - N_IN], 1280
                elif name.startswith("DP"):
                    src, n = w_dp[int(name[2])], 1024
                else:
                    src, n = w_out[int(name[2])], 1024
                s = c % RING
                sp.dma_start(ring[:, s * WCH:s * WCH + n], src).then_inc(w_ld[s], 16)

            def cache(j):
                b, half, is_v = j % 16 // 2, j % 2, j // 16
                if j >= 2:
                    i = j - 2
                    sp.wait_ge(*((k_used, i + 1) if i < 16 else (v_used, i - 15)))
                if j == 0:
                    sp.wait_ge(ld_pt, 16)
                    sp.wait_ge(kv0, 1)
                src = vc if is_v else kc
                for g in range(HALF):
                    at = b * PAGES + half * HALF + g
                    page = sp.value_load(pts[0:1, at:at + 1], min_val=0, max_val=kc.shape[0] - 1)
                    sp.dma_start(kvb[half][:, g, :], src[bass.ds(page, 1), :, :].rearrange("a p c -> (a p) c"))\
                      .then_inc(kv_ld[half], 16)
                if half:
                    if j == 1:
                        sp.wait_ge(s_qk, 16)
                        sp.wait_ge(s_v, 16)
                    row = scr_v[b:b + 1, 0:256] if is_v else scr_qk[b:b + 1, 256:512]
                    sp.dma_start(kvb[1][0:1, HALF, :], row).then_inc(kv_ld[1], 16)

            def values(j):
                if j >= 2:
                    sp.wait_ge(g_p, j - 1)
                    sp.wait_ge(g_st, j - 1)
                else:
                    sp.wait_ge(s_dv, 16)
                    sp.wait_ge(br_ok, 2)
                for h in range(H):
                    src = scr_dv[h * 64 + j * NV:h * 64 + (j + 1) * NV, :]
                    sp.dma_start(vb[32 * h:32 * h + 32, j % 2, :, :], src.partition_broadcast(32))\
                      .then_inc(vb_ld[j % 2], 16)

            sp.dma_start(xraw, xT_d).then_inc(ld_x, 16)
            for c in range(RING):
                chunk(c)
            sp.dma_start(pts[0:1, :], pt).then_inc(ld_pt, 16)
            sp.dma_start(g0[:, :], gla0_d).then_inc(ld_g0, 16)
            c = RING
            while c < CAT["BG0"]:
                chunk(c)
                c += 1
            sp.wait_ge(xn_ok, 1)
            cache(0)
            cache(1)
            while c < CAT["GB0"]:
                chunk(c)
                c += 1
            sp.wait_ge(rot_ok, 4)
            sp.dma_start(rs0, ret0_d).then_inc(ld_rs, 16)
            sp.wait_ge(sav, 16)
            for h in range(H):
                sp.dma_start(rv[64 * (h % 2):64 * (h % 2) + 64, h // 2, :, :],
                             scr_v[:, 256 + h * 64:256 + h * 64 + 64].partition_broadcast(64)).then_inc(ld_rs, 16)
            while c < CAT["GC0"]:
                chunk(c)
                c += 1
            sp.wait_ge(br_ok, 2)
            sp.wait_ge(rs_out, 16)
            sp.dma_start(qbc, scr_qk[:, 0:256].partition_broadcast(P)).then_inc(ld_q, 16)
            for j in range(2, 18):
                cache(j)
                if j % 2 and c < CAT["GD2"]:
                    chunk(c)
                    c += 1
            values(0)
            values(1)
            for j in range(18, 32):
                while c < min(CAT["GD0"] + (j - 18) // 2 + 3, CAT["GA0"]):
                    chunk(c)
                    c += 1
                cache(j)
            for j in range(2, GROUPS):
                while c < min(CAT["GA0"] + (j - 2) // 4 + 4, len(CH)):
                    chunk(c)
                    c += 1
                values(j)
            while c < len(CH):
                chunk(c)
                c += 1
            sp.wait_ge(g_mm, GROUPS)
            for b in range(NB):
                sp.dma_start(hres[b], x_d[b * RB:(b + 1) * RB, :]).then_inc(ld_x2, 16)
            sp.dma_start(n2row, n2_d.partition_broadcast(RB).rearrange("p a n -> p (a n)")).then_inc(ld_n2, 16)

            def expert(i, w):
                w1, w2 = (w_13[i], w_2[i]) if isinstance(i, int) else \
                    [m[bass.ds(i, 1), :, :, :].rearrange("a p k n -> (a p) k n") for m in (w_13, w_2)]
                sp.dma_start(w13b[w], w1).then_inc(m_w[w], 16)
                sp.dma_start(w2b[w], w2).then_inc(m_w[w], 16)

            def rows(i, s):
                src = scr_x[i * P:(i + 1) * P, :] if isinstance(i, int) else scr_x[bass.ds(i * P, P), :]
                sp.dma_start(xe[s], src).then_inc(m_xe[s], 16)

            sp.wait_ge(br_ok, 4)
            sp.wait_ge(mg_used, 4 * KT)
            expert(0, 0)
            expert(1, 1)
            sp.wait_ge(lgm, 1)
            expert(2, 2)
            sp.wait_ge(xs_ok, 16 * 2 * NB)
            rows(0, 0)
            rows(1, 1)
            expert(3, 3)
            sp.wait_ge(m_t, 1)
            rows(2, 0)
            with sp.Fori(1, NE // DEEP) as q:
                for w in range(DEEP):
                    sp.wait_ge(m_t, q * DEEP + (w - 2))
                    rows(q * DEEP + (w - 1), (w - 1) % 2)
                    sp.wait_ge(m_y, q * DEEP + (w - DEEP + 1))
                    expert(q * DEEP + w, w)
            sp.wait_ge(m_t, NE - 2)
            rows(NE - 1, 1)
            sp.wait_ge(idx_ok, 1)
            n_over = sp.value_load(itab[0:1, 10 + OVER:11 + OVER], min_val=0, max_val=OVER)
            with sp.If(n_over > 0):
                sp.wait_ge(m_h1, NE)
                sp.wait_ge(m_y, NE)
                sp.wait_ge(m_t, NE)
                with sp.Fori(0, n_over) as i:
                    sp.wait_ge(o_go, i + 1)
                    e = sp.value_load(itab[0:1, bass.ds(i + 10, 1)], min_val=0, max_val=NE - 1)
                    sp.dma_start(w13b[0], w_13[bass.ds(e, 1), :, :, :].rearrange("a p k n -> (a p) k n")).then_inc(o_ld, 16)
                    sp.dma_start(w2b[0], w_2[bass.ds(e, 1), :, :, :].rearrange("a p k n -> (a p) k n")).then_inc(o_ld, 16)
                    sp.dma_start(xe[0], scr_x[bass.ds(i * P + NE * P, P), :]).then_inc(o_ld, 16)
            for b in range(NB):
                sp.wait_ge(y_ok, b + 1)
                sp.dma_start(o["y"][b * RB:(b + 1) * RB, :], hres[b]).then_inc(y_out, 16)
            sp.wait_ge(y_out, 16 * NB)

        @block.tensor
        def _(pe):
            def loaded(c):
                pe.wait_ge(w_ld[c % RING], 16 * (c // RING + 1))

            def wsl(c, k, n=P):
                s = c % RING * WCH
                return ring[:, s + k * P:s + k * P + n]

            def free(t):
                if t >= 2:
                    pe.wait_ge(pj_free, t - 1)

            def stat(name, lhsT, srcs, hw):
                t = AT[name]
                free(t)
                for h in range(2):
                    for i, s in enumerate(srcs):
                        mm = pe.matmul(ps[:, 2 * (t % 2) + h, 0:hw], lhsT, s[:, h * hw:(h + 1) * hw],
                                       start=(i == 0), stop=(i == len(srcs) - 1))
                mm.then_inc(pj, 1)

            def tiled(name, hw=HT, col0=0):
                t, c = AT[name], CAT[name]
                free(t)
                loaded(c)
                for h in range(2):
                    for k in range(KT):
                        mm = pe.matmul(ps[:, 2 * (t % 2) + h, 0:hw], wsl(c, k),
                                       xnv[:, k, col0 + h * hw:col0 + (h + 1) * hw], start=(k == 0), stop=(k == KT - 1))
                mm.then_inc(pj, 1)

            pe.wait_ge(ld_c, 16)
            for k in range(KT):
                pe.wait_ge(x_sq, k + 1)
                for h in range(2):
                    mm = pe.matmul(ps[:, 4 + h, 0:HT], cc(C_ONE, P), view(kv, (k % 2) * T, 2, HT)[:, h, :],
                                   start=(k == 0), stop=(k == KT - 1))
                mm.then_inc(xms, 1)
            pe.wait_ge(xn_ok, 1)
            pe.wait_ge(ld_v, 16)

            def values_tile(i):
                t, c = AT[f"V{i}"], CAT[f"V{i}"]
                free(t)
                loaded(c)
                for b in range(NB):
                    rows = min(P, T - b * P)
                    for k in range(KT):
                        mm = pe.matmul(ps[0:rows, 2 * (t % 2) + b // 4, (b % 4) * P:(b % 4 + 1) * P],
                                       xnv[:, k, b * P:b * P + rows], wsl(c, k), start=(k == 0), stop=(k == KT - 1))
                mm.then_inc(pj, 1)

            def scores(s):
                h, i = s // 4, s % 4
                n = META + P * (i + 1)
                if s >= 1:
                    pe.wait_ge(sexp, 2 * s)
                if n > 512:
                    pe.wait_ge(sav_ev, s - 1)
                for m in range(2):
                    r = slice(32 * ((2 * h + m) % 4), 32 * ((2 * h + m) % 4) + 32)
                    for a, b, bk, at in ((0, min(n, 512), 4 + m, 0), (512, n, 7, 256 + META * m)):
                        if a < b:
                            if bk == 7 and m:
                                pe.wait_ge(sco, 2 * s + 1)
                            mm = pe.matmul(ps[:, bk, at:at + b - a], aqk[r, h // 2, META + P * i:META + P * (i + 1)],
                                           aqk[r, 2 + h // 2, a:b], start=True, stop=True)
                    mm.then_inc(sco, 1)

            def wt_at(b):
                return (6, P * b) if b < 4 else (7, 0)

            def transposes(s):
                i = s % 4
                pe.wait_ge(scomb, s + 1)
                if s >= 1:
                    pe.wait_ge(swt_ev, s)
                if i == 3:
                    pe.wait_ge(sav_ev, s)
                for b in range(i + 2):
                    rows = P if b <= i else META
                    bk, c0 = wt_at(b)
                    mm = pe.transpose(ps[0:rows, bk, c0:c0 + P], prb[:, s % 2, 0, b * P:b * P + rows], ident)
                mm.then_inc(swt, 1)

            def weighted(s):
                h, i = s // 4, s % 4
                pe.wait_ge(swt_ev, s + 1)
                if s >= 1:
                    pe.wait_ge(sav_ev, s)
                if i == 2:
                    pe.wait_ge(sexp, 2 * s + 4)
                for b in range(i + 2):
                    rows = P if b <= i else META
                    mm = pe.matmul(ps[64 * (h % 2):64 * (h % 2) + 64, 7, 384:512], vt[0:rows, b, h * 64:h * 64 + 64],
                                   wtb[0:rows, s % 2, b, :], start=(b == 0), stop=(b == i + 1))
                mm.then_inc(sav, 1)

            def extras(name):
                s = AT[name] - UNIT0
                if s == 0:
                    pe.wait_ge(a_ok, 4)
                if 2 <= s < 18:
                    weighted(s - 2)
                if 1 <= s < 17:
                    transposes(s - 1)
                if 0 <= s < 16:
                    scores(s)

            for name in PROJ[:AT["LA"] + 1]:
                t = AT[name]
                if name == "BQ1":
                    pe.wait_ge(a_ok, 4)
                    for i in range(4):
                        mm = pe.transpose(ps[0:DEC, 4, i * P:(i + 1) * P], aqk[:, i, L:T], ident)
                    mm.then_inc(t8, 1)
                if name[0] == "V":
                    values_tile(int(name[1]))
                elif name.startswith("AMS"):
                    pe.wait_ge(a_sq, int(name[3]) + 1)
                    stat(name, cc(C_B32, P), [asq[:, int(name[3]), :]], HT)
                elif name.startswith("ROT"):
                    pe.wait_ge(pj_free, AT["BK1"] + 1)
                    stat(name, cc(C_PERM, P), [bqk[:, int(name[3]), :]], HT)
                elif name == "DA":
                    free(t)
                    for h in range(2):
                        for k in range(KT):
                            mm = pe.matmul(ps[0:16, 2 * (t % 2) + h, 0:HT], vv(V_DA + 16 * k, 16),
                                           xnv[:, k, h * HT:(h + 1) * HT], start=(k == 0), stop=(k == KT - 1))
                    mm.then_inc(pj, 1)
                elif name == "LA":
                    free(t)
                    pe.wait_ge(pj_free, AT["DA"] + 1)
                    for h in range(2):
                        mm = pe.matmul(ps[:, 2 * (t % 2) + h, 0:HT], vv(V_G2, P, slice(0, 16)),
                                       das[:, h * HT:(h + 1) * HT], start=True, stop=True)
                    mm.then_inc(pj, 1)
                else:
                    tiled(name)
                if UNIT0 <= t:
                    if t == UNIT0:
                        pe.wait_ge(t8_ev, 1)
                    extras(name)

            pe.wait_ge(rot_ok, 4)
            pe.wait_ge(sexp, 32)
            pe.wait_ge(swt_ev, 16)
            pe.wait_ge(sav_ev, 16)
            units = [(h, j) for h in range(H) for j in range(NB)]

            def ret_scores(u):
                h, j = units[u]
                rows, t0 = min(P, L - j * P), max(META, j * P)
                r = slice(64 * (h % 2), 64 * (h % 2) + 64)
                if u >= 2:
                    pe.wait_ge(at_w, u - 1)
                pe.matmul(ps[0:rows, 4 + u % 2, 0:L - t0], bqk[r, 2 + h // 2, j * P:j * P + rows],
                          bqk[r, h // 2, t0:L], start=True, stop=True).then_inc(at_s, 1)

            def ret_out(u):
                h, j = units[u]
                rows, t0 = min(P, L - j * P), max(META, j * P)
                pe.wait_ge(at_w, u + 1)
                pe.matmul(ps[64 * (h % 2):64 * (h % 2) + 64, 6 + h // 2, t0 - META:SEQ],
                          vt[0:rows, j, 256 + h * 64:256 + h * 64 + 64], atb[0:rows, u % 2, 0:L - t0],
                          start=(j == 0), stop=(j == NB - 1)).then_inc(at_o, 1)

            for u in range(len(units) + 1):
                if u < len(units):
                    ret_scores(u)
                if u >= 1:
                    ret_out(u - 1)
            for t in range(2):
                for b in range(4):
                    pe.transpose(ps[:, 4 + t, b * P:(b + 1) * P], bqk[:, 2 + t, b * P:(b + 1) * P], ident)
            pe.wait_ge(ob_ev, 1)
            for t in range(2):
                mm = pe.transpose(ps[0:TAIL, 6, t * P:(t + 1) * P], bqk[:, 2 + t, 4 * P:L], ident)
            mm.then_inc(kt_t, 1)
            pe.wait_ge(kd_ok, 1)
            pe.wait_ge(ob_ev, 2)
            for h in range(H):
                for b in range(NB):
                    rows = P if b < 4 else TAIL
                    mm = pe.matmul(ps[0:64, 7, h * 64:h * 64 + 64], kdv[0:rows, b, h * 64:h * 64 + 64],
                                   vt[0:rows, b, 256 + h * 64:256 + h * 64 + 64], start=(b == 0), stop=(b == NB - 1))
            mm.then_inc(st_mm, 1)
            pe.wait_ge(rs_ok, 1)
            for h in range(H):
                r = slice(64 * (h % 2), 64 * (h % 2) + 64)
                for b in range(DEC):
                    mm = pe.matmul(ps[r, 6, (h // 2) * DEC + b:(h // 2) * DEC + b + 1], rs0[r, h // 2, b, :],
                                   bqk[r, h // 2, L + b:L + b + 1], start=True, stop=True)
            mm.then_inc(ro_mm, 1)
            pe.wait_ge(b_raw, 1)
            for t in range(2):
                stat(f"BMEAN{t}", cc(C_B64, P), [brv[:, 2 + t, :]], HN)
            for t in range(2):
                pe.wait_ge(b_sq, t + 1)
                stat(f"BVAR{t}", cc(C_B64, P), [bn[:, t, :]], HN)

            for g, at in (("CR", V_WA), ("CI", V_WX)):
                for t in range(2):
                    pe.wait_ge(conv_ok, 2)
                    stat(f"{g}{t}", vv(at + t * P, P), [xc[:, t, :]], HT)

            def gate_tile(n, m):
                tiled(f"G{n}{m}", HN, META)

            def branch_tile(n, m):
                name = f"P{n}{m}"
                t = AT[name]
                free(t)
                if n == "D":
                    c = CAT["DP0"] + m // 4
                    loaded(c)
                for h in range(2):
                    for k in range(2):
                        w = (wsl(CAT["DP0"] + m // 4, (m % 4) * 2 + k) if n == "D" else wsl(CAT[f"G{n}{m}"], KT + k))
                        mm = pe.matmul(ps[:, 2 * (t % 2) + h, 0:HN], w,
                                       brv[:, BR[n] + k, h * HN:(h + 1) * HN], start=(k == 0), stop=(k == 1))
                mm.then_inc(pj, 1)

            for i, n in enumerate("BC"):
                for m in range(KT):
                    gate_tile(n, m)
                    if m == 0:
                        pe.wait_ge(br_ok, i + 1)
                    branch_tile(n, m)
            pe.wait_ge(s_mx, 1)
            pe.transpose(ps[0:64, 4, 0:P], mx, ident).then_inc(s_mxt, 1)
            pe.wait_ge(s_mx1, 1)
            pe.matmul(ps[:, 5, 0:64], mxb, cst[0:64, C_ID:C_ID + 64], start=True, stop=True).then_inc(s_mxm, 1)
            gate_tile("D", 0)
            pe.wait_ge(s_sum, 1)
            pe.matmul(ps[:, 5, 64:128], cc(C_ONE, P), sm, start=True, stop=True).then_inc(s_tot, 1)
            gate_tile("D", 1)
            pe.wait_ge(s_w, 1)

            def sample_values(j):
                b, half = j // 2, j % 2
                ns = HALF + half
                pe.wait_ge(kv_ld[half], (128, 144)[half] * (DEC + b + 1))
                for s in range(ns):
                    for t in range(2):
                        mm = pe.matmul(ps[:, 4 + t, 256 + 2 * b:256 + 2 * b + 2], kvb[half][:, s, t * P:(t + 1) * P],
                                       W[:, b, half * HALF + s, 2 * t:2 * t + 2],
                                       start=(half == 0 and s == 0), stop=(half == 1 and s == ns - 1))
                mm.then_inc(v_used, 1)

            j = 0
            for m in range(2, KT):
                gate_tile("D", m)
                for _ in range(3 if m < 6 else 2):
                    sample_values(j)
                    j += 1
            assert j == 16

            for t in range(2):
                pe.wait_ge(a_osq, t + 1)
                stat(f"AOS{t}", cc(C_B64, P), [osq[:, t, :]], HN)
            pe.wait_ge(st_ev, 1)

            def gla(j):
                pe.wait_ge(g_p, j + 1)
                for i in range(NV):
                    v = j * NV + i
                    g, v32 = v // 32, v % 32
                    lhsT = cst[:, C_SEL + 31 - v32:C_SEL + 31 - v32 + P]
                    pe.matmul(ps[:, 6 + g, 0:SEQ], lhsT, pbv[:, j % 2, i, 0:SEQ], start=(v32 == 0), stop=(v32 == 31))
                    mm = pe.matmul(ps[:, 4, g * DEC:(g + 1) * DEC], lhsT, pbv[:, j % 2, i, SEQ + 1:L:2],
                                   start=(v32 == 0), stop=(v32 == 31))
                mm.then_inc(g_mm, 1)

            for m in range(KT):
                gate_tile("A", m)
                gla(4 * m)
                gla(4 * m + 1)
                if m == 0:
                    pe.wait_ge(br_ok, 3)
                branch_tile("A", m)
                gla(4 * m + 2)
                gla(4 * m + 3)
            pe.wait_ge(d_sq, 2)
            stat("DOS", cc(C_B32, P), [osq[:, t, :] for t in range(2)], HN)
            pe.wait_ge(br_ok, 4)
            for m in range(KT):
                branch_tile("D", m)

            pe.wait_ge(mg_used, 4 * KT)
            pe.wait_ge(pj_free, len(PROJ))
            for c8 in range(8):
                half, kp = c8 // 4, c8 % 4
                c = CAT[f"WO{c8}"]
                loaded(c)
                for kk in range(2):
                    k = 2 * kp + kk
                    for b in range(NB):
                        if k == 0 and half and b >= 3:
                            pe.wait_ge(wo_free, b - 2)
                        s0 = c % RING * WCH + kk * 512
                        mm = pe.matmul(ps[0:RB, (half * NB + b) % 8, :], acc[:, k, b * RB:(b + 1) * RB],
                                       ring[:, s0:s0 + 512], start=(k == 0), stop=(k == KT - 1))
                        if k == KT - 1:
                            mm.then_inc(wo, 1)
                if c8 < len(CH) - RING - CAT["WO0"]:
                    mm.then_inc(wo_rd[c8], 1)
            pe.wait_ge(wo_free, 2 * NB)
            for b in range(NB):
                pe.wait_ge(t_ok, b + 1)
                if b >= 2:
                    pe.wait_ge(tt_a, b - 1)
                    pe.wait_ge(tt_d, b - 1)
                for k in range(KT):
                    mm = pe.transpose(ps[:, 2 * (b % 2) + k // 4, (k % 4) * P:(k % 4) * P + RB], tk[b][:, k * P:(k + 1) * P],
                                      cst[0:RB, C_ID:C_ID + RB])
                mm.then_inc(tt_t, 1)
            for b in range(NB):
                pe.wait_ge(tt_a, b + 1)
                pe.wait_ge(tt_d, b + 1)
                for k in range(KT):
                    mm = pe.matmul(ps[0:RB, 6, b * 32:b * 32 + 20], tT[:, k, b * RB:(b + 1) * RB],
                                   vv(V_RW + 20 * k, 20), start=(k == 0), stop=(k == KT - 1))
            mm.then_inc(lgm, 1)
            pe.wait_ge(sel_ok, 1)
            selm = sel[0:RB].rearrange("p b g e -> p (b g e)")
            pe.matmul(ps[0:RB, 4, 0:NB * NE], cst[0:RB, C_LT:C_LT + RB], selm, start=True, stop=True)
            pe.matmul(ps[:, 5, 0:NB * NE], cst[0:RB, C_ONE:C_ONE + P], selm, start=True, stop=True).then_inc(rank_ok, 1)

            def rows_T(s):
                for k in range(KT):
                    mm = pe.transpose(ps[:, k // 4, (k % 4) * P:(k % 4 + 1) * P], xe[s][:, k * P:(k + 1) * P], ident)
                return mm

            def hidden(s, w):
                for k in range(KT):
                    mm = pe.matmul(ps[:, 2 + s, :], xeT[s][:, k, :], w13b[w][:, k, :], start=(k == 0), stop=(k == KT - 1))
                return mm

            def hidden_T(s):
                for f in range(2):
                    mm = pe.transpose(ps[:, 4 + s, f * P:(f + 1) * P], hm[s][:, f * P:(f + 1) * P], ident)
                return mm

            def outputs(s, w):
                for n in range(2):
                    for f in range(2):
                        mm = pe.matmul(ps[:, 6 + n, :], hT[s][:, f, :], w2b[w][:, f, n * 512:(n + 1) * 512],
                                       start=(f == 0), stop=(f == 1))
                return mm

            def step(q, w):
                i, s, o_ = q * DEEP + w, w % 2, 1 - w % 2
                first, last = (isinstance(i, int) and i == n for n in (0, NE - 1))
                if not first:
                    pe.wait_ge(m_h, i)
                    hidden_T(o_).then_inc(m_ht, 1)
                pe.wait_ge(m_tev, i + 1)
                pe.wait_ge(m_w[w], q * 32 + 32)
                hidden(s, w).then_inc(m_h1, 1)
                if not last:
                    pe.wait_ge(m_xe[o_], q * (8 * DEEP) + 16 * ((w + 1) // 2 + 1))
                    rows_T(o_).then_inc(m_t, 1)
                if not first:
                    end(i, w)

            def end(i, w):
                pe.wait_ge(m_htev, i)
                if not (isinstance(i, int) and i < 2):
                    pe.wait_ge(m_ya, i - 1)
                    pe.wait_ge(m_yd, i - 1)
                outputs((w - 1) % 2, (w - 1) % DEEP).then_inc(m_y, 1)

            pe.wait_ge(m_xe[0], 16)
            rows_T(0).then_inc(m_t, 1)
            for w in range(DEEP):
                step(0, w)
            with pe.Fori(1, NE // DEEP - 1) as q:
                for w in range(DEEP):
                    step(q, w)
            for w in range(DEEP):
                step(NE // DEEP - 1, w)
            pe.wait_ge(m_h, NE)
            hidden_T(1).then_inc(m_ht, 1)
            end(NE, 0)

            pe.wait_ge(idx_ok, 1)
            n_over = pe.value_load(itab[0:1, 10 + OVER:11 + OVER], min_val=0, max_val=OVER)
            with pe.If(n_over > 0):
                pe.wait_ge(m_ya, NE)
                pe.wait_ge(m_yd, NE)
                with pe.Fori(0, n_over) as i:
                    pe.wait_ge(o_ld, i * 48 + 48)
                    rows_T(0).then_inc(o_t, 1)
                    pe.wait_ge(o_tev, i + 1)
                    hidden(0, 0).then_inc(o_h1, 1)
                    pe.wait_ge(o_h, i + 1)
                    hidden_T(0).then_inc(o_ht, 1)
                    pe.wait_ge(o_htev, i + 1)
                    outputs(0, 0).then_inc(o_y, 1)

        @block.scalar
        def _(act):
            link = Chain(act, ach)
            act.dma_start(cst[:, :], const_d).then_inc(ld_c, 16)
            act.dma_start(vec[:, :], vec_d).then_inc(ld_v, 16)
            act.wait_ge(ld_x, 16)
            for k in range(KT):
                if k >= 2:
                    act.wait_ge(xms, k - 1)
                act.activation(view(kv, (k % 2) * T, T), xraw[:, k, :], ACT.Square).then_inc(x_sq, 1)
            act.wait_ge(ld_c, 16)
            act.wait_ge(ld_v, 16)
            eps = cc(C_EPS)
            act.wait_ge(xms, KT)
            act.activation(fold(view(kv, 0, T), HT), bank2(2, HT), ACT.Sqrt, bias=eps, scale=1.0 / DM).then_inc(xsd, 1)

            act.activation(xxs[:, :, :, 0:3], view(vec, V_ST, 2, DEC, 3), ACT.Copy).then_inc(c_st, 1)
            act.wait_ge(par, 1)
            act.activation(sc[:, 3:5], sc[:, 1:3], ACT.Exp).then_inc(lam_e, 1)
            link(act.activation(sc[:, 24:26], vv(V_LL, 2), ACT.Abs))
            act.activation(sc[:, 26:28], sc[:, 24:26], ACT.Exp, scale=-1.0).then_inc(lam_e, 1)

            def ready(name):
                act.wait_ge(pj, AT[name] + 1)
                return 2 * (AT[name] % 2)

            def pair(name, w):
                b = ready(name)
                return ps[:, b:b + 2, 0:w]

            def copy(name, dst, w, func=ACT.Copy, **kw):
                act.activation(fold(dst, w), pair(name, w), func, **kw).then_inc(pj_free, 1)

            def spread(name, dst, off=0, scale=1.0, smp=None):
                b = ready(name)
                act.activation(dst[:, off:off + HT], ps[:, b, 0:HT], ACT.Copy, scale=scale)
                act.activation(dst[:, off + HT:off + L], ps[:, b + 1, 0:L - HT], ACT.Copy, scale=scale)
                act.activation(smp, ps[:, b + 1, L - HT:HT], ACT.Copy, scale=scale).then_inc(pj_free, 1)

            def exps(s):
                i = s % 4
                n = META + P * (i + 1)
                if s >= 2:
                    act.wait_ge(swt, s - 1)
                for m in range(2):
                    act.wait_ge(smx, 2 * s + (2 if i == 3 else m + 1))
                    nb = sc[:, 8 + 2 * (s % 2) + m:9 + 2 * (s % 2) + m]
                    ins = act.activation(prb[:, s % 2, m, 0:min(n, 512)], ps[:, 4 + m, 0:min(n, 512)], ACT.Exp, bias=nb,
                                         accum_out=sc[:, 12 + 2 * (s % 2) + m:13 + 2 * (s % 2) + m])
                    if i == 3:
                        c0 = 256 + META * m
                        ins = act.activation(prb[:, s % 2, m, 512:n], ps[:, 7, c0:c0 + META], ACT.Exp, bias=nb,
                                             accum_out=sc[:, 36 + m:37 + m])
                    ins.then_inc(sexp, 1)

            def wt_copy(s):
                i = s % 4
                act.wait_ge(swt, s + 1)
                if s >= 2:
                    act.wait_ge(sav, s - 1)
                act.activation(wtb[:, s % 2, 0:i + 1, :], ps[:, 6, 0:(i + 1) * P].rearrange("p (a b) -> p a b", b=P),
                               ACT.Copy)
                src = ps[0:META, 7, 0:P] if i == 3 else ps[0:META, 6, P * (i + 1):P * (i + 2)]
                act.activation(wtb[0:META, s % 2, i + 1, :], src, ACT.Copy).then_inc(swt_ev, 1)

            for name in PROJ[:AT["LA"] + 1]:
                t = AT[name]
                kind, i = name[:-1], (int(name[-1]) if name[-1].isdigit() else 0)
                if kind in ("AQ", "AK"):
                    j = 2 * (kind == "AK") + i
                    act.activation(fold(aqk[:, j, :], HT), pair(name, HT), ACT.Copy).then_inc(pj_free, 1)
                    act.wait_ge(pj_free, t + 1)
                    act.wait_ge(xn_ok, 1)
                    act.activation(asq[:, j, :], aqk[:, j, :], ACT.Square).then_inc(a_sq, 1)
                elif kind == "V":
                    b = ready(name)
                    act.activation(vt[:, 0:4, i * P:(i + 1) * P], ps[:, b, :].rearrange("p (a c) -> p a c", c=P), ACT.Copy)
                    act.activation(vt[0:T - 4 * P, 4, i * P:(i + 1) * P], ps[0:T - 4 * P, b + 1, 0:P], ACT.Copy)\
                       .then_inc(pj_free, 1)
                    if i == 3:
                        act.wait_ge(pj_free, t + 1)
                        act.dma_start(scr_v[:, :], vt[TAIL:TAIL + DEC, 4, :]).then_inc(s_v, 16)
                elif kind == "AMS":
                    copy(name, arr[:, i, :], HT, ACT.Sqrt, bias=eps)
                elif kind == "BQ":
                    copy(name, bqk[:, i, :], HT)
                    if i == 1:
                        act.wait_ge(t8, 1)
                        link(act.activation(qk8, ps[0:DEC, 4, :], ACT.Copy))
                        act.sem_inc(t8_ev, 1)
                        act.dma_start(scr_qk[:, :], qk8).then_inc(s_qk, 16)
                elif kind == "BK":
                    copy(name, bqk[:, 2 + i, :], HT, ACT.Copy, scale=0.125)
                elif kind == "BG":
                    copy(name, bgv[:, i, :], HT, ACT.Silu)
                elif kind == "ROT":
                    if i >= 2:
                        act.wait_ge(rot_ok, i - 1)
                    copy(name, rot[:, i % 2, :], HT)
                elif kind == "CX":
                    spread(name, cxv[:, i, :], 3, smp=xxs[:, i, :, 3])
                elif kind == "CG":
                    copy(name, cgv[:, i, :], HT, ACT.Gelu_apprx_tanh)
                elif name == "DQ":
                    spread(name, dqv, 0, 32 ** -0.5, smp=dqv[:, L + 1:XT:2])
                elif name == "DK":
                    spread(name, dkv, smp=dkv[:, L + 1:XT:2])
                elif kind == "DV":
                    spread(name, dvv[:, i, :], smp=dvv[:, i, L + 1:XT:2])
                    if i == 1:
                        act.wait_ge(pj_free, t + 1)
                        act.wait_ge(kv0, 1)
                        act.dma_start(scr_dv.rearrange("(a p) t -> p a t", p=P), dvv).then_inc(s_dv, 16)
                elif kind == "DR":
                    copy(name, drv[:, i, :], HT, ACT.Silu)
                elif name == "DA":
                    b = ready(name)
                    act.wait_ge(s_qk, 16)
                    act.activation(fold(das, HT), ps[0:16, b:b + 2, 0:HT], ACT.Copy).then_inc(pj_free, 1)
                elif name == "LA":
                    act.activation(fold(dg[:, 0, :], HT), pair(name, HT), ACT.Identity, bias=vv(V_GB)).then_inc(pj_free, 1)
                    act.wait_ge(pj_free, t + 1)
                    link(act.activation(dg[:, 1, :], dg[:, 0, :], ACT.Abs))
                    link(act.activation(dg[:, 1, :], dg[:, 1, :], ACT.Exp, scale=-1.0))
                    act.activation(dg[:, 1, :], dg[:, 1, :], ACT.Ln, bias=cc(C_ONE)).then_inc(la_z, 1)
                s = t - UNIT0
                if 0 <= s < 16:
                    exps(s)
                if 1 <= s < 17:
                    wt_copy(s - 1)
            act.wait_ge(la_m, 1)
            for i in range(NV):
                act.activation(ea[:, i * XT:i * XT + L], dg[:, 0, 0:L], ACT.Exp, scale=1.0 / 16)
                act.activation(ea[:, i * XT + L + 1:(i + 1) * XT:2], dg[:, 0, L:T], ACT.Exp, scale=1.0 / 16).then_inc(la_e, 1)
            for t in range(2):
                act.wait_ge(at_o, 2 * NB * (t + 1))
                act.activation(brv[:, 2 + t, 0:SEQ], ps[:, 6 + t, :], ACT.Copy).then_inc(ob_ev, 1)
            act.wait_ge(st_mm, 1)
            act.activation(rst, ps[0:64, 7, 0:256].rearrange("p (h v) -> p h v", h=H), ACT.Copy).then_inc(st_ev, 1)
            act.wait_ge(ro_mm, 1)
            act.activation(brv[:, 2:4, SEQ:N], ps[:, 6, 0:2 * DEC].rearrange("p (t b) -> p t b", t=2), ACT.Copy)\
               .then_inc(b_raw, 1)
            for t in range(2):
                copy(f"BMEAN{t}", bsd[:, t, :], HN)
            for t in range(2):
                act.wait_ge(b_cen, t + 1)
                act.activation(bn[:, t, :], brv[:, 2 + t, :], ACT.Square).then_inc(b_sq, 1)
            for t in range(2):
                copy(f"BVAR{t}", bsd[:, t, :], HN, ACT.Sqrt, bias=eps)
            act.wait_ge(c_par, 1)
            for t in range(2):
                copy(f"CR{t}", rr[:, t, :], HT, ACT.Sigmoid, bias=vv(V_BA + t))
            for t in range(2):
                copy(f"CI{t}", ri[:, t, :], HT, ACT.Sigmoid, bias=vv(V_BX + t))
            act.wait_ge(pj_free, AT["CI1"] + 1)
            for t in range(2):
                act.activation(aa[:, t, :], rr[:, t, :], ACT.Exp, scale=sc[:, 20 + t:21 + t])
                act.activation(th[:, t, :], rr[:, t, :], ACT.Tanh, scale=sc[:, 20 + t:21 + t]).then_inc(c_act, 1)
            act.wait_ge(c_q, 1)
            act.activation(rr[:, :, :], th[:, :, :], ACT.Sqrt, scale=-1.0).then_inc(c_act, 1)

            def merge(n, m, i):
                if i >= 2:
                    act.wait_ge(mg_used, i - 1)
                if i == 0:
                    act.wait_ge(br_ok, 1)
                copy(f"G{n}{m}", sgtv[:, i % 2, :], HN, ACT.Sigmoid, bias=vv(V_BM + 8 * "ABCD".index(n) + m))
                copy(f"P{n}{m}", ptv[:, i % 2, :], HN)
                act.wait_ge(pj_free, AT[f"P{n}{m}"] + 1)
                act.sem_inc(mg, 1)

            for i in range(2 * KT):
                merge("BC"[i // KT], i % KT, i)
            act.wait_ge(rst_out, 16)
            act.wait_ge(la_e, NV)
            for m in range(KT):
                if m == 1:
                    act.wait_ge(s_sub, 1)
                    act.activation(S[:, :, :, :], S[:, :, :, :], ACT.Exp).then_inc(s_exp, 1)
                copy(f"GD{m}", sgv[:, m, :], HN, ACT.Sigmoid, bias=vv(V_BM + 24 + m))
            act.wait_ge(v_used, 2 * DEC)
            for t in range(2):
                for hh_ in range(2):
                    r = slice(64 * hh_, 64 * hh_ + 64)
                    ins = act.activation(brv[r, t, SEQ:N], ps[r, 4 + t, 256 + hh_:256 + 2 * DEC:2], ACT.Copy)
                ins.then_inc(a_raw, 1)
            for t in range(2):
                act.wait_ge(a_raw, 2)
                act.activation(osq[:, t, :], brv[:, t, :], ACT.Square).then_inc(a_osq, 1)
            for t in range(2):
                copy(f"AOS{t}", osd[:, t, :], HN, ACT.Sqrt, bias=eps)
            for m in range(KT):
                merge("A", m, 2 * KT + m)
            act.wait_ge(g_mm, GROUPS)
            for g in range(2):
                act.activation(brv[:, 6 + g, 0:SEQ], ps[:, 6 + g, :], ACT.Copy)
                act.activation(brv[:, 6 + g, SEQ:N], ps[:, 4, g * DEC:(g + 1) * DEC], ACT.Copy).then_inc(d_raw, 1)
            act.wait_ge(d_raw, 2)
            act.wait_ge(br_ok, 3)
            for g in range(2):
                act.activation(osq[:, g, :], brv[:, 6 + g, :], ACT.Square).then_inc(d_sq, 1)
            copy("DOS", osd[:, 0, :], HN, ACT.Sqrt, bias=eps, scale=0.5)
            for m in range(KT):
                i = 3 * KT + m
                act.wait_ge(mg_used, i - 1)
                copy(f"PD{m}", ptv[:, i % 2, :], HN)
                act.wait_ge(pj_free, AT[f"PD{m}"] + 1)
                act.sem_inc(mg, 1)
            for b in range(NB):
                act.wait_ge(wo_free, NB + b + 1)
                if b:
                    act.wait_ge(h_sq, b)
                act.activation(sgt[0:RB, 0:DM], hres[b], ACT.Square, accum_out=sc[0:RB, 40 + b:41 + b]).then_inc(h_sq, 1)
            act.wait_ge(h_sq, NB)
            act.activation(sc[0:RB, 45:50], sc[0:RB, 40:45], ACT.Sqrt, bias=cst[0:RB, C_EPS:C_EPS + 1], scale=1.0 / DM)\
               .then_inc(n2_sd, 1)
            for b in range(NB):
                act.wait_ge(tt_t, b + 1)
                act.activation(tT[:, 0:4, b * RB:(b + 1) * RB],
                               ps[:, 2 * (b % 2), :].rearrange("p (k n) -> p k n", n=P)[:, :, 0:RB], ACT.Copy).then_inc(tt_a, 1)
            act.wait_ge(r1, 1)
            act.activation(rt[0:RB, 0, :, :], rt[0:RB, 0, :, :], ACT.Exp).then_inc(r2, 1)
            act.wait_ge(r1, 2)
            act.activation(rt[0:RB, 1, :, 0:1], rt[0:RB, 1, :, 0:1], ACT.Exp).then_inc(r2, 1)

            def rows_copy(s):
                return act.activation(xeT[s].rearrange("p (a k) n -> p a (k n)", a=2), ps[:, 0:2, :], ACT.Copy)

            def silu(s):
                return act.activation(si[s], ps[:, 2 + s, 0:256], ACT.Silu)

            def out_copy(s):
                return act.activation(yb[s][:, 0, :], ps[:, 6, :], ACT.Copy)

            def step(q, s, last=False):
                i, o_ = q * 2 + s, 1 - s
                act.wait_ge(m_h1, i + 1)
                silu(s).then_inc(m_si, 1)
                if not last:
                    act.wait_ge(m_t, i + 2)
                    rows_copy(o_).then_inc(m_tev, 1)
                if isinstance(i, int) and i == 0:
                    return
                act.wait_ge(m_y, i)
                if not (isinstance(i, int) and i < 3):
                    act.wait_ge(m_yst[o_], q * 16 - (16 if s == 0 else 0))
                out_copy(o_).then_inc(m_ya, 1)

            act.wait_ge(m_t, 1)
            rows_copy(0).then_inc(m_tev, 1)
            step(0, 0)
            step(0, 1)
            step(1, 0)
            step(1, 1)
            with act.Fori(2, PAIRS - 1) as q:
                step(q, 0)
                step(q, 1)
            step(PAIRS - 1, 0)
            step(PAIRS - 1, 1, last=True)
            act.wait_ge(m_y, NE)
            act.wait_ge(m_yst[1], 16 * (PAIRS - 1))
            out_copy(1).then_inc(m_ya, 1)

            act.wait_ge(idx_ok, 1)
            n_over = act.value_load(itab[0:1, 10 + OVER:11 + OVER], min_val=0, max_val=OVER)
            with act.If(n_over > 0):
                act.wait_ge(m_yst[0], 16 * PAIRS)
                with act.Fori(0, n_over) as i:
                    act.wait_ge(o_t, i + 1)
                    rows_copy(0).then_inc(o_tev, 1)
                    act.wait_ge(o_h1, i + 1)
                    silu(0).then_inc(o_si, 1)
                    act.wait_ge(o_y, i + 1)
                    out_copy(0).then_inc(o_ya, 1)

        @block.vector
        def _(dve):
            link = Chain(dve, dch)
            tt, ts, stt = dve.tensor_tensor, dve.tensor_scalar, dve.scalar_tensor_tensor

            dve.wait_ge(ld_v, 16)
            lv = view(vec, V_LAM, 2, 2, 32)
            lp = view(sgt, 0, 2, 32)
            link(tt(lp, lv[:, :, 0, :], lv[:, :, 1, :], ALU.mult))
            dve.tensor_reduce(sc[:, 1:3], lp, X, ALU.add).then_inc(par, 1)
            dve.wait_ge(lam_e, 1)
            link(tt(sc[:, 5:6], sc[:, 3:4], sc[:, 4:5], ALU.subtract))
            link(ts(sc[:, 0:1], sc[:, 5:6], LAM0, None, ALU.add))
            link(ts(sc[:, 22:23], vv(V_AN), 1.0 - LAM0, None, ALU.mult))
            link(ts(sc[:, 23:24], vv(V_QN), 32 ** -0.5, None, ALU.mult))
            dve.wait_ge(lam_e, 2)
            e, z, z2, q = sc[:, 26:28], sc[:, 28:30], sc[:, 30:32], sc[:, 32:34]
            link(ts(z, e, 2.0, None, ALU.add))
            link(dve.reciprocal(z, z))
            link(tt(z, z, e, ALU.mult))
            link(tt(z2, z, z, ALU.mult))
            link(ts(q, z2, 1.0 / 17, None, ALU.mult))
            for k in range(15, 1, -2):
                link(stt(q, q, 1.0 / k, z2, ALU.add, ALU.mult))
            link(stt(q, q, 1.0, z, ALU.add, ALU.mult))
            link(ts(z, vv(V_LL, 2), 0.0, 8.0, ALU.min, ALU.mult))
            stt(sc[:, 20:22], q, -16.0, z, ALU.mult, ALU.add).then_inc(c_par, 1)

            dve.wait_ge(xsd, 1)
            link(dve.reciprocal(view(kv, 0, T), view(kv, 0, T)))
            for k in range(KT):
                ins = stt(xnv[:, k, :], xraw[:, k, :], vv(V_N1 + k), view(kv, 0, T), ALU.mult, ALU.mult)
            ins.then_inc(xn_ok, 1)
            for i in range(4):
                dve.wait_ge(pj_free, AT[f"AMS{i}"] + 1)
                link(dve.reciprocal(arr[:, i, :], arr[:, i, :]))
                stt(aqk[:, i, :], aqk[:, i, :], sc[:, 23:24] if i < 2 else vv(V_KN), arr[:, i, :], ALU.mult, ALU.mult)\
                   .then_inc(a_ok, 1)

            def causal_max(s):
                i = s % 4
                n = META + P * (i + 1)
                for m in range(2):
                    dve.wait_ge(sco, 2 * s + m + 1)
                    main, nb = ps[:, 4 + m, :], sc[:, 8 + 2 * (s % 2) + m:9 + 2 * (s % 2) + m]
                    k = min(n, 512)
                    last = ps[:, 7, 256 + META * m:256 + META * (m + 1)]
                    link(tt(main[:, n - 144:k], main[:, n - 144:k], cc(C_MASK, k - n + 144), ALU.add))
                    if i < 3:
                        dve.tensor_reduce(nb, main[:, 0:k], X, ALU.max, negate=True).then_inc(smx, 1)
                    else:
                        dve.wait_ge(sco, 2 * s + 2)
                        link(tt(last, last, cc(C_MASK + P, META), ALU.add))
                        dve.tensor_reduce(sc[:, 38:39], main, X, ALU.max, negate=True)
                        link(dve.tensor_reduce(sc[:, 39:40], last, X, ALU.max, negate=True))
                        tt(nb, sc[:, 38:39], sc[:, 39:40], ALU.min).then_inc(smx, 1)

            def combine(s):
                i = s % 4
                n = META + P * (i + 1)
                dve.wait_ge(sexp, 2 * s + 2)
                r = sc[:, 16:18]
                sums = sc[:, 12 + 2 * (s % 2):14 + 2 * (s % 2)]
                if i == 3:
                    link(tt(sums, sums, sc[:, 36:38], ALU.add))
                link(dve.reciprocal(r, sums))
                link(tt(r[:, 1:2], r[:, 1:2], sc[:, 0:1], ALU.mult))
                link(ts(prb[:, s % 2, 1, 0:n], prb[:, s % 2, 1, 0:n], r[:, 1:2], None, ALU.mult))
                stt(prb[:, s % 2, 0, 0:n], prb[:, s % 2, 0, 0:n], r[:, 0:1], prb[:, s % 2, 1, 0:n], ALU.mult, ALU.subtract)\
                   .then_inc(scomb, 1)

            def av_copy(s):
                h, i = s // 4, s % 4
                dve.wait_ge(sav, s + 1)
                if s == 0:
                    dve.wait_ge(zeroed, 16 * (NE + 2 * OVER))
                r = slice(64 * (h % 2), 64 * (h % 2) + 64)
                dve.tensor_copy(brv[r, h // 2, P * i:P * (i + 1)], ps[r, 7, 384:512]).then_inc(sav_ev, 1)

            def rotate(i):
                dve.wait_ge(pj_free, AT[f"ROT{i}"] + 1)
                link(tt(rot[:, i % 2, :], rot[:, i % 2, :], cc(C_SIN, T), ALU.mult))
                link(tt(bqk[:, i, :], bqk[:, i, :], cc(C_COS, T), ALU.mult))
                tt(bqk[:, i, :], bqk[:, i, :], rot[:, i % 2, :], ALU.add).then_inc(rot_ok, 1)

            def conv(t):
                dve.wait_ge(pj_free, AT[f"CX{t}"] + 1)
                dve.wait_ge(c_st, 1)
                dve.wait_ge(kv0, 1)
                w = [vv(V_CW + 2 * k + t) for k in range(4)]
                link(ts(xc[:, t, 0:L], cxv[:, t, 0:L], w[0], vv(V_CB + t), ALU.mult, ALU.add))
                link(ts(xc[:, t, L:T], xxs[:, t, :, 0], w[0], vv(V_CB + t), ALU.mult, ALU.add))
                for k in range(1, 4):
                    link(stt(xc[:, t, 0:L], cxv[:, t, k:k + L], w[k], xc[:, t, 0:L], ALU.mult, ALU.add))
                    ins = stt(xc[:, t, L:T], xxs[:, t, :, k], w[k], xc[:, t, L:T], ALU.mult, ALU.add)
                    if k < 3:
                        link(ins)
                ins.then_inc(conv_ok, 1)

            for s in range(18):
                if s >= 2:
                    av_copy(s - 2)
                if s < 16:
                    causal_max(s)
                if 5 <= s < 9:
                    rotate(s - 5)
                if s in (10, 11):
                    conv(s - 10)
                if s < 16:
                    combine(s)
            dve.wait_ge(la_z, 1)
            stt(dg[:, 0, :], dg[:, 0, :], 0.0, dg[:, 1, :], ALU.min, ALU.subtract).then_inc(la_m, 1)
            for u in range(H * NB):
                h, j = u // NB, u % NB
                rows, t0 = min(P, L - j * P), max(META, j * P)
                dve.wait_ge(at_s, u + 1)
                if u >= 2:
                    dve.wait_ge(at_o, u - 1)
                d0 = C_DT + h * L + t0 - j * P
                tt(atb[0:rows, u % 2, 0:L - t0], ps[0:rows, 4 + u % 2, 0:L - t0], cst[0:rows, d0:d0 + L - t0], ALU.mult)\
                  .then_inc(at_w, 1)
            dve.wait_ge(kt_t, 1)
            for t in range(2):
                dec = view(cst, C_DEC, NB, H)[:, :, 2 * t:2 * t + 2]
                tt(kdv[:, 0:4, t * P:(t + 1) * P].rearrange("p b (h k) -> p b h k", h=2),
                   ps[:, 4 + t, :].rearrange("p (b h k) -> p b h k", b=4, h=2),
                   dec[:, 0:4, :].unsqueeze(3).to_broadcast([P, 4, 2, 64]), ALU.mult)
                ins = tt(kdv[0:TAIL, 4, t * P:(t + 1) * P].rearrange("p (h k) -> p h k", h=2),
                         ps[0:TAIL, 6, t * P:(t + 1) * P].rearrange("p (h k) -> p h k", h=2),
                         dec[0:TAIL, 4, :].unsqueeze(2).to_broadcast([TAIL, 2, 64]), ALU.mult)
            ins.then_inc(kd_ok, 1)
            dve.wait_ge(ld_rs, 16 * (1 + H))
            for t in range(2):
                kb = bqk[:, 2 + t, L:T].unsqueeze(2).to_broadcast([P, DEC, 64])
                link(tt(rv[:, t, :, :], rv[:, t, :, :], kb, ALU.mult))
                ins = stt(rs0[:, t, :, :], rs0[:, t, :, :], cc(C_GAM + t), rv[:, t, :, :], ALU.mult, ALU.add)
            ins.then_inc(rs_ok, 1)
            for t in range(2):
                dve.wait_ge(pj_free, AT[f"BMEAN{t}"] + 1)
                tt(brv[:, 2 + t, :], brv[:, 2 + t, :], bsd[:, t, :], ALU.subtract).then_inc(b_cen, 1)
            for t in range(2):
                dve.wait_ge(pj_free, AT[f"BVAR{t}"] + 1)
                link(dve.reciprocal(bsd[:, t, :], bsd[:, t, :]))
                link(stt(brv[:, 2 + t, :], brv[:, 2 + t, :], vv(V_RN), bsd[:, t, :], ALU.mult, ALU.mult))
                ins = tt(brv[:, 2 + t, :], brv[:, 2 + t, :], bgv[:, t, META:T], ALU.mult)
            ins.then_inc(br_ok, 1)
            dve.wait_ge(c_act, 2)
            link(tt(rr[:, :, :], aa[:, :, :], aa[:, :, :], ALU.mult))
            stt(th[:, :, :], rr[:, :, :], 1.0, th[:, :, :], ALU.add, ALU.mult).then_inc(c_q, 1)
            link(tt(ri[:, :, :], ri[:, :, :], xc[:, :, :], ALU.mult))
            dve.wait_ge(c_act, 3)
            link(tt(ri[:, :, :], ri[:, :, :], rr[:, :, :], ALU.mult))
            for t in range(2):
                dve.tensor_tensor_scan(th[:, t, 0:L], aa[:, t, 0:L], ri[:, t, 0:L], 0.0, ALU.mult, ALU.add)
            link(tt(th[:, :, L:T], aa[:, :, L:T], view(vec, V_ST + 48, 2, DEC), ALU.mult))
            link(tt(th[:, :, L:T], th[:, :, L:T], ri[:, :, L:T], ALU.add))
            tt(brv[:, 4:6, :], th[:, :, META:T], cgv[:, :, META:T], ALU.mult).then_inc(br_ok, 1)
            dve.tensor_copy(cst_out[:, :, 0:1 + DEC], th[:, :, L - 1:T])
            dve.tensor_copy(cst_out[:, :, 9:12], cxv[:, :, L:L + 3])
            dve.tensor_copy(cst_out[:, :, 12:36].rearrange("p t (b i) -> p t b i", b=DEC), xxs[:, :, :, 1:4]).then_inc(c_out, 1)

            dve.wait_ge(ld_q, 16)
            for j in range(2 * DEC):
                b, half = j // 2, j % 2
                ns = HALF + half
                dve.wait_ge(kv_ld[half], (128, 144)[half] * (b + 1))
                kb = kvb[half]
                link(tt(kb, kb, qbc[:, b:b + 1, :].to_broadcast([P, ns, 256]), ALU.mult))
                dve.tensor_reduce(S[:, b, half * HALF:half * HALF + ns, :], kb.rearrange("p s (m d) -> p s m d", d=32),
                                  X, ALU.add).then_inc(k_used, 1)
            dve.wait_ge(k_used, 2 * DEC)
            link(ts(S[:, :, PAGES, :], S[:, :, PAGES, :], cc(C_NEW), None, ALU.add))
            dve.tensor_reduce(mx.rearrange("p (b m) -> p b m", m=8), S.rearrange("p b s m -> p b m s"), X, ALU.max)\
               .then_inc(s_mx, 1)
            dve.wait_ge(s_mxt, 1)
            link(dve.tensor_reduce(mx1, ps[0:64, 4, 0:P], X, ALU.max))
            ts(mxb, cst[0:64, C_ONE:C_ONE + P], mx1, None, ALU.mult).then_inc(s_mx1, 1)
            dve.wait_ge(s_mxm, 1)
            link(dve.tensor_copy(Mb.rearrange("p b m -> p (b m)"), ps[:, 5, 0:64]))
            tt(S, S, Mb.unsqueeze(2).to_broadcast([P, DEC, SLOTS, 8]), ALU.subtract).then_inc(s_sub, 1)
            dve.wait_ge(s_exp, 1)
            dve.tensor_reduce(sm.rearrange("p (b m) -> p b m", m=8), S.rearrange("p b s m -> p b m s"), X, ALU.add)\
               .then_inc(s_sum, 1)
            dve.wait_ge(s_tot, 1)
            rc = Mb
            link(dve.reciprocal(rc.rearrange("p b m -> p (b m)"), ps[:, 5, 64:128]))
            odd = rc.rearrange("p b (h m) -> p (b h) m", m=2)[:, :, 1]
            link(ts(odd, odd, sc[:, 0:1], None, ALU.mult))
            link(tt(S, S, rc.unsqueeze(2).to_broadcast([P, DEC, SLOTS, 8]), ALU.mult))
            Sp = S.rearrange("p b s (h m) -> p (b s h) m", m=2)
            tt(W.rearrange("p b s h -> p (b s h)"), Sp[:, :, 0], Sp[:, :, 1], ALU.subtract).then_inc(s_w, 1)

            qx = dqv[:, META:XT].unsqueeze(1).to_broadcast([P, NV, L])
            kx = dkv.unsqueeze(1).to_broadcast([P, NV, XT])
            dve.wait_ge(ea_ok, 1)

            def gla(j):
                v = vb[:, j % 2, :, :]
                dve.wait_ge(vb_s0, j + 1)
                link(tt(v, v, kx, ALU.mult))
                vf = v.rearrange("p a t -> p (a t)")
                link(dve.tensor_tensor_scan(vf, ea[:, :], vf, 0.0, ALU.mult, ALU.add))
                dve.sem_inc(g_scan, 1)
                if j >= 2:
                    dve.wait_ge(g_mm, j - 1)
                tt(pbv[:, j % 2, :, :], v[:, :, META:XT], qx, ALU.mult).then_inc(g_p, 1)

            def a_norm():
                for t in range(2):
                    dve.wait_ge(pj_free, AT[f"AOS{t}"] + 1)
                    link(dve.reciprocal(osd[:, t, :], osd[:, t, :]))
                    ins = stt(brv[:, t, :], brv[:, t, :], sc[:, 22:23], osd[:, t, :], ALU.mult, ALU.mult)
                ins.then_inc(br_ok, 1)

            for j in range(GROUPS):
                if j == 2:
                    a_norm()
                gla(j)
            dve.wait_ge(pj_free, AT["DOS"] + 1)
            link(dve.reciprocal(osd[:, 0, :], osd[:, 0, :]))
            for g in range(2):
                link(stt(brv[:, 6 + g, :], brv[:, 6 + g, :], vv(V_GN + g), osd[:, 0, :], ALU.mult, ALU.mult))
                ins = tt(brv[:, 6 + g, :], brv[:, 6 + g, :], drv[:, g, META:T], ALU.mult)
            ins.then_inc(br_ok, 1)

            dve.wait_ge(ld_x2, 16 * NB)
            for half in range(2):
                for b in range(NB):
                    dve.wait_ge(wo, half * NB + b + 1)
                    hb = hres[b][:, half * 512:half * 512 + 512]
                    tt(hb, hb, ps[0:RB, (half * NB + b) % 8, :], ALU.add).then_inc(wo_free, 1)
            dve.wait_ge(n2_sd, 1)
            dve.wait_ge(ld_n2, 16)
            link(dve.reciprocal(sc[0:RB, 45:50], sc[0:RB, 45:50]))
            for b in range(NB):
                stt(tk[b], hres[b], sc[0:RB, 45 + b:46 + b], n2row, ALU.mult, ALU.mult).then_inc(t_ok, 1)
            for b in range(NB):
                dve.wait_ge(tt_t, b + 1)
                dve.tensor_copy(tT[:, 4:8, b * RB:(b + 1) * RB],
                                ps[:, 2 * (b % 2) + 1, :].rearrange("p (k n) -> p k n", n=P)[:, :, 0:RB]).then_inc(tt_d, 1)

            dve.wait_ge(lgm, 1)
            R = slice(0, RB)
            l_ = lg[R, :, :]
            link(tt(l_, ps[R, 6, 0:NB * 32].rearrange("p (b n) -> p b n", b=NB)[:, :, 0:20],
                    vec[R, V_RB:V_RB + 20].unsqueeze(1).to_broadcast([RB, NB, 20]), ALU.add))
            r = [rt[R, i, :, :] for i in range(20)]
            one = [rt[R, i, :, 0:1] for i in range(20)]

            def first_of(oh, eq, c):
                link(dve.tensor_copy(oh[:, :, 0:1], eq[:, :, 0:1]))
                link(dve.tensor_copy(c, eq[:, :, 0:1]))
                for i in range(1, 4):
                    link(tt(oh[:, :, i:i + 1], eq[:, :, i:i + 1], c, ALU.is_gt))
                    link(tt(c, c, eq[:, :, i:i + 1], ALU.max))

            gl, le = l_[:, :, 0:4], l_[:, :, 4:20].rearrange("p b (g e) -> p b g e", g=4)
            link(dve.tensor_reduce(one[2], gl, X, ALU.max))
            tt(r[0], gl, one[2].to_broadcast([RB, NB, 4]), ALU.subtract).then_inc(r1, 1)
            link(tt(r[3], gl, one[2].to_broadcast([RB, NB, 4]), ALU.is_equal))
            first_of(r[4], r[3], one[5])
            dve.wait_ge(r2, 1)
            link(dve.tensor_reduce(one[6], r[0], X, ALU.add))
            link(dve.reciprocal(one[6], one[6]))
            ge = f1[R]
            for b in range(NB):
                ins = tt(ge[:, b, :, :], le[:, b, :, :], r[4][:, b, :].unsqueeze(2).to_broadcast([RB, 4, 4]), ALU.mult)
            link(ins)
            link(dve.tensor_reduce(r[7], ge.rearrange("p b g e -> p b e g"), X, ALU.add))
            link(dve.tensor_reduce(one[8], r[7], X, ALU.max))
            link(tt(r[9], r[7], one[8].to_broadcast([RB, NB, 4]), ALU.is_equal))
            first_of(r[10], r[9], one[5])
            link(stt(r[11], r[10], NEG, r[7], ALU.mult, ALU.add))
            link(dve.tensor_reduce(one[12], r[11], X, ALU.max))
            tt(one[1], one[12], one[8], ALU.subtract).then_inc(r1, 1)
            link(tt(r[13], r[11], one[12].to_broadcast([RB, NB, 4]), ALU.is_equal))
            first_of(r[14], r[13], one[5])
            dve.wait_ge(r2, 2)
            link(ts(one[15], one[1], 1.0, None, ALU.add))
            link(dve.reciprocal(one[15], one[15]))
            link(tt(one[15], one[15], one[6], ALU.mult))
            link(tt(one[16], one[15], one[1], ALU.mult))
            for fx, oh in ((f1, r[10]), (f2, r[14])):
                for b in range(NB):
                    ins = tt(fx[R][:, b, :, :], oh[:, b, :].unsqueeze(1).to_broadcast([RB, 4, 4]),
                             r[4][:, b, :].unsqueeze(2).to_broadcast([RB, 4, 4]), ALU.mult)
                link(ins)
            fl = [v[R].rearrange("p b g e -> p b (g e)") for v in (f1, f2, sel, pos)]
            tt(fl[2], fl[0], fl[1], ALU.add).then_inc(sel_ok, 1)
            dve.wait_ge(rank_ok, 1)
            link(dve.tensor_copy(fl[3], ps[R, 4, 0:NB * NE].rearrange("p (b e) -> p b e", b=NB)))
            link(dve.tensor_copy(tot, ps[:, 5, 0:NB * NE].rearrange("p (b e) -> p b e", b=NB)))
            link(dve.tensor_copy(ecnt, tot[:, 0, :]))
            for b in range(1, NB):
                link(tt(fl[3][:, b, :], fl[3][:, b, :], ecnt[R], ALU.add))
                link(tt(ecnt, ecnt, tot[:, b, :], ALU.add))
            link(ts(eov, ecnt, float(P), None, ALU.is_gt))
            for n in range(2, NB):
                link(stt(eov, ecnt, float(n * P), eov, ALU.is_gt, ALU.add))
            link(ts(edel, eov, 1.0, None, ALU.mult))
            link(dve.tensor_tensor_scan(eend, cst[:, C_ONE:C_ONE + NE], edel, 0.0, ALU.mult, ALU.add))
            link(tt(edel, eend, eov, ALU.subtract))
            io = cst[:, C_IO:C_IO + NE]
            link(tt(edel, edel, io, ALU.subtract))
            link(ts(edel, edel, float(P), float((NE - 1) * P), ALU.mult, ALU.add))
            for b in range(NB):
                link(stt(fl[2][:, b, :], fl[3][:, b, :], float(P), edel[R], ALU.is_ge, ALU.mult))
                link(tt(fl[3][:, b, :], fl[3][:, b, :], fl[2][:, b, :], ALU.add))
                link(stt(fl[3][:, b, :], io[R], float(P), fl[3][:, b, :], ALU.mult, ALU.add))
            for n in range(2):
                link(tt(fl[n], fl[n], fl[3], ALU.mult))
                link(dve.tensor_reduce(pos_f[R, 5 * n:5 * n + 5], fl[n], X, ALU.add))
            link(tt(ecmp, eend.unsqueeze(1).to_broadcast([P, OVER, NE]),
                    io[:, 0:OVER].unsqueeze(2).to_broadcast([P, OVER, NE]), ALU.is_le))
            link(dve.tensor_reduce(tab_f[:, 0:OVER], ecmp, X, ALU.add))
            link(ts(tab_f[:, 0:OVER], tab_f[:, 0:OVER], float(NE - 1), None, ALU.min))
            link(dve.tensor_copy(tab_f[:, OVER:OVER + 1], eend[:, NE - 1:NE]))
            link(dve.tensor_copy(itab[R, 0:10], pos_f[R, :]))
            dve.tensor_copy(itab[:, 10:11 + OVER], tab_f).then_inc(idx_ok, 1)

            def h_mult(s):
                return tt(hm[s], si[s], ps[:, 2 + s, 256:512], ALU.mult)

            def hT_copy(s):
                return dve.tensor_copy(hT[s].rearrange("p f n -> p (f n)"), ps[:, 4 + s, 0:256])

            def out_copy(s):
                return dve.tensor_copy(yb[s][:, 1, :], ps[:, 7, :])

            def step(q, s):
                i, o_ = q * 2 + s, 1 - s
                if not (isinstance(i, int) and i == 0):
                    dve.wait_ge(m_ht, i)
                    hT_copy(o_).then_inc(m_htev, 1)
                dve.wait_ge(m_si, i + 1)
                h_mult(s).then_inc(m_h, 1)
                if isinstance(i, int) and i == 0:
                    return
                dve.wait_ge(m_y, i)
                if not (isinstance(i, int) and i < 3):
                    dve.wait_ge(m_yst[o_], q * 16 - (16 if s == 0 else 0))
                out_copy(o_).then_inc(m_yd, 1)

            step(0, 0)
            step(0, 1)
            step(1, 0)
            step(1, 1)
            with dve.Fori(2, PAIRS) as q:
                step(q, 0)
                step(q, 1)
            dve.wait_ge(m_ht, NE)
            hT_copy(1).then_inc(m_htev, 1)
            dve.wait_ge(m_y, NE)
            dve.wait_ge(m_yst[1], 16 * (PAIRS - 1))
            out_copy(1).then_inc(m_yd, 1)

            n_over = dve.value_load(itab[0:1, 10 + OVER:11 + OVER], min_val=0, max_val=OVER)
            with dve.If(n_over > 0):
                dve.wait_ge(m_yst[0], 16 * PAIRS)
                with dve.Fori(0, n_over) as i:
                    dve.wait_ge(o_si, i + 1)
                    h_mult(0).then_inc(o_h, 1)
                    dve.wait_ge(o_ht, i + 1)
                    hT_copy(0).then_inc(o_htev, 1)
                    dve.wait_ge(o_y, i + 1)
                    out_copy(0).then_inc(o_yd, 1)
            for b in range(NB):
                dve.wait_ge(yg[b], 32)
                link(stt(hres[b], y1[b], one[15][:, b, :], hres[b], ALU.mult, ALU.add))
                stt(hres[b], y2[b], one[16][:, b, :], hres[b], ALU.mult, ALU.add).then_inc(y_ok, 1)

        @block.gpsimd
        def _(pool):
            link = Chain(pool, pch)
            pool.memset(cxv[:, :, 0:3], 0.0)
            pool.memset(dqv[:, L:XT:2], 0.0)
            pool.memset(dkv[:, L:XT:2], 1.0)
            pool.memset(dvv[:, :, L:XT:2], 0.0)
            for i in range(NV):
                pool.memset(ea[:, i * XT + L:(i + 1) * XT:2], 0.0)
            pool.memset(kvb[1][:, HALF, :], 0.0).then_inc(kv0, 1)
            zero = br[:, 0:DM]
            pool.memset(zero, 0.0).then_inc(zero_ok, 1)
            pool.wait_ge(zero_ok, 1)
            for i in range(NE + OVER):
                pool.dma_start(scr_x[i * P:(i + 1) * P, :], zero).then_inc(zeroed, 16)
            for i in range(NE, NE + OVER):
                pool.dma_start(scr_y[i * P:(i + 1) * P, :], zero).then_inc(zeroed, 16)
            pool.wait_ge(a_ok, 4)
            pool.dma_start(o["k"], aqk[:, 2:4, :]).then_inc(k_out, 16)
            pool.wait_ge(s_v, 16)
            pool.dma_start(o["v"][0:4 * P, :].rearrange("(b p) c -> p b c", p=P), vt[:, 0:4, 0:256]).then_inc(outs, 16)
            pool.dma_start(o["v"][4 * P:T, :], vt[0:T - 4 * P, 4, 0:256]).then_inc(outs, 16)
            pool.wait_ge(la_e, NV)
            for i in range(NV):
                ins = pool.memset(ea[:, i * XT:i * XT + 1], 0.0)
            ins.then_inc(ea_ok, 1)
            pool.wait_ge(st_ev, 1)
            pool.dma_start(o["ret_p"], rst).then_inc(rst_out, 16)
            pool.wait_ge(rs_ok, 1)
            pool.dma_start(o["ret_s"], rs0).then_inc(rs_out, 16)
            pool.wait_ge(c_out, 1)
            pool.dma_start(o["c"], cst_out).then_inc(outs, 16)

            def merge(i, n, m):
                pool.wait_ge(mg, i + 1)
                p_ = ptv[:, i % 2, :]
                g = sgv[:, m, :] if n == "D" else sgtv[:, i % 2, :]
                if i < KT:
                    pool.tensor_tensor(acc[:, m, :], g, p_, ALU.mult).then_inc(mg_used, 1)
                else:
                    link(pool.tensor_tensor(p_, g, p_, ALU.mult))
                    pool.tensor_tensor(acc[:, m, :], acc[:, m, :], p_, ALU.add).then_inc(mg_used, 1)

            pool.wait_ge(k_out, 16)
            pool.wait_ge(ro_mm, 1)
            for i in range(2 * KT):
                merge(i, "BC"[i // KT], i % KT)
            pool.wait_ge(ld_g0, 16)

            def fill(j):
                pool.wait_ge(vb_ld[j % 2], 64 * (j // 2 + 1))
                pool.tensor_copy(vb[:, j % 2, :, L:XT:2], view(g0, 0, 64, DEC)[:, j * NV:(j + 1) * NV, :]).then_inc(vb_s0, 1)

            def states(j):
                pool.wait_ge(g_scan, j + 1)
                pool.tensor_copy(gst[:, :, j * NV:(j + 1) * NV].rearrange("p n v -> p v n"), vb[:, j % 2, :, L - 1:XT:2])\
                    .then_inc(g_st, 1)

            fill(0)
            fill(1)
            for m in range(KT):
                for q in range(4):
                    j = 4 * m + q
                    states(j)
                    if j + 2 < GROUPS:
                        fill(j + 2)
                    if q == 2:
                        merge(2 * KT + m, "A", m)
            pool.wait_ge(g_st, GROUPS)
            pool.dma_start(o["gla"], gst).then_inc(outs, 16)
            for m in range(KT):
                merge(3 * KT + m, "D", m)
            pool.wait_ge(idx_ok, 1)
            pool.wait_ge(zeroed, 16 * (NE + 2 * OVER))
            for n in range(2):
                for b in range(NB):
                    at = 5 * n + b
                    pool.indirect_dma_start(out=scr_x, out_offset=on_rows(itab[0:RB, at:at + 1]),
                                            in_=tk[b], in_offset=None).then_inc(xs_ok, 16)

            def store(q, s):
                i = q * 2 + s
                pool.wait_ge(m_ya, i + 1)
                pool.wait_ge(m_yd, i + 1)
                dst = scr_y[i * P:(i + 1) * P, :] if isinstance(i, int) else scr_y[bass.ds(i * P, P), :]
                pool.dma_start(dst, yb[s].rearrange("p a n -> p (a n)")).then_inc(m_yst[s], 16)

            with pool.Fori(0, PAIRS) as q:
                store(q, 0)
                store(q, 1)
            for s in range(2):
                pool.wait_ge(m_yst[s], 16 * PAIRS)
            n_over = pool.value_load(itab[0:1, 10 + OVER:11 + OVER], min_val=0, max_val=OVER)
            with pool.If(n_over > 0):
                pool.sem_inc(o_go, 1)
                with pool.Fori(0, n_over) as i:
                    pool.wait_ge(o_ya, i + 1)
                    pool.wait_ge(o_yd, i + 1)
                    pool.dma_start(scr_y[bass.ds(i * P + NE * P, P), :], yb[0].rearrange("p a n -> p (a n)")).then_inc(o_st, 16)
                    pool.wait_ge(o_st, i * 16 + 16)
                    pool.sem_inc(o_go, 1)
            for b in range(NB):
                for n, dst in ((0, y1[b]), (1, y2[b])):
                    at = 5 * n + b
                    pool.indirect_dma_start(out=dst, out_offset=None, in_=scr_y,
                                            in_offset=on_rows(itab[0:RB, at:at + 1])).then_inc(yg[b], 16)
            for stored, n in ((k_out, 1), (rst_out, 1), (rs_out, 1), (outs, POOL_OUTS)):
                pool.wait_ge(stored, 16 * n)



def constants():
    import numpy as np
    c = np.zeros((P, C_W), np.float32)
    p = np.arange(P)
    c[:, C_ID:C_ID + P] = np.eye(P)
    c[p, C_PERM + (p ^ 32)] = 1.0
    c[:, C_B32:C_B32 + P] = (p[:, None] // 32 == p[None] // 32) / 32.0
    c[:, C_B64:C_B64 + P] = (p[:, None] // 64 == p[None] // 64) / 64.0
    c[:, C_ONE:C_ONE + P] = 1.0
    c[p, C_SEL + 31 + 32 * (p // 32)] = 1.0
    inv = (np.float32(10000.0) ** (-np.linspace(0.0, 1.0, 32, dtype=np.float32))).astype(np.float32)
    pos = np.concatenate([np.arange(L), np.full(DEC, PAST)]).astype(np.float32)
    ang = (pos[None, :] * inv[p % 32][:, None]).astype(np.float32)
    c[:, C_COS:C_COS + T] = np.cos(ang)
    c[:, C_SIN:C_SIN + T] = np.where(p[:, None] % 64 < 32, -np.sin(ang), np.sin(ang))
    lgam = np.log(1.0 - 2.0 ** (-5.0 - np.arange(H)))
    x = np.arange(L)
    for h in range(H):
        rel = x[None, :] - p[:, None]
        c[:, C_DT + h * L:C_DT + (h + 1) * L] = np.where(rel >= 0, np.exp(np.maximum(rel, 0) * lgam[h]), 0.0)
    q = np.arange(144)
    c[:, C_MASK:C_MASK + 144] = np.where(q[None, :] <= p[:, None] + META, 0.0, NEG)
    for b in range(NB):
        for h in range(H):
            at = np.minimum(b * P + p, L - 1)
            c[:, C_DEC + b * H + h] = np.exp((L - 1 - at) * lgam[h])
    for t in range(2):
        c[:, C_GAM + t] = np.exp(lgam[2 * t + p // 64])
    c[1:, C_NEW] = NEG
    c[:, C_EPS] = EPS
    c[:, C_LT:C_LT + P] = p[:, None] < p[None]
    c[:, C_IO:C_IO + NE] = np.arange(NE)
    return c


_OUT = {"y": (N, DM), "k": (P, 2, T), "v": (T, 256), "ret_p": (64, H, 64), "ret_s": (P, 2, DEC, 64),
        "c": (P, 2, 36), "gla": (P, 1 + DEC, 64)}


def kernel(**inputs):
    import numpy as np
    import concourse.bacc as bacc
    from concourse.bass_utils import run_bass_kernel_spmd as run

    a = {k: np.asarray(v) for k, v in inputs.items()}

    def cols(v):
        return np.ascontiguousarray(v.reshape(-1, P).T)

    def tiles(w):
        return w.reshape(KT, P, -1).transpose(1, 0, 2)

    w = a["w_in"][0]
    cut = np.cumsum([0, 256, 256, 256, 256, 256, 256, 256, 256, 256, 128, 128, 256, 256, 16])
    aq, ak, av, bq, bk, bv, bg_, cx_, cg_, dq, dk, dv_, dr_, da = [w[:, i:j] for i, j in zip(cut[:-1], cut[1:])]
    dr_ = dr_.reshape(DM, H, 2, 32).transpose(0, 2, 1, 3).reshape(DM, 256)
    w_in = np.concatenate([aq, ak, av, bv, bq, bk, bg_, cx_, cg_, dq, dk, dv_, dr_], 1)
    w_in = w_in.reshape(KT, P, N_IN, P).transpose(2, 1, 0, 3).reshape(N_IN, P, 1024)
    wb = a["w_branch"][0].copy()
    wb = np.stack([wb[0], wb[1], wb[2], wb[3].reshape(H, 2, 32, DM).transpose(1, 0, 2, 3).reshape(256, DM)])
    wm = a["w_merge"][0].reshape(KT, P, 4, KT, P).transpose(2, 3, 1, 0, 4)
    wbt = wb.reshape(4, 2, P, KT, P).transpose(0, 3, 2, 1, 4)
    both = np.concatenate([wm.reshape(4, KT, P, 1024), wbt.reshape(4, KT, P, 256)], 3)
    w_mg = np.concatenate([both["ABCD".index(n)] for n in "BCDA"])
    w_dp = wbt[3].reshape(2, 4, P, 256).transpose(0, 2, 1, 3).reshape(2, P, 1024)
    w_out = a["w_out"][0].reshape(4, 2, P, 2, 512).transpose(3, 0, 2, 1, 4).reshape(8, P, 1024)
    w_13 = np.concatenate([a["ex_w1"][0].reshape(NE, KT, P, 256), a["ex_w3"][0].reshape(NE, KT, P, 256)], 3).transpose(0, 2, 1, 3)
    w_2 = a["ex_w2"][0].reshape(NE, 2, P, DM).transpose(0, 2, 1, 3)

    x = np.concatenate([a["meta"], a["x_prompt"][0], a["x_sample"][:, 0]], 0)
    xT = x.T.reshape(KT, P, T).transpose(1, 0, 2)

    v = np.zeros((P, V_W), np.float32)
    v[:, V_N1:V_N1 + 8], v[:, V_N2:V_N2 + 8] = cols(a["norm1"][0]), cols(a["norm2"][0])
    v[:, V_QN], v[:, V_KN] = np.tile(a["qn"][0], 4), np.tile(a["kn"][0], 4)
    v[:, V_AN], v[:, V_RN] = np.tile(a["an"][0], 2), np.tile(a["rn"][0], 2)
    v[:, V_GN], v[:, V_GN + 1] = np.tile(a["gn"][0][:32], 4), np.tile(a["gn"][0][32:], 4)
    for k in range(4):
        v[:, V_CW + 2 * k:V_CW + 2 * k + 2] = cols(a["conv_w"][0, k])
    for at, name in ((V_CB, "conv_b"), (V_BA, "lru_ba"), (V_BX, "lru_bx"), (V_LL, "lru_lam")):
        v[:, at:at + 2] = cols(a[name][0])
    v[:, V_GB] = a["gla_b"][0]
    v[:, V_BM:V_BM + 32] = cols(a["b_merge"][0])
    v[:, V_RB:V_RB + 4], v[:, V_RB + 4:V_RB + 20] = a["rg_b"][0], a["re_b"][0]
    v[:, V_LAM:V_LAM + 128] = a["lam"][0].reshape(-1)
    v[:, V_ST:V_ST + 48] = a["state_lru_conv"][0].transpose(2, 0, 1).reshape(2, P, 24).transpose(1, 0, 2).reshape(P, 48)
    v[:, V_ST + 48:V_ST + 64] = a["state_lru_h"][0].T.reshape(2, P, DEC).transpose(1, 0, 2).reshape(P, 16)
    for at, name in ((V_WA, "lru_wa"), (V_WX, "lru_wx")):
        for h in range(H):
            r = 64 * (h % 2)
            v[r:r + 64, at + P * (h // 2) + r:at + P * (h // 2) + r + 64] = a[name][0, h]
    v[:, V_RW:V_RW + 160] = tiles(np.concatenate([a["rg_w"][0], a["re_w"][0]], 1)).reshape(P, 160)
    v[:, V_DA:V_DA + 128] = tiles(da).reshape(P, 128)
    v[0:16, V_G2:V_G2 + 128] = a["gla_w2"][0]

    ret0 = a["state_ret"][0].reshape(DEC, 2, P, 64).transpose(2, 1, 0, 3)
    gla0 = a["state_gla"][0].reshape(DEC, P, 64).transpose(1, 2, 0).reshape(P, 512)
    kcache = a["cache_k_a"][0].reshape(-1, PAGE, 256)
    vcache = a["cache_v_a"][0].reshape(-1, PAGE, 256)
    pt = a["page_table"].reshape(1, -1)

    nc = bacc.Bacc("TRN2", target_bir_lowering=False, num_devices=1)
    arrays, args = {}, []
    for name, arr in (("w_in", w_in), ("w_mg", w_mg), ("w_dp", w_dp), ("w_out", w_out), ("w_13", w_13), ("w_2", w_2),
                      ("x", x[META:]), ("n2", a["norm2"]), ("xT", xT),
                      ("const", constants()), ("vec", v), ("ret0", ret0), ("gla0", gla0), ("kc", kcache),
                      ("vc", vcache), ("pt", pt)):
        arr = np.ascontiguousarray(arr)
        arrays["in_" + name] = arr
        args.append(nc.dram_tensor("in_" + name, arr.shape, mybir.dt.from_np(arr.dtype), kind="ExternalInput").ap())
    o = {k: nc.dram_tensor("out_" + k, s, F32, kind="ExternalOutput").ap() for k, s in _OUT.items()}
    program(nc, *args, o)
    res = run(nc, [arrays], core_ids=[0]).results[0]
    r = {k: np.asarray(res["out_" + k]).reshape(s) for k, s in _OUT.items()}

    y = r["y"]
    k = r["k"].transpose(2, 1, 0).reshape(T, H, 64)
    vv_ = r["v"].reshape(T, H, 64)
    c = r["c"].transpose(1, 0, 2).reshape(256, 36)
    g = r["gla"]
    rs = r["ret_s"].reshape(2, 64, 2, DEC, 64).transpose(3, 2, 0, 1, 4).reshape(DEC, H, 64, 64)
    outs = (y[:SEQ][None], y[SEQ:][:, None], k[:L][None, None], vv_[:L][None, None],
            r["ret_p"].transpose(1, 0, 2)[None, None], c[:, 0][None, None], c[:, 9:12].T[None, None],
            g[:, 0].reshape(H, 32, 64)[None, None],
            k[L:][None, :, None], vv_[L:][None, :, None], rs[None], c[:, 1:9].T[None],
            c[:, 12:36].reshape(256, DEC, 3).transpose(1, 2, 0)[None],
            g[:, 1:].transpose(1, 0, 2).reshape(DEC, H, 32, 64)[None])
    return tuple(np.ascontiguousarray(t) for t in outs)
```

```python
from contextlib import ExitStack

import concourse.bass as bass
from concourse import mybir

F32 = mybir.dt.float32
I32 = mybir.dt.int32
ALU = mybir.AluOpType
ACT = mybir.ActivationFunctionType
X = mybir.AxisListType.X

P = 128
DM = 1024
KT = DM // P
META, SEQ, DEC = 16, 512, 8
L = META + SEQ
T = L + DEC
HT = T // 2
N = SEQ + DEC
HN = N // 2
NB = 5
TAIL = L - 4 * P
H = 4
PAST, PAGE = 2048, 128
PAGES = PAST // PAGE
HALF = PAGES // 2
SLOTS = PAGES + 1
XT = L + 2 * DEC
NV = 2
GROUPS = 64 // NV
VR = 4
NE = 16
PAIRS = NE // 2
DEEP = 4
OVER = 8
ROWS = (NE + OVER) * P
RB = N // NB
WCH = 1280
RING = 6
EPS = 1e-6
LAM0 = 0.8 - 0.6
NEG = -1.0e30

C_ID, C_PERM, C_B32, C_B64, C_ONE = 0, 128, 256, 384, 512
C_SEL = 640
C_COS = C_SEL + 159
C_SIN = C_COS + T
C_DT = C_SIN + T
C_MASK = C_DT + H * L
C_DEC = C_MASK + 144
C_GAM = C_DEC + NB * H
C_NEW = C_GAM + 2
C_EPS = C_NEW + 1
C_LT = C_EPS + 1
C_IO = C_LT + P
C_W = C_IO + 16

V_N1, V_QN, V_KN, V_AN, V_RN, V_GN = 0, 16, 17, 18, 19, 20
V_CW, V_CB, V_BA, V_BX, V_LL, V_GB, V_BM, V_RB = 22, 30, 32, 34, 36, 38, 39, 71
V_LAM, V_ST = 91, 219
V_WA = V_ST + 64
V_WX = V_WA + 256
V_RW = V_WX + 256
V_DA = V_RW + 160
V_G2 = V_DA + 128
V_W = V_G2 + 128

PROJ = (["AQ0", "AQ1", "AK0", "AK1", "V0", "AMS0", "AMS1", "AMS2", "AMS3", "V1",
         "BQ0", "BQ1", "BK0", "BK1", "BG0", "BG1", "V2", "ROT0", "V3", "ROT1", "CX0", "ROT2", "CX1", "ROT3", "CG0", "CG1", "DQ", "DK", "DV0", "DV1", "DR0", "DR1", "DA", "LA"]
        + ["BMEAN0", "BMEAN1", "BVAR0", "BVAR1", "CR0", "CR1", "CI0", "CI1"]
        + [f"{k}{n}{m}" for n in "BC" for m in range(KT) for k in "GP"]
        + ["GA0", "AOS0", "AOS1", "GA1", "PA0", "PA1"] + [f"{k}A{m}" for m in range(2, KT) for k in "GP"]
        + [f"GD{m}" for m in range(4)] + ["DOS"] + [f"GD{m}" for m in range(4, KT)] + [f"PD{m}" for m in range(KT)])
AT = {name: i for i, name in enumerate(PROJ)}
STEPS = [name for name in PROJ[AT["BK0"]:AT["LA"] + 1] if not name.startswith("ROT")]
CHUNKS = ["AQ0", "AQ1", "AK0", "AK1", "V0", "V1", "BQ0", "BQ1", "BK0", "BK1",
          "BG0", "BG1", "V2", "V3", "CX0", "CX1", "CG0", "CG1", "DQ", "DK", "DV0", "DV1", "DR0", "DR1"]
N_IN = len(CHUNKS)
MERGES = [f"G{n}{m}" for n in "BCAD" for m in range(KT)]
ORDER = [(n, m) for n in "BCA" for m in range(KT)]
HALVES = [0, 0] + [1] * 6 + [2] * 3 + [1] * 4 + [0] * 9
SCANS = [0, 0] + [1] * 6 + [2] * 10 + [1] * 6
BR = {"A": 0, "B": 2, "C": 4, "D": 6}
CH = CHUNKS + MERGES + ["DP0", "DP1"] + [f"WO{m}" for m in range(KT)]
CAT = {name: i for i, name in enumerate(CH)}


def program(nc, w_in, w_mg, w_dp, w_out, w_13, w_2, x_d, n2_d, xT_d, const_d, vec_d, ret0_d, gla0_d, kc, vc, pt, o):
    with ExitStack() as ctx:
        def sb(name, cols, dt=F32):
            return ctx.enter_context(nc.sbuf_tensor(name, [P, cols], dt))

        def sem(name):
            return ctx.enter_context(nc.semaphore(name))

        def scratch(name, shape):
            return nc.dram_tensor(name, shape, F32, kind="Internal").ap()

        scr_qk = scratch("scr_qk", (DEC, 512))
        scr_v = scratch("scr_v", (DEC, 512))
        scr_dv = scratch("scr_dv", (256, XT))
        scr_x = scratch("scr_x", (ROWS, DM))
        scr_y = scratch("scr_y", (ROWS, DM))

        cst = sb("cst", C_W)
        vec = sb("vec", V_W)
        xn = sb("xn", KT * T)
        ring = sb("ring", RING * WCH)
        sgd = sb("sgd", KT * N)
        qk = sb("qk", 8 * T)
        bg, cg, dr = sb("bg", 2 * T), sb("cg", 2 * T), sb("dr", 2 * T)
        cx = sb("cx", 2 * (L + 3))
        dqk = sb("dqk", 2 * XT)
        dv = sb("dv", 2 * XT)
        ea = sb("ea", NV * XT)
        vtok = sb("vtok", NB * 512)
        br = sb("br", 8 * N)
        kv = sb("kv", SLOTS * 256)
        tmp = sb("tmp", 4288)
        qb = sb("qb", 2144)
        sgt = sb("sgt", 2 * N)
        g0 = sb("g0", 512)
        small = sb("small", 200)
        pts = ctx.enter_context(nc.sbuf_tensor("pts", [1, DEC * PAGES], I32))
        itab = ctx.enter_context(nc.sbuf_tensor("itab", [P, 10 + OVER + 1], I32))
        ps = ctx.enter_context(nc.psum_tensor("ps", [P, 8, 512], F32))

        def cc(at, n=1, rows=slice(0, P)):
            return cst[rows, at:at + n]

        def vv(at, n=1, rows=slice(0, P)):
            return vec[rows, at:at + n]

        def view(t, off, *dims):
            n = 1
            for d in dims:
                n *= d
            a = t[:, off:off + n]
            if len(dims) == 1:
                return a
            names = "abcd"[:len(dims)]
            return a.rearrange(f"p ({' '.join(names)}) -> p {' '.join(names)}", **dict(zip(names[1:], dims[1:])))

        ident = cc(C_ID, P)
        xnv, xraw = view(xn, 0, KT, T), view(tmp, 0, KT, T)
        aqk, bqk = view(qk, 0, 4, T), view(qk, 4 * T, 4, T)
        acc = view(qk, 0, KT, N)
        bgv, cgv, drv = view(bg, 0, 2, T), view(cg, 0, 2, T), view(dr, 0, 2, T)
        cxv = view(cx, 0, 2, L + 3)
        dqv, dkv = dqk[:, 0:XT], dqk[:, XT:2 * XT]
        dvv = view(dv, 0, 2, XT)
        gst = view(dv, 0, 1 + DEC, 64)
        vt = view(vtok, 0, NB, 512)
        brv = view(br, 0, 8, N)
        sgv, sgtv = view(sgd, 0, KT, N), view(sgt, 0, 2, N)
        ptv = view(cst, C_COS, 2, N)
        kvv = view(kv, 0, SLOTS, 256)
        kvb = [kvv[:, 0:HALF, :], kvv[:, HALF:SLOTS, :]]
        asq, arr = view(tmp, 0, 4, T), view(tmp, 4 * T, 4, T)
        prb = view(tmp, 0, 2, 2, L)
        wtb = view(tmp, 4 * L, 2, NB, P)
        rot = view(qb, 0, 2, T)
        xc = view(qb, 2 * T, 2, T)
        atb = view(tmp, 0, 2, 512)
        kdv = view(tmp, 1024, NB, 256)
        rv = view(tmp, 2304, 2, DEC, 64)
        rs0 = view(qb, 0, 2, DEC, 64)
        rst = br[0:64, 7 * N:7 * N + 256].rearrange("p (h v) -> p h v", h=H)
        bn, bsd = view(tmp, 0, 2, N), view(sgt, 0, 2, N)
        osq, osd = view(kv, 0, 2, N), view(kv, 2 * N, 2, N)
        rr, ri = view(tmp, 0, 2, T), view(tmp, 2 * T, 2, T)
        aa, th = view(tmp, 4 * T, 2, T), view(tmp, 6 * T, 2, T)
        xxs = view(small, 0, 2, DEC, 4)
        cst_out = view(small, 64, 2, 36)
        sc = small[:, 136:200]
        qbc = view(sgd, 0, DEC, 256)
        S = view(sgd, 2048, DEC, SLOTS, 8)
        mx, sm, Mb = view(sgd, 3136, 64), view(sgd, 3200, 64), view(sgd, 3264, DEC, 8)
        mxb, mx1 = sgd[0:64, 3328:3456], sgd[0:64, 3456:3457]
        srow = sgd[0:H, 0:DEC * 256].rearrange("h (b c) -> h b c", b=DEC)
        W = view(cst, C_DT, DEC, SLOTS, 4)
        qk8 = sgt[0:DEC, 0:512]
        ones, eps0 = qb[:, 0:P], sc[:, 60:61]
        vb = [view(t, i * NV * XT, NV, XT) for t in (tmp, vtok) for i in range(2)]
        pbv = view(tmp, 2 * NV * XT, 2, NV, L)
        dg = view(br, 4 * N, 2, T)
        das = sgt[0:16, 0:T]
        hres = [view(tmp, b * DM, DM)[0:RB] for b in range(4)] + [bg[0:RB, 0:DM]]
        tk = [view(xn, b * DM, DM)[0:RB] for b in range(4)] + [cg[0:RB, 0:DM]]
        tT = view(qk, 0, KT, N)
        n2row = dqk[0:RB, 0:DM]
        lg = view(ea, 0, NB, 20)
        rt = view(ea, 100, 20, NB, 4)
        f1, f2, sel, pos = [view(dr, 80 * i, NB, 4, 4) for i in range(4)]
        tot = view(dr, 320, NB, NE)
        ecnt, eov, eend, edel = [view(dr, 400 + 16 * i, NE) for i in range(4)]
        ecmp = view(dr, 464, OVER, NE)
        pos_f, tab_f = view(dr, 600, 10), view(dr, 610, OVER + 1)
        w13b = [view(t, 0, KT, 512) for t in (kv, br, qk, xn)]
        w2b = [view(sgd, 0, 2, DM), view(sgd, 2 * DM, 2, DM), view(qb, 0, 2, DM), view(vtok, 0, 2, DM)]
        xe = [view(ring, DM * i, DM) for i in range(2)]
        xeT = [view(ring, 2 * DM + DM * i, KT, P) for i in range(2)]
        yb = [view(ring, 4 * DM + DM * i, 2, 512) for i in range(2)]
        si = [view(ring, 6 * DM + 256 * i, 256) for i in range(2)]
        hm = [view(ring, 6 * DM + 512 + 256 * i, 256) for i in range(2)]
        hT = [view(cx, 256 * i, 2, P) for i in range(2)]
        y1 = [view(kv, b * DM, DM)[0:RB] for b in range(4)] + [view(xn, 0, DM)[0:RB]]
        y2 = [view(br, b * DM, DM)[0:RB] for b in range(4)] + [view(xn, DM, DM)[0:RB]]

        w_ld = [sem(f"w_ld{i}") for i in range(RING)]
        ld_x, init_ok = [sem("ld_x0"), sem("ld_x1")], sem("init_ok")
        ld_c, ld_v, ld_s = sem("ld_c"), sem("ld_v"), sem("ld_s")
        ld_rs, ld_q = sem("ld_rs"), sem("ld_q")
        x_sq = sem("x_sq")
        xms, xsd, xn_ok = sem("xms"), sem("xsd"), sem("xn_ok")
        pj, pj_free = sem("pj"), sem("pj_free")
        a_sq, a_ok = sem("a_sq"), sem("a_ok")
        t8, t8_ev, s_qk, s_v = sem("t8"), sem("t8_ev"), sem("s_qk"), sem("s_v")
        sco, smx, sexp, scomb = sem("sco"), sem("smx"), sem("sexp"), sem("scomb")
        swt, swt_ev, sav, sav_ev = sem("swt"), sem("swt_ev"), sem("sav"), sem("sav_ev")
        rot_ok, conv_ok = sem("rot_ok"), sem("conv_ok")
        at_s, at_w, at_o, ob_ev = sem("at_s"), sem("at_w"), sem("at_o"), sem("ob_ev")
        kt_t, kd_ok, st_mm, st_ev = sem("kt_t"), sem("kd_ok"), sem("st_mm"), sem("st_ev")
        rs_ok, ro_mm, b_raw = sem("rs_ok"), sem("ro_mm"), sem("b_raw")
        b_cen, b_sq, br_ok = sem("b_cen"), sem("b_sq"), sem("br_ok")
        c_par, c_act, c_q, c_out = sem("c_par"), sem("c_act"), sem("c_q"), sem("c_out")
        mg, mg_used = sem("mg"), sem("mg_used")
        kv_ld = [sem("kv_ld0"), sem("kv_ld1")]
        k_used, v_used = sem("k_used"), sem("v_used")
        s_mx, s_mxt, s_mx1, s_mxm, s_sub, s_exp, s_sum, s_tot, s_w = [sem(f"smp{i}") for i in range(9)]
        a_raw, a_osq, sr_ok, s_av = sem("a_raw"), sem("a_osq"), sem("sr_ok"), sem("s_av")
        la_z, la_e, la_m, s_dv = sem("la_z"), sem("la_e"), sem("la_m"), sem("s_dv")
        vb_ld = [sem(f"vb_ld{i}") for i in range(VR)]
        vb_s0, g_scan, g_st, g_p, g_mm = sem("vb_s0"), sem("g_scan"), sem("g_st"), sem("g_p"), sem("g_mm")
        d_raw, d_sq = sem("d_raw"), sem("d_sq")
        wo, wo_free, ld_x2 = sem("wo"), sem("wo_free"), sem("ld_x2")
        wo_rd = [sem("wo_rd0"), sem("wo_rd1")]
        y_out, n2_sd, t_ok = sem("y_out"), sem("n2_sd"), sem("t_ok")
        tt_t, tt_a, tt_d, lgm = sem("tt_t"), sem("tt_a"), sem("tt_d"), sem("lgm")
        r1, r2, sel_ok, rank_ok, idx_ok = sem("r1"), sem("r2"), sem("sel_ok"), sem("rank_ok"), sem("idx_ok")
        zeroed, xs_ok = sem("zeroed"), sem("xs_ok")
        m_w = [sem(f"m_w{i}") for i in range(DEEP)]
        m_xe, m_yst = [sem("m_xe0"), sem("m_xe1")], [sem("m_yst0"), sem("m_yst1")]
        m_t, m_tev, m_h1, m_si, m_h = sem("m_t"), sem("m_tev"), sem("m_h1"), sem("m_si"), sem("m_h")
        m_ht, m_htev, m_y, m_ya, m_yd = sem("m_ht"), sem("m_htev"), sem("m_y"), sem("m_ya"), sem("m_yd")
        o_go, o_ld, o_t, o_tev, o_h1 = sem("o_go"), sem("o_ld"), sem("o_t"), sem("o_tev"), sem("o_h1")
        o_si, o_h, o_ht, o_htev, o_y, o_ya, o_yd, o_st = [sem(f"o_{k}") for k in ("si", "h", "ht", "htev", "y", "ya", "yd", "st")]
        yg, y_ok = [sem(f"yg{b}") for b in range(NB)], sem("y_ok")
        dch, ach, pch, outs = sem("dch"), sem("ach"), sem("pch"), sem("outs")
        kv0, ea_ok, rst_out, rs_out = sem("kv0"), sem("ea_ok"), sem("rst_out"), sem("rs_out")
        kv_out, par, lam_e, c_st = sem("kv_out"), sem("par"), sem("lam_e"), sem("c_st")
        block = ctx.enter_context(nc.Block())

        def on_rows(idx):
            return bass.IndirectOffsetOnAxis(ap=idx, axis=0)

        class Chain:
            def __init__(self, eng, s):
                self.eng, self.s, self.n = eng, s, 0

            def __call__(self, ins):
                self.n += 1
                ins.then_inc(self.s, 1)
                self.eng.wait_ge(self.s, self.n)

        def bank2(pair, w, base=0):
            return ps[:, 2 * pair + base:2 * pair + base + 2, 0:w]

        def fold(a, w):
            return a.rearrange("p (a b) -> p a b", a=2)

        POOL_OUTS = 2

        @block.sync
        def _(sp):
            def reader_done(c):
                name = CH[c]
                if name in MERGES and name[1] != "D":
                    sp.wait_ge(pj, AT["P" + name[1:]] + 1)
                elif name.startswith("DP"):
                    sp.wait_ge(pj, AT[f"PD{4 * int(name[2]) + 3}"] + 1)
                elif name.startswith("WO"):
                    sp.wait_ge(wo_rd[int(name[2])], 1)
                else:
                    sp.wait_ge(pj, AT[name] + 1)

            def chunk(c):
                name = CH[c]
                if c >= RING:
                    reader_done(c - RING)
                if name in CHUNKS:
                    src, n = w_in[c], 1024
                elif name in MERGES:
                    src, n = w_mg[c - N_IN], 1280
                elif name.startswith("DP"):
                    src, n = w_dp[int(name[2])], 1024
                else:
                    src, n = w_out[int(name[2])], 1024
                s = c % RING
                sp.dma_start(ring[:, s * WCH:s * WCH + n], src).then_inc(w_ld[s], 16)

            def cache(j):
                b, half, is_v = j % 16 // 2, j % 2, j // 16
                pages = [sp.value_load(pts[0:1, at:at + 1], min_val=0, max_val=kc.shape[0] - 1)
                         for at in range(b * PAGES + half * HALF, b * PAGES + half * HALF + HALF)]
                if j >= 2:
                    i = j - 2
                    sp.wait_ge(*((k_used, i + 1) if i < 16 else (v_used, i - 15)))
                src = vc if is_v else kc
                for g, page in enumerate(pages):
                    sp.dma_start(kvb[half][:, g, :], src[bass.ds(page, 1), :, :].rearrange("a p c -> (a p) c"))\
                      .then_inc(kv_ld[half], 16)
                if half:
                    row = scr_v[b:b + 1, 0:256] if is_v else scr_qk[b:b + 1, 256:512]
                    sp.dma_start(kvb[1][0:1, HALF, :], row).then_inc(kv_ld[1], 16)

            def values(j):
                if j >= VR:
                    sp.wait_ge(g_p, j - VR + 1)
                    sp.wait_ge(g_st, j - VR + 1)
                for h in range(H):
                    src = scr_dv[h * 64 + j * NV:h * 64 + (j + 1) * NV, :]
                    sp.dma_start(vb[j % VR][32 * h:32 * h + 32, :, :], src.partition_broadcast(32))\
                      .then_inc(vb_ld[j % VR], 16)

            for i in range(2):
                half = slice(i * KT // 2, (i + 1) * KT // 2)
                sp.dma_start(xraw[:, half, :], xT_d[:, half, :]).then_inc(ld_x[i], 16)
            chunk(0)
            chunk(1)
            sp.dma_start(cst[:, :], const_d).then_inc(ld_c, 16)
            for c in range(2, RING):
                chunk(c)
            sp.dma_start(pts[0:1, :], pt).then_inc(ld_s, 16)
            sp.dma_start(g0[:, :], gla0_d).then_inc(ld_s, 16)
            def chunks_to(c, end):
                for i in range(c, end):
                    chunk(i)
                return end

            c = chunks_to(RING, CAT["AK0"] + RING)
            sp.wait_ge(xn_ok, KT)
            sp.wait_ge(kv0, 1)
            sp.wait_ge(ld_s, 32) 
            cache(0)
            c = chunks_to(c, CAT["BQ1"] + RING)
            sp.wait_ge(s_qk, 16)
            sp.dma_start(qbc, scr_qk[:, 0:256].partition_broadcast(P)).then_inc(ld_q, 16)
            cache(1)
            for j in range(2, 16):
                end = c
                while AT[CH[end - RING]] <= AT[STEPS[j - 2]]:
                    end += 1
                c = chunks_to(c, end)
                cache(j)
                if j == 10:
                    sp.wait_ge(rot_ok, 4)
                    sp.dma_start(rs0, ret0_d).then_inc(ld_rs, 16)
            c = chunks_to(c, CAT["GB0"] + RING)
            sp.wait_ge(s_v, 16)
            cache(16)
            cache(17)
            sp.wait_ge(sav, 16)
            for h in range(H):
                sp.dma_start(rv[64 * (h % 2):64 * (h % 2) + 64, h // 2, :, :],
                             scr_v[:, 256 + h * 64:256 + h * 64 + 64].partition_broadcast(64)).then_inc(ld_rs, 16)
            sp.wait_ge(s_dv, 16)
            sp.wait_ge(br_ok, 2)
            sp.wait_ge(st_ev, 1)
            sp.wait_ge(kv_out, 48)
            for j in range(VR):
                values(j)
            jk, jv = 18, VR
            for halves, scans in zip(HALVES, SCANS):
                for _ in range(scans):
                    if jv < GROUPS:
                        values(jv)
                        jv += 1
                for _ in range(halves):
                    if jk < 32:
                        cache(jk)
                        jk += 1
                c = chunks_to(c, c + 1)
            chunks_to(c, len(CH))
            sp.wait_ge(g_mm, GROUPS)
            for b in range(NB):
                sp.dma_start(hres[b], x_d[b * RB:(b + 1) * RB, :]).then_inc(ld_x2, 16)
            sp.dma_start(n2row, n2_d.partition_broadcast(RB).rearrange("p a n -> p (a n)")).then_inc(ld_x2, 16)

            def expert(i, w):
                w1, w2 = (w_13[i], w_2[i]) if isinstance(i, int) else \
                    [m[bass.ds(i, 1), :, :, :].rearrange("a p k n -> (a p) k n") for m in (w_13, w_2)]
                sp.dma_start(w13b[w], w1).then_inc(m_w[w], 16)
                sp.dma_start(w2b[w], w2).then_inc(m_w[w], 16)

            def rows(i, s):
                src = scr_x[i * P:(i + 1) * P, :] if isinstance(i, int) else scr_x[bass.ds(i * P, P), :]
                sp.dma_start(xe[s], src).then_inc(m_xe[s], 16)

            sp.wait_ge(br_ok, 4)
            sp.wait_ge(rs_out, 16)
            sp.wait_ge(mg_used, 4 * KT)
            expert(0, 0)
            expert(1, 1)
            sp.wait_ge(lgm, 1)
            expert(2, 2)
            sp.wait_ge(xs_ok, 16 * 2 * NB)
            rows(0, 0)
            rows(1, 1)
            expert(3, 3)
            sp.wait_ge(m_t, 1)
            rows(2, 0)
            with sp.Fori(1, NE // DEEP) as q:
                for w in range(DEEP):
                    sp.wait_ge(m_t, q * DEEP + (w - 2))
                    rows(q * DEEP + (w - 1), (w - 1) % 2)
                    sp.wait_ge(m_y, q * DEEP + (w - DEEP + 1))
                    expert(q * DEEP + w, w)
            sp.wait_ge(m_t, NE - 2)
            rows(NE - 1, 1)
            sp.wait_ge(idx_ok, 1)
            n_over = sp.value_load(itab[0:1, 10 + OVER:11 + OVER], min_val=0, max_val=OVER)
            with sp.If(n_over > 0):
                sp.wait_ge(m_h1, NE)
                sp.wait_ge(m_y, NE)
                sp.wait_ge(m_t, NE)
                with sp.Fori(0, n_over) as i:
                    sp.wait_ge(o_go, i + 1)
                    e = sp.value_load(itab[0:1, bass.ds(i + 10, 1)], min_val=0, max_val=NE - 1)
                    sp.dma_start(w13b[0], w_13[bass.ds(e, 1), :, :, :].rearrange("a p k n -> (a p) k n")).then_inc(o_ld, 16)
                    sp.dma_start(w2b[0], w_2[bass.ds(e, 1), :, :, :].rearrange("a p k n -> (a p) k n")).then_inc(o_ld, 16)
                    sp.dma_start(xe[0], scr_x[bass.ds(i * P + NE * P, P), :]).then_inc(o_ld, 16)
            for b in range(NB):
                sp.wait_ge(y_ok, b + 1)
                sp.dma_start(o["y"][b * RB:(b + 1) * RB, :], hres[b]).then_inc(y_out, 16)
            sp.wait_ge(y_out, 16 * NB)

        @block.tensor
        def _(pe):
            def loaded(c):
                pe.wait_ge(w_ld[c % RING], 16 * (c // RING + 1))

            def wsl(c, k, n=P):
                s = c % RING * WCH
                return ring[:, s + k * P:s + k * P + n]

            def free(t):
                if t >= 2:
                    pe.wait_ge(pj_free, t - 1)

            def stat(name, lhsT, srcs, hw):
                t = AT[name]
                free(t)
                for h in range(2):
                    for i, s in enumerate(srcs):
                        mm = pe.matmul(ps[:, 2 * (t % 2) + h, 0:hw], lhsT, s[:, h * hw:(h + 1) * hw],
                                       start=(i == 0), stop=(i == len(srcs) - 1))
                mm.then_inc(pj, 1)

            def tiled(name, hw=HT, col0=0):
                t, c = AT[name], CAT[name]
                free(t)
                loaded(c)
                for h in range(2):
                    for k in range(KT):
                        if t == 0 and h == 0:
                            pe.wait_ge(xn_ok, k + 1)
                        mm = pe.matmul(ps[:, 2 * (t % 2) + h, 0:hw], wsl(c, k),
                                       xnv[:, k, col0 + h * hw:col0 + (h + 1) * hw], start=(k == 0), stop=(k == KT - 1))
                mm.then_inc(pj, 1)

            pe.wait_ge(init_ok, 1)
            for k in range(KT):
                pe.wait_ge(x_sq, k + 1)
                for h in range(2):
                    mm = pe.matmul(ps[:, 4 + h, 0:HT], ones, view(kv, (k % 2) * T, 2, HT)[:, h, :],
                                   start=(k == 0), stop=(k == KT - 1))
                mm.then_inc(xms, 1)
            pe.wait_ge(ld_v, 16)

            def values_tile(i):
                t, c = AT[f"V{i}"], CAT[f"V{i}"]
                free(t)
                loaded(c)
                for b in range(NB):
                    rows = min(P, T - b * P)
                    for k in range(KT):
                        mm = pe.matmul(ps[0:rows, 2 * (t % 2) + b // 4, (b % 4) * P:(b % 4 + 1) * P],
                                       xnv[:, k, b * P:b * P + rows], wsl(c, k), start=(k == 0), stop=(k == KT - 1))
                mm.then_inc(pj, 1)

            def scores(s):
                h, i = s // 4, s % 4
                n = META + P * (i + 1)
                if s >= 1:
                    pe.wait_ge(sexp, 2 * s)
                if n > 512:
                    pe.wait_ge(sav_ev, s - 1)
                for m in range(2):
                    r = slice(32 * ((2 * h + m) % 4), 32 * ((2 * h + m) % 4) + 32)
                    for a, b, bk, at in ((0, min(n, 512), 4 + m, 0), (512, n, 7, 256 + META * m)):
                        if a < b:
                            if bk == 7 and m:
                                pe.wait_ge(sco, 2 * s + 1)
                            mm = pe.matmul(ps[:, bk, at:at + b - a], aqk[r, h // 2, META + P * i:META + P * (i + 1)],
                                           aqk[r, 2 + h // 2, a:b], start=True, stop=True)
                    mm.then_inc(sco, 1)

            def wt_at(b):
                return (6, P * b) if b < 4 else (7, 0)

            def transposes(s):
                i = s % 4
                pe.wait_ge(scomb, s + 1)
                if s >= 1:
                    pe.wait_ge(swt_ev, s)
                if i == 3:
                    pe.wait_ge(sav_ev, s)
                for b in range(i + 2):
                    rows = P if b <= i else META
                    bk, c0 = wt_at(b)
                    mm = pe.transpose(ps[0:rows, bk, c0:c0 + P], prb[:, s % 2, 0, b * P:b * P + rows], ident)
                mm.then_inc(swt, 1)

            def weighted(s):
                h, i = s // 4, s % 4
                pe.wait_ge(swt_ev, s + 1)
                if s >= 1:
                    pe.wait_ge(sav_ev, s)
                if i == 2:
                    pe.wait_ge(sexp, 2 * s + 4)
                for b in range(i + 2):
                    rows = P if b <= i else META
                    mm = pe.matmul(ps[64 * (h % 2):64 * (h % 2) + 64, 7, 384:512], vt[0:rows, b, h * 64:h * 64 + 64],
                                   wtb[0:rows, s % 2, b, :], start=(b == 0), stop=(b == i + 1))
                mm.then_inc(sav, 1)

            def attention_step(name):
                s = STEPS.index(name)
                if 2 <= s < 18:
                    weighted(s - 2)
                if 1 <= s < 17:
                    transposes(s - 1)
                if 0 <= s < 16:
                    scores(s)

            for name in PROJ[:AT["LA"] + 1]:
                t = AT[name]
                if name == "BK0":
                    pe.wait_ge(a_ok, 4)
                    for i in range(4):
                        mm = pe.transpose(ps[0:DEC, 4, i * P:(i + 1) * P], aqk[:, i, L:T], ident)
                    mm.then_inc(t8, 1)
                if name[0] == "V":
                    values_tile(int(name[1]))
                elif name.startswith("AMS"):
                    pe.wait_ge(ld_c, 16)
                    pe.wait_ge(a_sq, int(name[3]) + 1)
                    stat(name, cc(C_B32, P), [asq[:, int(name[3]), :]], HT)
                elif name.startswith("ROT"):
                    pe.wait_ge(pj_free, AT["BK1"] + 1)
                    stat(name, cc(C_PERM, P), [bqk[:, int(name[3]), :]], HT)
                elif name == "DA":
                    free(t)
                    for h in range(2):
                        for k in range(KT):
                            mm = pe.matmul(ps[0:16, 2 * (t % 2) + h, 0:HT], vv(V_DA + 16 * k, 16),
                                           xnv[:, k, h * HT:(h + 1) * HT], start=(k == 0), stop=(k == KT - 1))
                    mm.then_inc(pj, 1)
                elif name == "LA":
                    free(t)
                    pe.wait_ge(pj_free, AT["DA"] + 1)
                    for h in range(2):
                        mm = pe.matmul(ps[:, 2 * (t % 2) + h, 0:HT], vv(V_G2, P, slice(0, 16)),
                                       das[:, h * HT:(h + 1) * HT], start=True, stop=True)
                    mm.then_inc(pj, 1)
                else:
                    tiled(name)
                if name in STEPS:
                    if name == STEPS[0]:
                        pe.wait_ge(t8_ev, 1)
                    attention_step(name)

            pe.wait_ge(rot_ok, 4)
            pe.wait_ge(sexp, 32)
            pe.wait_ge(swt_ev, 16)
            pe.wait_ge(sav_ev, 16)
            units = [(h, j) for h in range(H) for j in range(NB)]

            def ret_scores(u):
                h, j = units[u]
                rows, t0 = min(P, L - j * P), max(META, j * P)
                r = slice(64 * (h % 2), 64 * (h % 2) + 64)
                if u >= 2:
                    pe.wait_ge(at_w, u - 1)
                pe.matmul(ps[0:rows, 4 + u % 2, 0:L - t0], bqk[r, 2 + h // 2, j * P:j * P + rows],
                          bqk[r, h // 2, t0:L], start=True, stop=True).then_inc(at_s, 1)

            def ret_out(u):
                h, j = units[u]
                rows, t0 = min(P, L - j * P), max(META, j * P)
                pe.wait_ge(at_w, u + 1)
                pe.matmul(ps[64 * (h % 2):64 * (h % 2) + 64, 6 + h // 2, t0 - META:SEQ],
                          vt[0:rows, j, 256 + h * 64:256 + h * 64 + 64], atb[0:rows, u % 2, 0:L - t0],
                          start=(j == 0), stop=(j == NB - 1)).then_inc(at_o, 1)

            for u in range(len(units) + 1):
                if u < len(units):
                    ret_scores(u)
                if u >= 1:
                    ret_out(u - 1)
            for t in range(2):
                for b in range(4):
                    pe.transpose(ps[:, 4 + t, b * P:(b + 1) * P], bqk[:, 2 + t, b * P:(b + 1) * P], ident)
            pe.wait_ge(ob_ev, 1)
            for t in range(2):
                mm = pe.transpose(ps[0:TAIL, 6, t * P:(t + 1) * P], bqk[:, 2 + t, 4 * P:L], ident)
            mm.then_inc(kt_t, 1)
            pe.wait_ge(kd_ok, 1)
            pe.wait_ge(ob_ev, 2)
            for h in range(H):
                for b in range(NB):
                    rows = P if b < 4 else TAIL
                    mm = pe.matmul(ps[0:64, 7, h * 64:h * 64 + 64], kdv[0:rows, b, h * 64:h * 64 + 64],
                                   vt[0:rows, b, 256 + h * 64:256 + h * 64 + 64], start=(b == 0), stop=(b == NB - 1))
            mm.then_inc(st_mm, 1)
            pe.wait_ge(rs_ok, 1)
            for h in range(H):
                r = slice(64 * (h % 2), 64 * (h % 2) + 64)
                for b in range(DEC):
                    mm = pe.matmul(ps[r, 6, (h // 2) * DEC + b:(h // 2) * DEC + b + 1], rs0[r, h // 2, b, :],
                                   bqk[r, h // 2, L + b:L + b + 1], start=True, stop=True)
            mm.then_inc(ro_mm, 1)
            pe.wait_ge(s_mx, 1)
            pe.transpose(ps[0:64, 4, 0:P], mx, ident).then_inc(s_mxt, 1)
            pe.wait_ge(b_raw, 1)
            for t in range(2):
                stat(f"BMEAN{t}", cc(C_B64, P), [brv[:, 2 + t, :]], HN)
            pe.wait_ge(s_mx1, 1)
            pe.matmul(ps[:, 5, 0:64], mxb, cst[0:64, C_ID:C_ID + 64], start=True, stop=True).then_inc(s_mxm, 1)
            for t in range(2):
                pe.wait_ge(b_sq, t + 1)
                stat(f"BVAR{t}", cc(C_B64, P), [bn[:, t, :]], HN)

            for g, at in (("CR", V_WA), ("CI", V_WX)):
                for t in range(2):
                    pe.wait_ge(conv_ok, 2)
                    stat(f"{g}{t}", vv(at + t * P, P), [xc[:, t, :]], HT)

            def gate_tile(n, m):
                tiled(f"G{n}{m}", HN, META)

            def branch_tile(n, m):
                name = f"P{n}{m}"
                t = AT[name]
                free(t)
                if n == "D":
                    c = CAT["DP0"] + m // 4
                    loaded(c)
                for h in range(2):
                    for k in range(2):
                        w = (wsl(CAT["DP0"] + m // 4, (m % 4) * 2 + k) if n == "D" else wsl(CAT[f"G{n}{m}"], KT + k))
                        mm = pe.matmul(ps[:, 2 * (t % 2) + h, 0:HN], w,
                                       brv[:, BR[n] + k, h * HN:(h + 1) * HN], start=(k == 0), stop=(k == 1))
                mm.then_inc(pj, 1)

            def sample_values(j):
                b, half = j // 2, j % 2
                ns = HALF + half
                pe.wait_ge(kv_ld[half], (128, 144)[half] * (DEC + b + 1))
                if half == 0 and b >= 2:
                    pe.wait_ge(sr_ok, b - 1)
                for s in range(ns):
                    mm = pe.matmul(ps[0:H, 4 + b % 2, 0:256], W[:, b, half * HALF + s, :], kvb[half][:, s, :],
                                   start=(half == 0 and s == 0), stop=(half == 1 and s == ns - 1))
                mm.then_inc(v_used, 1)

            def sample_columns():
                pe.wait_ge(sr_ok, DEC)
                for b in range(DEC):
                    for t in range(2):
                        mm = pe.transpose(ps[:, 4, (b * 2 + t) * H:(b * 2 + t + 1) * H], srow[:, b, t * P:(t + 1) * P],
                                          cst[0:H, C_ID:C_ID + H])
                mm.then_inc(s_av, 1)

            def gla(j):
                g = j * NV // 32
                pe.wait_ge(g_p, j + 1)
                if j * NV == 32:
                    pe.wait_ge(d_raw, 1)
                for i in range(NV):
                    v32 = (j * NV + i) % 32
                    lhsT = cst[:, C_SEL + 31 - v32:C_SEL + 31 - v32 + P]
                    pe.matmul(ps[:, 6 + g, 0:SEQ], lhsT, pbv[:, j % 2, i, 0:SEQ], start=(v32 == 0), stop=(v32 == 31))
                    mm = pe.matmul(ps[:, 7 - g, 0:DEC], lhsT, pbv[:, j % 2, i, SEQ + 1:L:2],
                                   start=(v32 == 0), stop=(v32 == 31))
                mm.then_inc(g_mm, 1)

            jv = jg = 0
            for i, (n, m) in enumerate(ORDER):
                if (n, m) == ("C", 7):
                    sample_columns()
                gate_tile(n, m)
                if (n, m) == ("A", 0):
                    for t in range(2):
                        pe.wait_ge(a_osq, t + 1)
                        stat(f"AOS{t}", cc(C_B64, P), [osq[:, t, :]], HN)
                for q in range(SCANS[i]):
                    gla(jg)
                    jg += 1
                if m == (n == "A"):
                    pe.wait_ge(br_ok, i // KT + 1)
                if (n, m) == ("A", 1):
                    branch_tile("A", 0)
                if (n, m) != ("A", 0):
                    branch_tile(n, m)
                if i == 0:
                    pe.wait_ge(s_sum, 1)
                    pe.matmul(ps[:, 5, 64:128], cc(C_ONE, P), sm, start=True, stop=True).then_inc(s_tot, 1)
                if i == 2:
                    pe.wait_ge(s_w, 1)
                for q in range(HALVES[i]):
                    sample_values(jv)
                    jv += 1
            assert jv == 2 * DEC and jg == GROUPS
            for m in range(KT):
                if m == 4:
                    pe.wait_ge(d_sq, 2)
                    stat("DOS", cc(C_B32, P), [osq[:, t, :] for t in range(2)], HN)
                gate_tile("D", m)
            pe.wait_ge(br_ok, 4)
            for m in range(KT):
                branch_tile("D", m)

            pe.wait_ge(mg_used, 4 * KT)
            pe.wait_ge(pj_free, len(PROJ))
            for c8 in range(8):
                half, kp = c8 // 4, c8 % 4
                c = CAT[f"WO{c8}"]
                loaded(c)
                for kk in range(2):
                    k = 2 * kp + kk
                    for b in range(NB):
                        if k == 0 and half and b >= 3:
                            pe.wait_ge(wo_free, b - 2)
                        s0 = c % RING * WCH + kk * 512
                        mm = pe.matmul(ps[0:RB, (half * NB + b) % 8, :], acc[:, k, b * RB:(b + 1) * RB],
                                       ring[:, s0:s0 + 512], start=(k == 0), stop=(k == KT - 1))
                        if k == KT - 1:
                            mm.then_inc(wo, 1)
                if c8 < len(CH) - RING - CAT["WO0"]:
                    mm.then_inc(wo_rd[c8], 1)
            def logits(b):
                pe.wait_ge(tt_a, b + 1)
                pe.wait_ge(tt_d, b + 1)
                for k in range(KT):
                    mm = pe.matmul(ps[0:RB, 6, b * 32:b * 32 + 20], tT[:, k, b * RB:(b + 1) * RB],
                                   vv(V_RW + 20 * k, 20), start=(k == 0), stop=(k == KT - 1))
                return mm

            for b in range(NB):
                pe.wait_ge(t_ok, b + 1)
                for k in range(KT):
                    mm = pe.transpose(ps[:, 2 + 2 * (b % 2) + k // 4, (k % 4) * P:(k % 4) * P + RB], tk[b][:, k * P:(k + 1) * P],
                                      cst[0:RB, C_ID:C_ID + RB])
                mm.then_inc(tt_t, 1)
                if b:
                    logits(b - 1)
            logits(NB - 1).then_inc(lgm, 1)
            pe.wait_ge(sel_ok, 1)
            selm = sel[0:RB].rearrange("p b g e -> p (b g e)")
            pe.matmul(ps[0:RB, 4, 0:NB * NE], cst[0:RB, C_LT:C_LT + RB], selm, start=True, stop=True)
            pe.matmul(ps[:, 5, 0:NB * NE], cst[0:RB, C_ONE:C_ONE + P], selm, start=True, stop=True).then_inc(rank_ok, 1)

            def rows_T(s):
                for k in range(KT):
                    mm = pe.transpose(ps[:, k // 4, (k % 4) * P:(k % 4 + 1) * P], xe[s][:, k * P:(k + 1) * P], ident)
                return mm

            def hidden(s, w):
                for k in range(KT):
                    mm = pe.matmul(ps[:, 2 + s, :], xeT[s][:, k, :], w13b[w][:, k, :], start=(k == 0), stop=(k == KT - 1))
                return mm

            def hidden_T(s):
                for f in range(2):
                    mm = pe.transpose(ps[:, 4 + s, f * P:(f + 1) * P], hm[s][:, f * P:(f + 1) * P], ident)
                return mm

            def outputs(s, w):
                for n in range(2):
                    for f in range(2):
                        mm = pe.matmul(ps[:, 6 + n, :], hT[s][:, f, :], w2b[w][:, f, n * 512:(n + 1) * 512],
                                       start=(f == 0), stop=(f == 1))
                return mm

            def step(q, w):
                i, s, o_ = q * DEEP + w, w % 2, 1 - w % 2
                first, last = (isinstance(i, int) and i == n for n in (0, NE - 1))
                if not first:
                    pe.wait_ge(m_h, i)
                    hidden_T(o_).then_inc(m_ht, 1)
                pe.wait_ge(m_tev, i + 1)
                pe.wait_ge(m_w[w], q * 32 + 32)
                hidden(s, w).then_inc(m_h1, 1)
                if not last:
                    pe.wait_ge(m_xe[o_], q * (8 * DEEP) + 16 * ((w + 1) // 2 + 1))
                    rows_T(o_).then_inc(m_t, 1)
                if not first:
                    end(i, w)

            def end(i, w):
                pe.wait_ge(m_htev, i)
                if not (isinstance(i, int) and i < 2):
                    pe.wait_ge(m_ya, i - 1)
                    pe.wait_ge(m_yd, i - 1)
                outputs((w - 1) % 2, (w - 1) % DEEP).then_inc(m_y, 1)

            pe.wait_ge(m_xe[0], 16)
            rows_T(0).then_inc(m_t, 1)
            for w in range(DEEP):
                step(0, w)
            with pe.Fori(1, NE // DEEP - 1) as q:
                for w in range(DEEP):
                    step(q, w)
            for w in range(DEEP):
                step(NE // DEEP - 1, w)
            pe.wait_ge(m_h, NE)
            hidden_T(1).then_inc(m_ht, 1)
            end(NE, 0)

            pe.wait_ge(idx_ok, 1)
            n_over = pe.value_load(itab[0:1, 10 + OVER:11 + OVER], min_val=0, max_val=OVER)
            with pe.If(n_over > 0):
                pe.wait_ge(m_ya, NE)
                pe.wait_ge(m_yd, NE)
                with pe.Fori(0, n_over) as i:
                    pe.wait_ge(o_ld, i * 48 + 48)
                    rows_T(0).then_inc(o_t, 1)
                    pe.wait_ge(o_tev, i + 1)
                    hidden(0, 0).then_inc(o_h1, 1)
                    pe.wait_ge(o_h, i + 1)
                    hidden_T(0).then_inc(o_ht, 1)
                    pe.wait_ge(o_htev, i + 1)
                    outputs(0, 0).then_inc(o_y, 1)

        @block.scalar
        def _(act):
            link = Chain(act, ach)
            act.dma_start(vec[:, :], vec_d).then_inc(ld_v, 16)
            for k in range(KT):
                act.wait_ge(ld_x[k // (KT // 2)], 16)
                if k >= 2:
                    act.wait_ge(xms, k - 1)
                act.activation(view(kv, (k % 2) * T, T), xraw[:, k, :], ACT.Square).then_inc(x_sq, 1)
            act.wait_ge(init_ok, 1)
            act.wait_ge(xms, KT)
            act.activation(fold(view(kv, 0, T), HT), bank2(2, HT), ACT.Sqrt, bias=eps0, scale=1.0 / DM).then_inc(xsd, 1)
            act.wait_ge(ld_v, 16)
            act.activation(xxs[:, :, :, 0:3], view(vec, V_ST, 2, DEC, 3), ACT.Copy).then_inc(c_st, 1)
            act.wait_ge(par, 1)
            act.activation(sc[:, 3:5], sc[:, 1:3], ACT.Exp).then_inc(lam_e, 1)
            link(act.activation(sc[:, 24:26], vv(V_LL, 2), ACT.Abs))
            act.activation(sc[:, 26:28], sc[:, 24:26], ACT.Exp, scale=-1.0).then_inc(lam_e, 1)

            act.wait_ge(ld_c, 16)
            eps = cc(C_EPS)

            def ready(name):
                act.wait_ge(pj, AT[name] + 1)
                return 2 * (AT[name] % 2)

            def pair(name, w):
                b = ready(name)
                return ps[:, b:b + 2, 0:w]

            def copy(name, dst, w, func=ACT.Copy, **kw):
                act.activation(fold(dst, w), pair(name, w), func, **kw).then_inc(pj_free, 1)

            def spread(name, dst, off=0, scale=1.0, smp=None):
                b = ready(name)
                act.activation(dst[:, off:off + HT], ps[:, b, 0:HT], ACT.Copy, scale=scale)
                act.activation(dst[:, off + HT:off + L], ps[:, b + 1, 0:L - HT], ACT.Copy, scale=scale)
                act.activation(smp, ps[:, b + 1, L - HT:HT], ACT.Copy, scale=scale).then_inc(pj_free, 1)

            def exps(s):
                i = s % 4
                n = META + P * (i + 1)
                if s >= 2:
                    act.wait_ge(swt, s - 1)
                for m in range(2):
                    act.wait_ge(smx, 2 * s + (2 if i == 3 else m + 1))
                    nb = sc[:, 8 + 2 * (s % 2) + m:9 + 2 * (s % 2) + m]
                    ins = act.activation(prb[:, s % 2, m, 0:min(n, 512)], ps[:, 4 + m, 0:min(n, 512)], ACT.Exp, bias=nb,
                                         accum_out=sc[:, 12 + 2 * (s % 2) + m:13 + 2 * (s % 2) + m])
                    if i == 3:
                        c0 = 256 + META * m
                        ins = act.activation(prb[:, s % 2, m, 512:n], ps[:, 7, c0:c0 + META], ACT.Exp, bias=nb,
                                             accum_out=sc[:, 36 + m:37 + m])
                    ins.then_inc(sexp, 1)

            def wt_copy(s):
                i = s % 4
                act.wait_ge(swt, s + 1)
                if s >= 2:
                    act.wait_ge(sav, s - 1)
                act.activation(wtb[:, s % 2, 0:i + 1, :], ps[:, 6, 0:(i + 1) * P].rearrange("p (a b) -> p a b", b=P),
                               ACT.Copy)
                src = ps[0:META, 7, 0:P] if i == 3 else ps[0:META, 6, P * (i + 1):P * (i + 2)]
                act.activation(wtb[0:META, s % 2, i + 1, :], src, ACT.Copy).then_inc(swt_ev, 1)

            for name in PROJ[:AT["LA"] + 1]:
                t = AT[name]
                kind, i = name[:-1], (int(name[-1]) if name[-1].isdigit() else 0)
                if kind in ("AQ", "AK"):
                    j = 2 * (kind == "AK") + i
                    act.activation(fold(aqk[:, j, :], HT), pair(name, HT), ACT.Copy).then_inc(pj_free, 1)
                    act.wait_ge(pj_free, t + 1)
                    act.wait_ge(xn_ok, KT)
                    act.activation(asq[:, j, :], aqk[:, j, :], ACT.Square).then_inc(a_sq, 1)
                elif kind == "V":
                    b = ready(name)
                    act.activation(vt[:, 0:4, i * P:(i + 1) * P], ps[:, b, :].rearrange("p (a c) -> p a c", c=P), ACT.Copy)
                    act.activation(vt[0:T - 4 * P, 4, i * P:(i + 1) * P], ps[0:T - 4 * P, b + 1, 0:P], ACT.Copy)\
                       .then_inc(pj_free, 1)
                    if i == 3:
                        act.wait_ge(pj_free, t + 1)
                        act.dma_start(scr_v[:, :], vt[TAIL:TAIL + DEC, 4, :]).then_inc(s_v, 16)
                elif kind == "AMS":
                    copy(name, arr[:, i, :], HT, ACT.Sqrt, bias=eps)
                elif kind == "BQ":
                    copy(name, bqk[:, i, :], HT)
                    if i == 1:
                        act.wait_ge(t8, 1)
                        link(act.activation(qk8, ps[0:DEC, 4, :], ACT.Copy))
                        act.sem_inc(t8_ev, 1)
                        act.dma_start(scr_qk[:, :], qk8).then_inc(s_qk, 16)
                elif kind == "BK":
                    copy(name, bqk[:, 2 + i, :], HT, ACT.Copy, scale=0.125)
                elif kind == "BG":
                    copy(name, bgv[:, i, :], HT, ACT.Silu)
                elif kind == "ROT":
                    if i >= 2:
                        act.wait_ge(rot_ok, i - 1)
                    copy(name, rot[:, i % 2, :], HT)
                elif kind == "CX":
                    spread(name, cxv[:, i, :], 3, smp=xxs[:, i, :, 3])
                elif kind == "CG":
                    copy(name, cgv[:, i, :], HT, ACT.Gelu_apprx_tanh)
                elif name == "DQ":
                    spread(name, dqv, 0, 32 ** -0.5, smp=dqv[:, L + 1:XT:2])
                elif name == "DK":
                    spread(name, dkv, smp=dkv[:, L + 1:XT:2])
                elif kind == "DV":
                    spread(name, dvv[:, i, :], smp=dvv[:, i, L + 1:XT:2])
                    if i == 1:
                        act.wait_ge(pj_free, t + 1)
                        act.wait_ge(kv0, 1)
                        act.dma_start(scr_dv.rearrange("(a p) t -> p a t", p=P), dvv).then_inc(s_dv, 16)
                elif kind == "DR":
                    copy(name, drv[:, i, :], HT, ACT.Silu)
                elif name == "DA":
                    b = ready(name)
                    act.wait_ge(s_qk, 16)
                    act.activation(fold(das, HT), ps[0:16, b:b + 2, 0:HT], ACT.Copy).then_inc(pj_free, 1)
                elif name == "LA":
                    act.activation(fold(dg[:, 0, :], HT), pair(name, HT), ACT.Identity, bias=vv(V_GB)).then_inc(pj_free, 1)
                    act.wait_ge(pj_free, t + 1)
                    link(act.activation(dg[:, 1, :], dg[:, 0, :], ACT.Abs))
                    link(act.activation(dg[:, 1, :], dg[:, 1, :], ACT.Exp, scale=-1.0))
                    act.activation(dg[:, 1, :], dg[:, 1, :], ACT.Ln, bias=cc(C_ONE)).then_inc(la_z, 1)
                s = STEPS.index(name) if name in STEPS else -1
                if 0 <= s < 16:
                    exps(s)
                if 1 <= s < 17:
                    wt_copy(s - 1)
            act.wait_ge(la_m, 1)
            for i in range(NV):
                act.activation(ea[:, i * XT:i * XT + L], dg[:, 0, 0:L], ACT.Exp, scale=1.0 / 16)
                act.activation(ea[:, i * XT + L + 1:(i + 1) * XT:2], dg[:, 0, L:T], ACT.Exp, scale=1.0 / 16).then_inc(la_e, 1)
            for t in range(2):
                act.wait_ge(at_o, 2 * NB * (t + 1))
                act.activation(brv[:, 2 + t, 0:SEQ], ps[:, 6 + t, :], ACT.Copy).then_inc(ob_ev, 1)
            act.wait_ge(st_mm, 1)
            act.activation(rst, ps[0:64, 7, 0:256].rearrange("p (h v) -> p h v", h=H), ACT.Copy).then_inc(st_ev, 1)
            act.wait_ge(ro_mm, 1)
            act.activation(brv[:, 2:4, SEQ:N], ps[:, 6, 0:2 * DEC].rearrange("p (t b) -> p t b", t=2), ACT.Copy)\
               .then_inc(b_raw, 1)
            for t in range(2):
                copy(f"BMEAN{t}", bsd[:, t, :], HN)
            for t in range(2):
                act.wait_ge(b_cen, t + 1)
                act.activation(bn[:, t, :], brv[:, 2 + t, :], ACT.Square).then_inc(b_sq, 1)
            for t in range(2):
                copy(f"BVAR{t}", bsd[:, t, :], HN, ACT.Sqrt, bias=eps)
            act.wait_ge(s_sub, 1)
            act.activation(S[:, :, :, :], S[:, :, :, :], ACT.Exp).then_inc(s_exp, 1)
            act.wait_ge(c_par, 1)
            for t in range(2):
                copy(f"CR{t}", rr[:, t, :], HT, ACT.Sigmoid, bias=vv(V_BA + t))
            for t in range(2):
                copy(f"CI{t}", ri[:, t, :], HT, ACT.Sigmoid, bias=vv(V_BX + t))
            act.wait_ge(pj_free, AT["CI1"] + 1)
            for t in range(2):
                act.activation(aa[:, t, :], rr[:, t, :], ACT.Exp, scale=sc[:, 20 + t:21 + t])
                act.activation(th[:, t, :], rr[:, t, :], ACT.Tanh, scale=sc[:, 20 + t:21 + t]).then_inc(c_act, 1)
            act.wait_ge(c_q, 1)
            act.activation(rr[:, :, :], th[:, :, :], ACT.Sqrt, scale=-1.0).then_inc(c_act, 1)

            def merge(n, m, i):
                if i >= 2:
                    act.wait_ge(mg_used, i - 1)
                if i == 0:
                    act.wait_ge(br_ok, 1)
                copy(f"G{n}{m}", sgtv[:, i % 2, :], HN, ACT.Sigmoid, bias=vv(V_BM + 8 * "ABCD".index(n) + m))
                if (n, m) == ("A", 0):
                    for t in range(2):
                        copy(f"AOS{t}", osd[:, t, :], HN, ACT.Sqrt, bias=eps)
                    return
                if (n, m) == ("A", 1):
                    projection("A", 0, i - 1)
                projection(n, m, i)

            def projection(n, m, i):
                copy(f"P{n}{m}", ptv[:, i % 2, :], HN)
                act.wait_ge(pj_free, AT[f"P{n}{m}"] + 1)
                act.sem_inc(mg, 1)

            def gla_out(g):
                act.wait_ge(g_mm, (g + 1) * GROUPS // 2)
                act.activation(brv[:, 6 + g, 0:SEQ], ps[:, 6 + g, :], ACT.Copy)
                act.activation(brv[:, 6 + g, SEQ:N], ps[:, 7 - g, 0:DEC], ACT.Copy).then_inc(d_raw, 1)

            act.wait_ge(rst_out, 16)
            scans = halves = 0
            for i, (n, m) in enumerate(ORDER):
                if (n, m) == ("C", 7):
                    act.wait_ge(s_av, 1)
                    for t in range(2):
                        for hh_ in range(2):
                            r = slice(64 * hh_, 64 * hh_ + 64)
                            at = 2 * t + hh_
                            ins = act.activation(brv[r, t, SEQ:N], ps[r, 4, t * H + at:2 * DEC * H:2 * H], ACT.Copy)
                        ins.then_inc(a_raw, 1)
                    for t in range(2):
                        act.wait_ge(a_raw, 2)
                        act.activation(osq[:, t, :], brv[:, t, :], ACT.Square).then_inc(a_osq, 1)
                merge(n, m, i)
                for b in range(halves // 2, (halves + HALVES[i]) // 2):
                    act.wait_ge(v_used, 2 * b + 2)
                    act.activation(srow[:, b, :], ps[0:H, 4 + b % 2, 0:256], ACT.Copy).then_inc(sr_ok, 1)
                halves += HALVES[i]
                if scans < GROUPS // 2 <= scans + SCANS[i]:
                    gla_out(0)
                scans += SCANS[i]
            gla_out(1)
            act.wait_ge(d_raw, 2)
            act.wait_ge(br_ok, 3)
            for g in range(2):
                act.activation(osq[:, g, :], brv[:, 6 + g, :], ACT.Square).then_inc(d_sq, 1)
            act.wait_ge(s_w, 1)
            for m in range(KT):
                if m == 4:
                    copy("DOS", osd[:, 0, :], HN, ACT.Sqrt, bias=eps, scale=0.5)
                copy(f"GD{m}", sgv[:, m, :], HN, ACT.Sigmoid, bias=vv(V_BM + 24 + m))
            for m in range(KT):
                i = 3 * KT + m
                act.wait_ge(mg_used, i - 1)
                copy(f"PD{m}", ptv[:, i % 2, :], HN)
                act.wait_ge(pj_free, AT[f"PD{m}"] + 1)
                act.sem_inc(mg, 1)
            act.activation(sc[:, 54:55], eps, ACT.Sqrt)
            for b in range(NB):
                act.wait_ge(wo_free, NB + b + 1)
                link(act.activation(sgt[0:RB, 0:DM], hres[b], ACT.Square, accum_out=sc[0:RB, 40 + b:41 + b]))
                act.activation(sc[0:RB, 45 + b:46 + b], sc[0:RB, 40 + b:41 + b], ACT.Sqrt, bias=eps[0:RB, :],
                               scale=1.0 / DM).then_inc(n2_sd, 1)
            for b in range(NB):
                act.wait_ge(tt_t, b + 1)
                act.activation(tT[:, 0:4, b * RB:(b + 1) * RB],
                               ps[:, 2 + 2 * (b % 2), :].rearrange("p (k n) -> p k n", n=P)[:, :, 0:RB], ACT.Copy).then_inc(tt_a, 1)
            act.wait_ge(r1, 1)
            act.activation(rt[0:RB, 0, :, :], rt[0:RB, 0, :, :], ACT.Exp).then_inc(r2, 1)
            act.wait_ge(r1, 2)
            act.activation(rt[0:RB, 1, :, 0:1], rt[0:RB, 1, :, 0:1], ACT.Exp).then_inc(r2, 1)

            def rows_copy(s):
                return act.activation(xeT[s].rearrange("p (a k) n -> p a (k n)", a=2), ps[:, 0:2, :], ACT.Copy)

            def silu(s):
                return act.activation(si[s], ps[:, 2 + s, 0:256], ACT.Silu)

            def out_copy(s):
                return act.activation(yb[s][:, 0, :], ps[:, 6, :], ACT.Copy)

            def step(q, s, last=False):
                i, o_ = q * 2 + s, 1 - s
                act.wait_ge(m_h1, i + 1)
                silu(s).then_inc(m_si, 1)
                if not last:
                    act.wait_ge(m_t, i + 2)
                    rows_copy(o_).then_inc(m_tev, 1)
                if isinstance(i, int) and i == 0:
                    return
                act.wait_ge(m_y, i)
                if not (isinstance(i, int) and i < 3):
                    act.wait_ge(m_yst[o_], q * 16 - (16 if s == 0 else 0))
                out_copy(o_).then_inc(m_ya, 1)

            act.wait_ge(m_t, 1)
            rows_copy(0).then_inc(m_tev, 1)
            step(0, 0)
            step(0, 1)
            step(1, 0)
            step(1, 1)
            with act.Fori(2, PAIRS - 1) as q:
                step(q, 0)
                step(q, 1)
            step(PAIRS - 1, 0)
            step(PAIRS - 1, 1, last=True)
            act.wait_ge(m_y, NE)
            act.wait_ge(m_yst[1], 16 * (PAIRS - 1))
            out_copy(1).then_inc(m_ya, 1)

            act.wait_ge(idx_ok, 1)
            n_over = act.value_load(itab[0:1, 10 + OVER:11 + OVER], min_val=0, max_val=OVER)
            with act.If(n_over > 0):
                act.wait_ge(m_yst[0], 16 * PAIRS)
                with act.Fori(0, n_over) as i:
                    act.wait_ge(o_t, i + 1)
                    rows_copy(0).then_inc(o_tev, 1)
                    act.wait_ge(o_h1, i + 1)
                    silu(0).then_inc(o_si, 1)
                    act.wait_ge(o_y, i + 1)
                    out_copy(0).then_inc(o_ya, 1)

        @block.vector
        def _(dve):
            link = Chain(dve, dch)
            tt, ts, stt = dve.tensor_tensor, dve.tensor_scalar, dve.scalar_tensor_tensor

            dve.memset(eps0, EPS)
            dve.memset(ones, 1.0).then_inc(init_ok, 1)
            dve.wait_ge(ld_v, 16)
            dve.wait_ge(xsd, 1)
            link(dve.reciprocal(view(kv, 0, T), view(kv, 0, T)))
            for k in range(KT):
                stt(xnv[:, k, :], xraw[:, k, :], vv(V_N1 + k), view(kv, 0, T), ALU.mult, ALU.mult).then_inc(xn_ok, 1)
            lv = view(vec, V_LAM, 2, 2, 32)
            lp = view(sgt, 0, 2, 32)
            link(tt(lp, lv[:, :, 0, :], lv[:, :, 1, :], ALU.mult))
            dve.tensor_reduce(sc[:, 1:3], lp, X, ALU.add).then_inc(par, 1)
            dve.wait_ge(lam_e, 1)
            link(tt(sc[:, 5:6], sc[:, 3:4], sc[:, 4:5], ALU.subtract))
            link(ts(sc[:, 0:1], sc[:, 5:6], LAM0, None, ALU.add))
            link(ts(sc[:, 22:23], vv(V_AN), 1.0 - LAM0, None, ALU.mult))
            link(ts(sc[:, 23:24], vv(V_QN), 32 ** -0.5, None, ALU.mult))
            dve.wait_ge(lam_e, 2)
            e, z, z2, q = sc[:, 26:28], sc[:, 28:30], sc[:, 30:32], sc[:, 32:34]
            link(ts(z, e, 2.0, None, ALU.add))
            link(dve.reciprocal(z, z))
            link(tt(z, z, e, ALU.mult))
            link(tt(z2, z, z, ALU.mult))
            link(ts(q, z2, 1.0 / 17, None, ALU.mult))
            for k in range(15, 1, -2):
                link(stt(q, q, 1.0 / k, z2, ALU.add, ALU.mult))
            link(stt(q, q, 1.0, z, ALU.add, ALU.mult))
            link(ts(z, vv(V_LL, 2), 0.0, 8.0, ALU.min, ALU.mult))
            stt(sc[:, 20:22], q, -16.0, z, ALU.mult, ALU.add).then_inc(c_par, 1)

            for i in range(4):
                dve.wait_ge(pj_free, AT[f"AMS{i}"] + 1)
                link(dve.reciprocal(arr[:, i, :], arr[:, i, :]))
                stt(aqk[:, i, :], aqk[:, i, :], sc[:, 23:24] if i < 2 else vv(V_KN), arr[:, i, :], ALU.mult, ALU.mult)\
                   .then_inc(a_ok, 1)

            def causal_max(s):
                i = s % 4
                n = META + P * (i + 1)
                for m in range(2):
                    dve.wait_ge(sco, 2 * s + m + 1)
                    main, nb = ps[:, 4 + m, :], sc[:, 8 + 2 * (s % 2) + m:9 + 2 * (s % 2) + m]
                    k = min(n, 512)
                    last = ps[:, 7, 256 + META * m:256 + META * (m + 1)]
                    link(tt(main[:, n - 144:k], main[:, n - 144:k], cc(C_MASK, k - n + 144), ALU.add))
                    if i < 3:
                        dve.tensor_reduce(nb, main[:, 0:k], X, ALU.max, negate=True).then_inc(smx, 1)
                    else:
                        dve.wait_ge(sco, 2 * s + 2)
                        link(tt(last, last, cc(C_MASK + P, META), ALU.add))
                        dve.tensor_reduce(sc[:, 38:39], main, X, ALU.max, negate=True)
                        link(dve.tensor_reduce(sc[:, 39:40], last, X, ALU.max, negate=True))
                        tt(nb, sc[:, 38:39], sc[:, 39:40], ALU.min).then_inc(smx, 1)

            def combine(s):
                i = s % 4
                n = META + P * (i + 1)
                dve.wait_ge(sexp, 2 * s + 2)
                r = sc[:, 16:18]
                sums = sc[:, 12 + 2 * (s % 2):14 + 2 * (s % 2)]
                if i == 3:
                    link(tt(sums, sums, sc[:, 36:38], ALU.add))
                link(dve.reciprocal(r, sums))
                link(tt(r[:, 1:2], r[:, 1:2], sc[:, 0:1], ALU.mult))
                link(ts(prb[:, s % 2, 1, 0:n], prb[:, s % 2, 1, 0:n], r[:, 1:2], None, ALU.mult))
                stt(prb[:, s % 2, 0, 0:n], prb[:, s % 2, 0, 0:n], r[:, 0:1], prb[:, s % 2, 1, 0:n], ALU.mult, ALU.subtract)\
                   .then_inc(scomb, 1)

            def av_copy(s):
                h, i = s // 4, s % 4
                dve.wait_ge(sav, s + 1)
                if s == 0:
                    dve.wait_ge(zeroed, 16 * (NE + 2 * OVER))
                r = slice(64 * (h % 2), 64 * (h % 2) + 64)
                dve.tensor_copy(brv[r, h // 2, P * i:P * (i + 1)], ps[r, 7, 384:512]).then_inc(sav_ev, 1)

            def rotate(i):
                dve.wait_ge(pj_free, AT[f"ROT{i}"] + 1)
                link(tt(rot[:, i % 2, :], rot[:, i % 2, :], cc(C_SIN, T), ALU.mult))
                link(tt(bqk[:, i, :], bqk[:, i, :], cc(C_COS, T), ALU.mult))
                tt(bqk[:, i, :], bqk[:, i, :], rot[:, i % 2, :], ALU.add).then_inc(rot_ok, 1)

            def conv(t):
                dve.wait_ge(pj_free, AT[f"CX{t}"] + 1)
                dve.wait_ge(c_st, 1)
                dve.wait_ge(kv0, 1)
                w = [vv(V_CW + 2 * k + t) for k in range(4)]
                link(ts(xc[:, t, 0:L], cxv[:, t, 0:L], w[0], vv(V_CB + t), ALU.mult, ALU.add))
                link(ts(xc[:, t, L:T], xxs[:, t, :, 0], w[0], vv(V_CB + t), ALU.mult, ALU.add))
                for k in range(1, 4):
                    link(stt(xc[:, t, 0:L], cxv[:, t, k:k + L], w[k], xc[:, t, 0:L], ALU.mult, ALU.add))
                    ins = stt(xc[:, t, L:T], xxs[:, t, :, k], w[k], xc[:, t, L:T], ALU.mult, ALU.add)
                    if k < 3:
                        link(ins)
                ins.then_inc(conv_ok, 1)

            def sample_scores(j):
                b, half = j // 2, j % 2
                ns = HALF + half
                dve.wait_ge(kv_ld[half], (128, 144)[half] * (b + 1))
                dve.wait_ge(ld_q, 16)
                kb = kvb[half]
                link(tt(kb, kb, qbc[:, b:b + 1, :].to_broadcast([P, ns, 256]), ALU.mult))
                dve.tensor_reduce(S[:, b, half * HALF:half * HALF + ns, :], kb.rearrange("p s (m d) -> p s m d", d=32),
                                  X, ALU.add).then_inc(k_used, 1)

            for s in range(18):
                if s >= 2:
                    av_copy(s - 2)
                if s < 16:
                    causal_max(s)
                if 5 <= s < 9:
                    rotate(s - 5)
                if s in (9, 10):
                    conv(s - 9)
                if s < 16:
                    combine(s)
                    sample_scores(s)
            dve.wait_ge(la_z, 1)
            stt(dg[:, 0, :], dg[:, 0, :], 0.0, dg[:, 1, :], ALU.min, ALU.subtract).then_inc(la_m, 1)
            for u in range(H * NB):
                h, j = u // NB, u % NB
                rows, t0 = min(P, L - j * P), max(META, j * P)
                dve.wait_ge(at_s, u + 1)
                if u >= 2:
                    dve.wait_ge(at_o, u - 1)
                d0 = C_DT + h * L + t0 - j * P
                tt(atb[0:rows, u % 2, 0:L - t0], ps[0:rows, 4 + u % 2, 0:L - t0], cst[0:rows, d0:d0 + L - t0], ALU.mult)\
                  .then_inc(at_w, 1)
            dve.wait_ge(k_used, 2 * DEC)
            link(ts(S[:, :, PAGES, :], S[:, :, PAGES, :], cc(C_NEW), None, ALU.add))
            dve.tensor_reduce(mx.rearrange("p (b m) -> p b m", m=8), S.rearrange("p b s m -> p b m s"), X, ALU.max)\
               .then_inc(s_mx, 1)
            dve.wait_ge(kt_t, 1)
            for t in range(2):
                dec = view(cst, C_DEC, NB, H)[:, :, 2 * t:2 * t + 2]
                tt(kdv[:, 0:4, t * P:(t + 1) * P].rearrange("p b (h k) -> p b h k", h=2),
                   ps[:, 4 + t, :].rearrange("p (b h k) -> p b h k", b=4, h=2),
                   dec[:, 0:4, :].unsqueeze(3).to_broadcast([P, 4, 2, 64]), ALU.mult)
                ins = tt(kdv[0:TAIL, 4, t * P:(t + 1) * P].rearrange("p (h k) -> p h k", h=2),
                         ps[0:TAIL, 6, t * P:(t + 1) * P].rearrange("p (h k) -> p h k", h=2),
                         dec[0:TAIL, 4, :].unsqueeze(2).to_broadcast([TAIL, 2, 64]), ALU.mult)
            ins.then_inc(kd_ok, 1)
            dve.wait_ge(ld_rs, 16 * (1 + H))
            for t in range(2):
                kb = bqk[:, 2 + t, L:T].unsqueeze(2).to_broadcast([P, DEC, 64])
                link(tt(rv[:, t, :, :], rv[:, t, :, :], kb, ALU.mult))
                ins = stt(rs0[:, t, :, :], rs0[:, t, :, :], cc(C_GAM + t), rv[:, t, :, :], ALU.mult, ALU.add)
            ins.then_inc(rs_ok, 1)
            dve.wait_ge(s_mxt, 1)
            link(dve.tensor_reduce(mx1, ps[0:64, 4, 0:P], X, ALU.max))
            ts(mxb, cst[0:64, C_ONE:C_ONE + P], mx1, None, ALU.mult).then_inc(s_mx1, 1)
            for t in range(2):
                dve.wait_ge(pj_free, AT[f"BMEAN{t}"] + 1)
                tt(brv[:, 2 + t, :], brv[:, 2 + t, :], bsd[:, t, :], ALU.subtract).then_inc(b_cen, 1)
            dve.wait_ge(s_mxm, 1)
            link(dve.tensor_copy(Mb.rearrange("p b m -> p (b m)"), ps[:, 5, 0:64]))
            tt(S, S, Mb.unsqueeze(2).to_broadcast([P, DEC, SLOTS, 8]), ALU.subtract).then_inc(s_sub, 1)
            for t in range(2):
                dve.wait_ge(pj_free, AT[f"BVAR{t}"] + 1)
                link(dve.reciprocal(bsd[:, t, :], bsd[:, t, :]))
                link(stt(brv[:, 2 + t, :], brv[:, 2 + t, :], vv(V_RN), bsd[:, t, :], ALU.mult, ALU.mult))
                ins = tt(brv[:, 2 + t, :], brv[:, 2 + t, :], bgv[:, t, META:T], ALU.mult)
            ins.then_inc(br_ok, 1)
            dve.wait_ge(s_exp, 1)
            dve.tensor_reduce(sm.rearrange("p (b m) -> p b m", m=8), S.rearrange("p b s m -> p b m s"), X, ALU.add)\
               .then_inc(s_sum, 1)
            dve.wait_ge(c_act, 2)
            link(tt(rr[:, :, :], aa[:, :, :], aa[:, :, :], ALU.mult))
            stt(th[:, :, :], rr[:, :, :], 1.0, th[:, :, :], ALU.add, ALU.mult).then_inc(c_q, 1)
            link(tt(ri[:, :, :], ri[:, :, :], xc[:, :, :], ALU.mult))
            dve.wait_ge(c_act, 3)
            link(tt(ri[:, :, :], ri[:, :, :], rr[:, :, :], ALU.mult))
            for t in range(2):
                dve.tensor_tensor_scan(th[:, t, 0:L], aa[:, t, 0:L], ri[:, t, 0:L], 0.0, ALU.mult, ALU.add)
            link(tt(th[:, :, L:T], aa[:, :, L:T], view(vec, V_ST + 48, 2, DEC), ALU.mult))
            link(tt(th[:, :, L:T], th[:, :, L:T], ri[:, :, L:T], ALU.add))
            dve.wait_ge(la_e, NV)
            tt(brv[:, 4:6, :], th[:, :, META:T], cgv[:, :, META:T], ALU.mult).then_inc(br_ok, 1)
            dve.tensor_copy(cst_out[:, :, 0:1 + DEC], th[:, :, L - 1:T])
            dve.tensor_copy(cst_out[:, :, 9:12], cxv[:, :, L:L + 3])
            dve.tensor_copy(cst_out[:, :, 12:36].rearrange("p t (b i) -> p t b i", b=DEC), xxs[:, :, :, 1:4]).then_inc(c_out, 1)

            dve.wait_ge(s_tot, 1)
            rc = Mb
            link(dve.reciprocal(rc.rearrange("p b m -> p (b m)"), ps[:, 5, 64:128]))
            odd = rc.rearrange("p b (h m) -> p (b h) m", m=2)[:, :, 1]
            link(ts(odd, odd, sc[:, 0:1], None, ALU.mult))
            link(tt(S, S, rc.unsqueeze(2).to_broadcast([P, DEC, SLOTS, 8]), ALU.mult))
            Sp = S.rearrange("p b s (h m) -> p (b s h) m", m=2)
            tt(W.rearrange("p b s h -> p (b s h)"), Sp[:, :, 0], Sp[:, :, 1], ALU.subtract).then_inc(s_w, 1)

            qx = dqv[:, META:XT].unsqueeze(1).to_broadcast([P, NV, L])
            kx = dkv.unsqueeze(1).to_broadcast([P, NV, XT])
            dve.wait_ge(ea_ok, 1)

            def gla(j):
                v = vb[j % VR]
                dve.wait_ge(vb_s0, j + 1)
                link(tt(v, v, kx, ALU.mult))
                vf = v.rearrange("p a t -> p (a t)")
                link(dve.tensor_tensor_scan(vf, ea[:, :], vf, 0.0, ALU.mult, ALU.add))
                dve.sem_inc(g_scan, 1)
                if j >= 2:
                    dve.wait_ge(g_mm, j - 1)
                tt(pbv[:, j % 2, :, :], v[:, :, META:XT], qx, ALU.mult).then_inc(g_p, 1)

            def a_norm():
                for t in range(2):
                    dve.wait_ge(pj_free, AT[f"AOS{t}"] + 1)
                    link(dve.reciprocal(osd[:, t, :], osd[:, t, :]))
                    ins = stt(brv[:, t, :], brv[:, t, :], sc[:, 22:23], osd[:, t, :], ALU.mult, ALU.mult)
                ins.then_inc(br_ok, 1)

            for j in range(GROUPS):
                if j == sum(SCANS[:2 * KT + 1]):
                    a_norm()
                gla(j)
            dve.wait_ge(pj_free, AT["DOS"] + 1)
            link(dve.reciprocal(osd[:, 0, :], osd[:, 0, :]))
            for g in range(2):
                link(stt(brv[:, 6 + g, :], brv[:, 6 + g, :], vv(V_GN + g), osd[:, 0, :], ALU.mult, ALU.mult))
                ins = tt(brv[:, 6 + g, :], brv[:, 6 + g, :], drv[:, g, META:T], ALU.mult)
            ins.then_inc(br_ok, 1)

            dve.wait_ge(mg_used, 3 * KT)
            for m in range(KT):
                i = 3 * KT + m
                dve.wait_ge(mg, i + 1)
                p_ = ptv[:, i % 2, :]
                link(tt(p_, sgv[:, m, :], p_, ALU.mult))
                tt(acc[:, m, :], acc[:, m, :], p_, ALU.add).then_inc(mg_used, 1)

            dve.wait_ge(ld_x2, 16 * (NB + 1))
            def normalise(b):
                dve.wait_ge(n2_sd, b + 1)
                link(dve.reciprocal(sc[0:RB, 45 + b:46 + b], sc[0:RB, 45 + b:46 + b]))
                stt(tk[b], hres[b], sc[0:RB, 45 + b:46 + b], n2row, ALU.mult, ALU.mult).then_inc(t_ok, 1)

            for half in range(2):
                for b in range(NB):
                    dve.wait_ge(wo, half * NB + b + 1)
                    hb = hres[b][:, half * 512:half * 512 + 512]
                    tt(hb, hb, ps[0:RB, (half * NB + b) % 8, :], ALU.add).then_inc(wo_free, 1)
                    if half and b >= 2:
                        normalise(b - 2)

            def rows_T_copy(b):
                dve.wait_ge(tt_t, b + 1)
                dve.tensor_copy(tT[:, 4:8, b * RB:(b + 1) * RB],
                                ps[:, 3 + 2 * (b % 2), :].rearrange("p (k n) -> p k n", n=P)[:, :, 0:RB]).then_inc(tt_d, 1)

            rows_T_copy(0)
            normalise(NB - 2)
            rows_T_copy(1)
            normalise(NB - 1)
            for b in range(2, NB):
                rows_T_copy(b)

            R = slice(0, RB)
            w4 = sc[R, 50:54]
            ts(w4, cst[R, C_IO:C_IO + 4], -1.0, 4.0, ALU.mult, ALU.add)
            w4 = w4.unsqueeze(1).to_broadcast([RB, NB, 4])
            dve.wait_ge(lgm, 1)
            l_ = lg[R, :, :]
            link(tt(l_, ps[R, 6, 0:NB * 32].rearrange("p (b n) -> p b n", b=NB)[:, :, 0:20],
                    vec[R, V_RB:V_RB + 20].unsqueeze(1).to_broadcast([RB, NB, 20]), ALU.add))
            r = [rt[R, i, :, :] for i in range(20)]
            one = [rt[R, i, :, 0:1] for i in range(20)]

            def first_of(oh, eq, c):
                link(tt(oh, eq, w4, ALU.mult))
                link(dve.tensor_reduce(c, oh, X, ALU.max))
                link(tt(oh, oh, c.to_broadcast([RB, NB, 4]), ALU.is_equal))

            gl, le = l_[:, :, 0:4], l_[:, :, 4:20].rearrange("p b (g e) -> p b g e", g=4)
            link(dve.tensor_reduce(one[2], gl, X, ALU.max))
            tt(r[0], gl, one[2].to_broadcast([RB, NB, 4]), ALU.subtract).then_inc(r1, 1)
            link(tt(r[3], gl, one[2].to_broadcast([RB, NB, 4]), ALU.is_equal))
            first_of(r[4], r[3], one[5])
            dve.wait_ge(r2, 1)
            link(dve.tensor_reduce(one[6], r[0], X, ALU.add))
            link(dve.reciprocal(one[6], one[6]))
            ge = f1[R]
            for b in range(NB):
                ins = tt(ge[:, b, :, :], le[:, b, :, :], r[4][:, b, :].unsqueeze(2).to_broadcast([RB, 4, 4]), ALU.mult)
            link(ins)
            link(dve.tensor_reduce(r[7], ge.rearrange("p b g e -> p b e g"), X, ALU.add))
            link(dve.tensor_reduce(one[8], r[7], X, ALU.max))
            link(tt(r[9], r[7], one[8].to_broadcast([RB, NB, 4]), ALU.is_equal))
            first_of(r[10], r[9], one[5])
            link(stt(r[11], r[10], NEG, r[7], ALU.mult, ALU.add))
            link(dve.tensor_reduce(one[12], r[11], X, ALU.max))
            tt(one[1], one[12], one[8], ALU.subtract).then_inc(r1, 1)
            link(tt(r[13], r[11], one[12].to_broadcast([RB, NB, 4]), ALU.is_equal))
            first_of(r[14], r[13], one[5])
            dve.wait_ge(r2, 2)
            link(ts(one[15], one[1], 1.0, None, ALU.add))
            link(dve.reciprocal(one[15], one[15]))
            link(tt(one[15], one[15], one[6], ALU.mult))
            link(tt(one[16], one[15], one[1], ALU.mult))
            for fx, oh in ((f1, r[10]), (f2, r[14])):
                for b in range(NB):
                    ins = tt(fx[R][:, b, :, :], oh[:, b, :].unsqueeze(1).to_broadcast([RB, 4, 4]),
                             r[4][:, b, :].unsqueeze(2).to_broadcast([RB, 4, 4]), ALU.mult)
                link(ins)
            fl = [v[R].rearrange("p b g e -> p b (g e)") for v in (f1, f2, sel, pos)]
            tt(fl[2], fl[0], fl[1], ALU.add).then_inc(sel_ok, 1)
            dve.wait_ge(rank_ok, 1)
            link(dve.tensor_copy(fl[3], ps[R, 4, 0:NB * NE].rearrange("p (b e) -> p b e", b=NB)))
            link(dve.tensor_copy(tot, ps[:, 5, 0:NB * NE].rearrange("p (b e) -> p b e", b=NB)))
            link(dve.tensor_copy(ecnt, tot[:, 0, :]))
            for b in range(1, NB):
                link(tt(fl[3][:, b, :], fl[3][:, b, :], ecnt[R], ALU.add))
                link(tt(ecnt, ecnt, tot[:, b, :], ALU.add))
            link(ts(eov, ecnt, float(P), None, ALU.is_gt))
            for n in range(2, NB):
                link(stt(eov, ecnt, float(n * P), eov, ALU.is_gt, ALU.add))
            link(ts(edel, eov, 1.0, None, ALU.mult))
            link(dve.tensor_tensor_scan(eend, cst[:, C_ONE:C_ONE + NE], edel, 0.0, ALU.mult, ALU.add))
            link(tt(edel, eend, eov, ALU.subtract))
            io = cst[:, C_IO:C_IO + NE]
            link(tt(edel, edel, io, ALU.subtract))
            link(ts(edel, edel, float(P), float((NE - 1) * P), ALU.mult, ALU.add))
            link(stt(fl[2], fl[3], float(P), edel[R].unsqueeze(1).to_broadcast([RB, NB, NE]), ALU.is_ge, ALU.mult))
            link(tt(fl[3], fl[3], fl[2], ALU.add))
            link(stt(fl[3], io[R].unsqueeze(1).to_broadcast([RB, NB, NE]), float(P), fl[3], ALU.mult, ALU.add))
            for n in range(2):
                link(tt(fl[n], fl[n], fl[3], ALU.mult))
                link(dve.tensor_reduce(pos_f[R, 5 * n:5 * n + 5], fl[n], X, ALU.add))
            link(tt(ecmp, eend.unsqueeze(1).to_broadcast([P, OVER, NE]),
                    io[:, 0:OVER].unsqueeze(2).to_broadcast([P, OVER, NE]), ALU.is_le))
            link(dve.tensor_reduce(tab_f[:, 0:OVER], ecmp, X, ALU.add))
            link(ts(tab_f[:, 0:OVER], tab_f[:, 0:OVER], float(NE - 1), None, ALU.min))
            link(dve.tensor_copy(tab_f[:, OVER:OVER + 1], eend[:, NE - 1:NE]))
            link(dve.tensor_copy(itab[R, 0:10], pos_f[R, :]))
            dve.tensor_copy(itab[:, 10:11 + OVER], tab_f).then_inc(idx_ok, 1)

            def h_mult(s):
                return tt(hm[s], si[s], ps[:, 2 + s, 256:512], ALU.mult)

            def hT_copy(s):
                return dve.tensor_copy(hT[s].rearrange("p f n -> p (f n)"), ps[:, 4 + s, 0:256])

            def out_copy(s):
                return dve.tensor_copy(yb[s][:, 1, :], ps[:, 7, :])

            def step(q, s):
                i, o_ = q * 2 + s, 1 - s
                if not (isinstance(i, int) and i == 0):
                    dve.wait_ge(m_ht, i)
                    hT_copy(o_).then_inc(m_htev, 1)
                dve.wait_ge(m_si, i + 1)
                h_mult(s).then_inc(m_h, 1)
                if isinstance(i, int) and i == 0:
                    return
                dve.wait_ge(m_y, i)
                if not (isinstance(i, int) and i < 3):
                    dve.wait_ge(m_yst[o_], q * 16 - (16 if s == 0 else 0))
                out_copy(o_).then_inc(m_yd, 1)

            step(0, 0)
            step(0, 1)
            step(1, 0)
            step(1, 1)
            with dve.Fori(2, PAIRS) as q:
                step(q, 0)
                step(q, 1)
            dve.wait_ge(m_ht, NE)
            hT_copy(1).then_inc(m_htev, 1)
            dve.wait_ge(m_y, NE)
            dve.wait_ge(m_yst[1], 16 * (PAIRS - 1))
            out_copy(1).then_inc(m_yd, 1)

            n_over = dve.value_load(itab[0:1, 10 + OVER:11 + OVER], min_val=0, max_val=OVER)
            with dve.If(n_over > 0):
                dve.wait_ge(m_yst[0], 16 * PAIRS)
                with dve.Fori(0, n_over) as i:
                    dve.wait_ge(o_si, i + 1)
                    h_mult(0).then_inc(o_h, 1)
                    dve.wait_ge(o_ht, i + 1)
                    hT_copy(0).then_inc(o_htev, 1)
                    dve.wait_ge(o_y, i + 1)
                    out_copy(0).then_inc(o_yd, 1)
            for b in range(NB):
                dve.wait_ge(yg[b], 32)
                link(stt(hres[b], y1[b], one[15][:, b, :], hres[b], ALU.mult, ALU.add))
                stt(hres[b], y2[b], one[16][:, b, :], hres[b], ALU.mult, ALU.add).then_inc(y_ok, 1)

        @block.gpsimd
        def _(pool):
            link = Chain(pool, pch)
            pool.memset(cxv[:, :, 0:3], 0.0)
            pool.memset(dqv[:, L:XT:2], 0.0)
            pool.memset(dkv[:, L:XT:2], 1.0)
            pool.memset(dvv[:, :, L:XT:2], 0.0)
            for i in range(NV):
                pool.memset(ea[:, i * XT + L:(i + 1) * XT:2], 0.0)
            pool.memset(kvb[1][:, HALF, :], 0.0).then_inc(kv0, 1)
            pool.wait_ge(xn_ok, KT)
            zero = br[:, 0:DM]
            link(pool.memset(zero, 0.0))
            for i in range(NE + OVER):
                pool.dma_start(scr_x[i * P:(i + 1) * P, :], zero).then_inc(zeroed, 16)
            for i in range(NE, NE + OVER):
                pool.dma_start(scr_y[i * P:(i + 1) * P, :], zero).then_inc(zeroed, 16)
            pool.wait_ge(a_ok, 4)
            pool.dma_start(o["k"], aqk[:, 2:4, :]).then_inc(kv_out, 16)
            pool.wait_ge(s_v, 16)
            pool.dma_start(o["v"][0:4 * P, :].rearrange("(b p) c -> p b c", p=P), vt[:, 0:4, 0:256]).then_inc(kv_out, 16)
            pool.dma_start(o["v"][4 * P:T, :], vt[0:T - 4 * P, 4, 0:256]).then_inc(kv_out, 16)
            pool.wait_ge(la_e, NV)
            for i in range(NV):
                ins = pool.memset(ea[:, i * XT:i * XT + 1], 0.0)
            ins.then_inc(ea_ok, 1)
            pool.wait_ge(st_ev, 1)
            pool.dma_start(o["ret_p"], rst).then_inc(rst_out, 16)
            pool.wait_ge(rs_ok, 1)
            pool.dma_start(o["ret_s"], rs0).then_inc(rs_out, 16)
            pool.wait_ge(c_out, 1)
            pool.dma_start(o["c"], cst_out).then_inc(outs, 16)

            def merge(i, n, m):
                pool.wait_ge(mg, i + 1)
                p_ = ptv[:, i % 2, :]
                g = sgtv[:, i % 2, :]
                if i < KT:
                    pool.tensor_tensor(acc[:, m, :], g, p_, ALU.mult).then_inc(mg_used, 1)
                else:
                    link(pool.tensor_tensor(p_, g, p_, ALU.mult))
                    pool.tensor_tensor(acc[:, m, :], acc[:, m, :], p_, ALU.add).then_inc(mg_used, 1)

            pool.wait_ge(kv_out, 48)
            pool.wait_ge(ro_mm, 1)
            pool.wait_ge(ld_s, 32)

            def fill(j):
                pool.wait_ge(vb_ld[j % VR], 64 * (j // VR + 1))
                pool.tensor_copy(vb[j % VR][:, :, L:XT:2], view(g0, 0, 64, DEC)[:, j * NV:(j + 1) * NV, :]).then_inc(vb_s0, 1)

            def states(j):
                pool.wait_ge(g_scan, j + 1)
                pool.tensor_copy(gst[:, :, j * NV:(j + 1) * NV].rearrange("p n v -> p v n"), vb[j % VR][:, :, L - 1:XT:2])\
                    .then_inc(g_st, 1)

            j = 0
            for i, (n, m) in enumerate(ORDER):
                if i == 1:
                    fill(0)
                    fill(1)
                for q in range(SCANS[i]):
                    states(j)
                    if j + 2 < GROUPS:
                        fill(j + 2)
                    j += 1
                merge(i, n, m)
            pool.wait_ge(g_st, GROUPS)
            pool.dma_start(o["gla"], gst).then_inc(outs, 16)
            pool.wait_ge(idx_ok, 1)
            pool.wait_ge(zeroed, 16 * (NE + 2 * OVER))
            for n in range(2):
                for b in range(NB):
                    at = 5 * n + b
                    pool.indirect_dma_start(out=scr_x, out_offset=on_rows(itab[0:RB, at:at + 1]),
                                            in_=tk[b], in_offset=None).then_inc(xs_ok, 16)

            def store(q, s):
                i = q * 2 + s
                pool.wait_ge(m_ya, i + 1)
                pool.wait_ge(m_yd, i + 1)
                dst = scr_y[i * P:(i + 1) * P, :] if isinstance(i, int) else scr_y[bass.ds(i * P, P), :]
                pool.dma_start(dst, yb[s].rearrange("p a n -> p (a n)")).then_inc(m_yst[s], 16)

            with pool.Fori(0, PAIRS) as q:
                store(q, 0)
                store(q, 1)
            for s in range(2):
                pool.wait_ge(m_yst[s], 16 * PAIRS)
            n_over = pool.value_load(itab[0:1, 10 + OVER:11 + OVER], min_val=0, max_val=OVER)
            with pool.If(n_over > 0):
                pool.sem_inc(o_go, 1)
                with pool.Fori(0, n_over) as i:
                    pool.wait_ge(o_ya, i + 1)
                    pool.wait_ge(o_yd, i + 1)
                    pool.dma_start(scr_y[bass.ds(i * P + NE * P, P), :], yb[0].rearrange("p a n -> p (a n)")).then_inc(o_st, 16)
                    pool.wait_ge(o_st, i * 16 + 16)
                    pool.sem_inc(o_go, 1)
            for b in range(NB):
                for n, dst in ((0, y1[b]), (1, y2[b])):
                    at = 5 * n + b
                    pool.indirect_dma_start(out=dst, out_offset=None, in_=scr_y,
                                            in_offset=on_rows(itab[0:RB, at:at + 1])).then_inc(yg[b], 16)
            for stored, n in ((kv_out, 3), (rst_out, 1), (rs_out, 1), (outs, POOL_OUTS)):
                pool.wait_ge(stored, 16 * n)



def constants():
    import numpy as np
    c = np.zeros((P, C_W), np.float32)
    p = np.arange(P)
    c[:, C_ID:C_ID + P] = np.eye(P)
    c[p, C_PERM + (p ^ 32)] = 1.0
    c[:, C_B32:C_B32 + P] = (p[:, None] // 32 == p[None] // 32) / 32.0
    c[:, C_B64:C_B64 + P] = (p[:, None] // 64 == p[None] // 64) / 64.0
    c[:, C_ONE:C_ONE + P] = 1.0
    c[p, C_SEL + 31 + 32 * (p // 32)] = 1.0
    inv = (np.float32(10000.0) ** (-np.linspace(0.0, 1.0, 32, dtype=np.float32))).astype(np.float32)
    pos = np.concatenate([np.arange(L), np.full(DEC, PAST)]).astype(np.float32)
    ang = (pos[None, :] * inv[p % 32][:, None]).astype(np.float32)
    c[:, C_COS:C_COS + T] = np.cos(ang)
    c[:, C_SIN:C_SIN + T] = np.where(p[:, None] % 64 < 32, -np.sin(ang), np.sin(ang))
    lgam = np.log(1.0 - 2.0 ** (-5.0 - np.arange(H)))
    x = np.arange(L)
    for h in range(H):
        rel = x[None, :] - p[:, None]
        c[:, C_DT + h * L:C_DT + (h + 1) * L] = np.where(rel >= 0, np.exp(np.maximum(rel, 0) * lgam[h]), 0.0)
    q = np.arange(144)
    c[:, C_MASK:C_MASK + 144] = np.where(q[None, :] <= p[:, None] + META, 0.0, NEG)
    for b in range(NB):
        for h in range(H):
            at = np.minimum(b * P + p, L - 1)
            c[:, C_DEC + b * H + h] = np.exp((L - 1 - at) * lgam[h])
    for t in range(2):
        c[:, C_GAM + t] = np.exp(lgam[2 * t + p // 64])
    c[1:, C_NEW] = NEG
    c[:, C_EPS] = EPS
    c[:, C_LT:C_LT + P] = p[:, None] < p[None]
    c[:, C_IO:C_IO + NE] = np.arange(NE)
    return c


_OUT = {"y": (N, DM), "k": (P, 2, T), "v": (T, 256), "ret_p": (64, H, 64), "ret_s": (P, 2, DEC, 64),
        "c": (P, 2, 36), "gla": (P, 1 + DEC, 64)}


def kernel(**inputs):
    import numpy as np
    import concourse.bacc as bacc
    from concourse.bass_utils import run_bass_kernel_spmd as run

    a = {k: np.asarray(v) for k, v in inputs.items()}

    def cols(v):
        return np.ascontiguousarray(v.reshape(-1, P).T)

    def tiles(w):
        return w.reshape(KT, P, -1).transpose(1, 0, 2)

    w = a["w_in"][0]
    cut = np.cumsum([0, 256, 256, 256, 256, 256, 256, 256, 256, 256, 128, 128, 256, 256, 16])
    aq, ak, av, bq, bk, bv, bg_, cx_, cg_, dq, dk, dv_, dr_, da = [w[:, i:j] for i, j in zip(cut[:-1], cut[1:])]
    dr_ = dr_.reshape(DM, H, 2, 32).transpose(0, 2, 1, 3).reshape(DM, 256)
    w_in = np.concatenate([aq, ak, av, bq, bk, bg_, bv, cx_, cg_, dq, dk, dv_, dr_], 1)
    w_in = w_in.reshape(KT, P, N_IN, P).transpose(2, 1, 0, 3).reshape(N_IN, P, 1024)
    wb = a["w_branch"][0].copy()
    wb = np.stack([wb[0], wb[1], wb[2], wb[3].reshape(H, 2, 32, DM).transpose(1, 0, 2, 3).reshape(256, DM)])
    wm = a["w_merge"][0].reshape(KT, P, 4, KT, P).transpose(2, 3, 1, 0, 4)
    wbt = wb.reshape(4, 2, P, KT, P).transpose(0, 3, 2, 1, 4)
    both = np.concatenate([wm.reshape(4, KT, P, 1024), wbt.reshape(4, KT, P, 256)], 3)
    w_mg = np.concatenate([both["ABCD".index(n)] for n in "BCAD"])
    w_dp = wbt[3].reshape(2, 4, P, 256).transpose(0, 2, 1, 3).reshape(2, P, 1024)
    w_out = a["w_out"][0].reshape(4, 2, P, 2, 512).transpose(3, 0, 2, 1, 4).reshape(8, P, 1024)
    w_13 = np.concatenate([a["ex_w1"][0].reshape(NE, KT, P, 256), a["ex_w3"][0].reshape(NE, KT, P, 256)], 3).transpose(0, 2, 1, 3)
    w_2 = a["ex_w2"][0].reshape(NE, 2, P, DM).transpose(0, 2, 1, 3)

    x = np.concatenate([a["meta"], a["x_prompt"][0], a["x_sample"][:, 0]], 0)
    xT = x.T.reshape(KT, P, T).transpose(1, 0, 2)

    v = np.zeros((P, V_W), np.float32)
    v[:, V_N1:V_N1 + 8] = cols(a["norm1"][0])
    v[:, V_QN], v[:, V_KN] = np.tile(a["qn"][0], 4), np.tile(a["kn"][0], 4)
    v[:, V_AN], v[:, V_RN] = np.tile(a["an"][0], 2), np.tile(a["rn"][0], 2)
    v[:, V_GN], v[:, V_GN + 1] = np.tile(a["gn"][0][:32], 4), np.tile(a["gn"][0][32:], 4)
    for k in range(4):
        v[:, V_CW + 2 * k:V_CW + 2 * k + 2] = cols(a["conv_w"][0, k])
    for at, name in ((V_CB, "conv_b"), (V_BA, "lru_ba"), (V_BX, "lru_bx"), (V_LL, "lru_lam")):
        v[:, at:at + 2] = cols(a[name][0])
    v[:, V_GB] = a["gla_b"][0]
    v[:, V_BM:V_BM + 32] = cols(a["b_merge"][0])
    v[:, V_RB:V_RB + 4], v[:, V_RB + 4:V_RB + 20] = a["rg_b"][0], a["re_b"][0]
    v[:, V_LAM:V_LAM + 128] = a["lam"][0].reshape(-1)
    v[:, V_ST:V_ST + 48] = a["state_lru_conv"][0].transpose(2, 0, 1).reshape(2, P, 24).transpose(1, 0, 2).reshape(P, 48)
    v[:, V_ST + 48:V_ST + 64] = a["state_lru_h"][0].T.reshape(2, P, DEC).transpose(1, 0, 2).reshape(P, 16)
    for at, name in ((V_WA, "lru_wa"), (V_WX, "lru_wx")):
        for h in range(H):
            r = 64 * (h % 2)
            v[r:r + 64, at + P * (h // 2) + r:at + P * (h // 2) + r + 64] = a[name][0, h]
    v[:, V_RW:V_RW + 160] = tiles(np.concatenate([a["rg_w"][0], a["re_w"][0]], 1)).reshape(P, 160)
    v[:, V_DA:V_DA + 128] = tiles(da).reshape(P, 128)
    v[0:16, V_G2:V_G2 + 128] = a["gla_w2"][0]

    ret0 = a["state_ret"][0].reshape(DEC, 2, P, 64).transpose(2, 1, 0, 3)
    gla0 = a["state_gla"][0].reshape(DEC, P, 64).transpose(1, 2, 0).reshape(P, 512)
    kcache = a["cache_k_a"][0].reshape(-1, PAGE, 256)
    vcache = a["cache_v_a"][0].reshape(-1, PAGE, 256)
    pt = a["page_table"].reshape(1, -1)

    nc = bacc.Bacc("TRN2", target_bir_lowering=False, num_devices=1)
    arrays, args = {}, []
    for name, arr in (("w_in", w_in), ("w_mg", w_mg), ("w_dp", w_dp), ("w_out", w_out), ("w_13", w_13), ("w_2", w_2),
                      ("x", x[META:]), ("n2", a["norm2"]), ("xT", xT),
                      ("const", constants()), ("vec", v), ("ret0", ret0), ("gla0", gla0), ("kc", kcache),
                      ("vc", vcache), ("pt", pt)):
        arr = np.ascontiguousarray(arr)
        arrays["in_" + name] = arr
        args.append(nc.dram_tensor("in_" + name, arr.shape, mybir.dt.from_np(arr.dtype), kind="ExternalInput").ap())
    o = {k: nc.dram_tensor("out_" + k, s, F32, kind="ExternalOutput").ap() for k, s in _OUT.items()}
    program(nc, *args, o)
    res = run(nc, [arrays], core_ids=[0]).results[0]
    r = {k: np.asarray(res["out_" + k]).reshape(s) for k, s in _OUT.items()}

    y = r["y"]
    k = r["k"].transpose(2, 1, 0).reshape(T, H, 64)
    vv_ = r["v"].reshape(T, H, 64)
    c = r["c"].transpose(1, 0, 2).reshape(256, 36)
    g = r["gla"]
    rs = r["ret_s"].reshape(2, 64, 2, DEC, 64).transpose(3, 2, 0, 1, 4).reshape(DEC, H, 64, 64)
    outs = (y[:SEQ][None], y[SEQ:][:, None], k[:L][None, None], vv_[:L][None, None],
            r["ret_p"].transpose(1, 0, 2)[None, None], c[:, 0][None, None], c[:, 9:12].T[None, None],
            g[:, 0].reshape(H, 32, 64)[None, None],
            k[L:][None, :, None], vv_[L:][None, :, None], rs[None], c[:, 1:9].T[None],
            c[:, 12:36].reshape(256, DEC, 3).transpose(1, 2, 0)[None],
            g[:, 1:].transpose(1, 0, 2).reshape(DEC, H, 32, 64)[None])
    return tuple(np.ascontiguousarray(t) for t in outs)
```
